# Optimizing a Trainium2 kernel written in Bass

```python
import jax, jax.numpy as jnp
from jax import lax
import numpy as np
import math

D_MODEL = 1024
BATCH = 1
SEQ = 2048
DEPTH = 1

MLA_HEADS = 8
MLA_Q_RANK = 256
MLA_KV_RANK = 128
MLA_NOPE_DIM = 64
MLA_ROPE_DIM = 32
MLA_QK_DIM = MLA_NOPE_DIM + MLA_ROPE_DIM
MLA_V_DIM = 64
MLA_WIDTH = MLA_HEADS * MLA_V_DIM
DSA_HEADS = 8
DSA_KV_HEADS = 2
DSA_HEAD_DIM = 64
DSA_WIDTH = DSA_HEADS * DSA_HEAD_DIM
DSA_ROT_DIM = DSA_HEAD_DIM // 4
IDX_HEADS = 8
IDX_DIM = 32
IDX_ROT_DIM = IDX_DIM // 4
INDEX_TOPK_MAX = 256
ROPE_THETA = 500000.0
Q_BLOCK = 128
NORM_EPS = 1e-6

IN_SPLITS = (
    MLA_Q_RANK, MLA_KV_RANK, MLA_ROPE_DIM, MLA_WIDTH,
    DSA_HEADS * DSA_HEAD_DIM, DSA_KV_HEADS * DSA_HEAD_DIM,
    DSA_KV_HEADS * DSA_HEAD_DIM, DSA_WIDTH,
    IDX_HEADS * IDX_DIM, IDX_DIM, IDX_HEADS,
    D_MODEL, D_MODEL,
)
D_IN = sum(IN_SPLITS)


def rms_norm(x, gain):
    xf = x.astype(jnp.float32)
    y = xf * lax.rsqrt(jnp.mean(xf * xf, axis=-1, keepdims=True) + NORM_EPS)
    return (y * gain.astype(jnp.float32)).astype(x.dtype)

def rope_angles(positions, rot_dim):
    inv_freq = ROPE_THETA ** (-jnp.arange(0, rot_dim, 2, dtype=jnp.float32) / rot_dim)
    ang = positions.astype(jnp.float32)[..., None] * inv_freq
    return jnp.cos(ang), jnp.sin(ang)

def apply_rope(x, cos, sin):
    xf = x.astype(jnp.float32)
    half = xf.shape[-1] // 2
    x1, x2 = xf[..., :half], xf[..., half:]
    c, s = cos[:, :, None, :], sin[:, :, None, :]
    return jnp.concatenate([x1 * c - x2 * s, x2 * c + x1 * s], axis=-1).astype(x.dtype)

def partial_rope(x, cos, sin, rot_dim):
    return jnp.concatenate([apply_rope(x[..., :rot_dim], cos, sin), x[..., rot_dim:]], axis=-1)

def to_blocks(a):
    b, s = a.shape[0], a.shape[1]
    a = a.reshape((b, s // Q_BLOCK, Q_BLOCK) + a.shape[2:])
    return jnp.moveaxis(a, 1, 0)

def from_blocks(a):
    a = jnp.moveaxis(a, 0, 1)
    return a.reshape((a.shape[0], a.shape[1] * a.shape[2]) + a.shape[3:])

def mla_attention(q, k, v):
    s_len = q.shape[1]
    scale = MLA_QK_DIM ** -0.5
    key_pos = jnp.arange(s_len, dtype=jnp.int32)
    starts = jnp.arange(s_len // Q_BLOCK, dtype=jnp.int32) * Q_BLOCK

    def one_block(args):
        qb, start = args
        qpos = start + jnp.arange(Q_BLOCK, dtype=jnp.int32)
        sc = jnp.einsum('bqhd,bkhd->bhqk', qb, k).astype(jnp.float32) * scale
        causal = key_pos[None, :] <= qpos[:, None]
        sc = jnp.where(causal[None, None], sc, -jnp.inf)
        p = jax.nn.softmax(sc, axis=-1).astype(v.dtype)
        return jnp.einsum('bhqk,bkhd->bqhd', p, v)

    return from_blocks(lax.map(one_block, (to_blocks(q), starts)))

def dsa_attention(q, k, v, q_idx, k_idx, w_idx, k_top):
    bsz, s_len, n_heads, hd = q.shape
    n_kv = k.shape[2]
    grp = n_heads // n_kv
    scale = hd ** -0.5
    key_pos = jnp.arange(s_len, dtype=jnp.int32)
    starts = jnp.arange(s_len // Q_BLOCK, dtype=jnp.int32) * Q_BLOCK
    gather = jax.vmap(lambda kb, ib: kb[ib])

    def one_block(args):
        qb, qib, wb, start = args
        qpos = start + jnp.arange(Q_BLOCK, dtype=jnp.int32)
        rel = jax.nn.relu(jnp.einsum('bqhd,bsd->bqhs', qib, k_idx).astype(jnp.float32))
        score = jnp.einsum('bqhs,bqh->bqs', rel, wb.astype(jnp.float32))
        causal = key_pos[None, None, :] <= qpos[None, :, None]
        score = jnp.where(causal, score, -jnp.inf)
        _, sel = lax.top_k(score, k_top)
        valid = sel <= qpos[None, :, None]
        kg = gather(k, sel)
        vg = gather(v, sel)
        qg = qb.reshape(bsz, Q_BLOCK, n_kv, grp, hd)
        sc = jnp.einsum('bqkgd,bqjkd->bqkgj', qg, kg).astype(jnp.float32) * scale
        sc = jnp.where(valid[:, :, None, None, :], sc, -jnp.inf)
        p = jax.nn.softmax(sc, axis=-1).astype(v.dtype)
        o = jnp.einsum('bqkgj,bqjkd->bqkgd', p, vg)
        return o.reshape(bsz, Q_BLOCK, n_heads, hd)

    out = lax.map(one_block, (to_blocks(q), to_blocks(q_idx), to_blocks(w_idx), starts))
    return from_blocks(out)

def first_inputs(seed: int = 0) -> dict:
    key = jax.random.key(seed)
    ks = jax.random.split(key, 20)
    f32 = jnp.float32

    def w(k, shape, fan_in):
        return jax.random.normal(k, shape, f32) * fan_in ** -0.5

    def g(k, n):
        return 1.0 + 0.01 * jax.random.normal(k, (DEPTH, n), f32)

    x = jax.random.normal(ks[0], (BATCH, SEQ, D_MODEL), f32)
    positions = jnp.broadcast_to(jnp.arange(SEQ, dtype=jnp.int32)[None, :], (BATCH, SEQ))
    return {
        'x': x,
        'positions': positions,
        'norm_gain': g(ks[1], D_MODEL),
        'w_in': w(ks[2], (DEPTH, D_MODEL, D_IN), D_MODEL),
        'b_merge': 0.01 * jax.random.normal(ks[3], (DEPTH, 2, D_MODEL), f32),
        'mla_q_norm': g(ks[4], MLA_Q_RANK),
        'mla_w_uq': w(ks[5], (DEPTH, MLA_Q_RANK, MLA_HEADS * MLA_QK_DIM), MLA_Q_RANK),
        'mla_kv_norm': g(ks[6], MLA_KV_RANK),
        'mla_w_ukv': w(ks[7], (DEPTH, MLA_KV_RANK, MLA_HEADS * (MLA_NOPE_DIM + MLA_V_DIM)), MLA_KV_RANK),
        'mla_q_gain': g(ks[8], MLA_QK_DIM),
        'mla_k_gain': g(ks[9], MLA_QK_DIM),
        'dsa_q_gain': g(ks[10], DSA_HEAD_DIM),
        'dsa_k_gain': g(ks[11], DSA_HEAD_DIM),
        'w_branch_mla': w(ks[12], (DEPTH, MLA_WIDTH, D_MODEL), MLA_WIDTH),
        'w_branch_dsa': w(ks[13], (DEPTH, DSA_WIDTH, D_MODEL), DSA_WIDTH),
        'w_out': w(ks[14], (DEPTH, D_MODEL, D_MODEL), D_MODEL),
    }

def first_block(x, positions, norm_gain, w_in, b_merge, mla_q_norm, mla_w_uq, mla_kv_norm, mla_w_ukv,
              mla_q_gain, mla_k_gain, dsa_q_gain, dsa_k_gain, w_branch_mla, w_branch_dsa, w_out):
    bsz, s_len, _ = x.shape
    k_top = min(INDEX_TOPK_MAX, s_len // 4)
    offsets = [int(o) for o in np.cumsum(IN_SPLITS)[:-1]]
    cos_m, sin_m = rope_angles(positions, MLA_ROPE_DIM)
    cos_d, sin_d = rope_angles(positions, DSA_ROT_DIM)
    cos_i, sin_i = rope_angles(positions, IDX_ROT_DIM)

    for l in range(DEPTH):
        h = rms_norm(x, norm_gain[l])
        proj = h @ w_in[l]
        (c_q, c_kv, k_pe, gate_a, q_b, k_b, v_b, gate_b,
         q_i, k_i, w_i, m_a, m_b) = jnp.split(proj, offsets, axis=-1)

        q_a = (rms_norm(c_q, mla_q_norm[l]) @ mla_w_uq[l]).reshape(bsz, s_len, MLA_HEADS, MLA_QK_DIM)
        kv_a = (rms_norm(c_kv, mla_kv_norm[l]) @ mla_w_ukv[l]).reshape(
            bsz, s_len, MLA_HEADS, MLA_NOPE_DIM + MLA_V_DIM)
        k_nope, v_a = kv_a[..., :MLA_NOPE_DIM], kv_a[..., MLA_NOPE_DIM:]
        k_rope = jnp.broadcast_to(k_pe[:, :, None, :], (bsz, s_len, MLA_HEADS, MLA_ROPE_DIM))
        k_a = jnp.concatenate([k_nope, k_rope], axis=-1)
        q_a = rms_norm(q_a, mla_q_gain[l])
        k_a = rms_norm(k_a, mla_k_gain[l])
        q_a = jnp.concatenate([q_a[..., :MLA_NOPE_DIM], apply_rope(q_a[..., MLA_NOPE_DIM:], cos_m, sin_m)], axis=-1)
        k_a = jnp.concatenate([k_a[..., :MLA_NOPE_DIM], apply_rope(k_a[..., MLA_NOPE_DIM:], cos_m, sin_m)], axis=-1)
        o_a = mla_attention(q_a, k_a, v_a).reshape(bsz, s_len, MLA_WIDTH) * jax.nn.silu(gate_a)

        q_b = rms_norm(q_b.reshape(bsz, s_len, DSA_HEADS, DSA_HEAD_DIM), dsa_q_gain[l])
        k_b = rms_norm(k_b.reshape(bsz, s_len, DSA_KV_HEADS, DSA_HEAD_DIM), dsa_k_gain[l])
        v_b = v_b.reshape(bsz, s_len, DSA_KV_HEADS, DSA_HEAD_DIM)
        q_b = partial_rope(q_b, cos_d, sin_d, DSA_ROT_DIM)
        k_b = partial_rope(k_b, cos_d, sin_d, DSA_ROT_DIM)
        q_i = partial_rope(q_i.reshape(bsz, s_len, IDX_HEADS, IDX_DIM), cos_i, sin_i, IDX_ROT_DIM)
        k_i = partial_rope(k_i[:, :, None, :], cos_i, sin_i, IDX_ROT_DIM)[:, :, 0, :]
        w_i = w_i * (IDX_HEADS ** -0.5 * IDX_DIM ** -0.5)
        o_b = dsa_attention(q_b, k_b, v_b, q_i, k_i, w_i, k_top).reshape(bsz, s_len, DSA_WIDTH)
        o_b = o_b * jax.nn.silu(gate_b)

        merged = (jax.nn.sigmoid(m_a + b_merge[l, 0]) * (o_a @ w_branch_mla[l])
                  + jax.nn.sigmoid(m_b + b_merge[l, 1]) * (o_b @ w_branch_dsa[l]))
        x = x + merged @ w_out[l]
    return x


N_MIXERS = 4
EPS = 1e-6
NEG = -1e30
BIG = 1e30
T5_BUCKETS = 32
T5_MAX_DIST = 128
ATTN_HEADS = 16
HEAD_DIM = D_MODEL // ATTN_HEADS
KV_HEADS = 4
GQA = ATTN_HEADS // KV_HEADS
SWA_WINDOW = 128
RWKV_HEAD = 64
RWKV_HEADS = D_MODEL // RWKV_HEAD
RWKV_LORA_W = 64
RWKV_LORA_A = 64
RWKV_GN_EPS = 64e-5
NSA_CMP_LEN = 32
NSA_CMP_STRIDE = 16
NSA_CMP_HIDDEN = 128
NSA_SEL_LEN = 64
NSA_TOPK = 16
NSA_WINDOW = 512
NSA_SEL_QCHUNK = 64
LRU_WIDTH = 1280
LRU_BLOCKS = 16
LRU_BLOCK = LRU_WIDTH // LRU_BLOCKS
LRU_C = 8.0
CONV_WIDTH = 4


def _layers_of(m):
    return len(range(m, DEPTH, N_MIXERS))

def rms_norm_2(x, g):
    xf = x.astype(jnp.float32)
    y = xf * lax.rsqrt(jnp.mean(xf * xf, axis=-1, keepdims=True) + EPS)
    return (y * g.astype(jnp.float32)).astype(x.dtype)

def t5_bucket(dist):
    max_exact = T5_BUCKETS // 2
    d = jnp.maximum(dist, 0)
    df = jnp.maximum(d, 1).astype(jnp.float32)
    large = max_exact + (jnp.log(df / max_exact) / math.log(T5_MAX_DIST / max_exact)
                         * (T5_BUCKETS - max_exact)).astype(jnp.int32)
    large = jnp.minimum(large, T5_BUCKETS - 1)
    return jnp.where(d < max_exact, d, large)

def q_heads(t, B, T):
    return t.reshape(B, T, KV_HEADS, GQA, HEAD_DIM).transpose(0, 2, 3, 1, 4)

def kv_heads(t, B, T):
    return t.reshape(B, T, KV_HEADS, HEAD_DIM).transpose(0, 2, 1, 3)

def merge_heads(o, B, T):
    return o.transpose(0, 3, 1, 2, 4).reshape(B, T, ATTN_HEADS * HEAD_DIM)

def banded_attention(q, k, v, t5_table, window, sinks=None):
    B, G, R, T, Dh = q.shape
    nb = T // Q_BLOCK
    nprev = -(-window // Q_BLOCK)
    kc = (nprev + 1) * Q_BLOCK
    qb = q.reshape(B, G, R, nb, Q_BLOCK, Dh)
    pad = ((0, 0), (0, 0), (nprev * Q_BLOCK, 0), (0, 0))
    kp = jnp.pad(k, pad).reshape(B, G, nb + nprev, Q_BLOCK, Dh)
    vp = jnp.pad(v, pad).reshape(B, G, nb + nprev, Q_BLOCK, Dh)
    kb = jnp.concatenate([kp[:, :, j:j + nb] for j in range(nprev + 1)], axis=3)
    vb = jnp.concatenate([vp[:, :, j:j + nb] for j in range(nprev + 1)], axis=3)
    s = jnp.einsum('bgrnqd,bgnkd->bgrnqk', qb, kb,
                   preferred_element_type=jnp.float32) * (Dh ** -0.5)
    dist = nprev * Q_BLOCK + jnp.arange(Q_BLOCK)[:, None] - jnp.arange(kc)[None, :]
    kpos = (jnp.arange(nb)[:, None, None] - nprev) * Q_BLOCK + jnp.arange(kc)[None, None, :]
    valid = (dist >= 0) & (dist < window) & (kpos >= 0)
    bias = jnp.take(t5_table, t5_bucket(dist), axis=0)
    bias = jnp.moveaxis(bias, -1, 0).reshape(G, R, Q_BLOCK, kc).astype(jnp.float32)
    s = jnp.where(valid, s + bias[None, :, :, None], NEG)
    if sinks is None:
        p = jax.nn.softmax(s, axis=-1)
    else:
        sk = jnp.broadcast_to(sinks.astype(jnp.float32).reshape(1, G, R, 1, 1, 1), s.shape[:-1] + (1,))
        p = jax.nn.softmax(jnp.concatenate([s, sk], axis=-1), axis=-1)[..., :-1]
    o = jnp.einsum('bgrnqk,bgnkd->bgrnqd', p.astype(v.dtype), vb)
    return o.reshape(B, G, R, T, Dh)

def swa_sink_mixer(xn, w_in, sinks, w_out, t5_table):
    B, T, _ = xn.shape
    nq, nkv = ATTN_HEADS * HEAD_DIM, KV_HEADS * HEAD_DIM
    q, k, v, z = jnp.split(xn @ w_in, [nq, nq + nkv, nq + 2 * nkv], axis=-1)
    o = banded_attention(q_heads(q, B, T), kv_heads(k, B, T), kv_heads(v, B, T),
                         t5_table, SWA_WINDOW, sinks)
    return (merge_heads(o, B, T) * jax.nn.silu(z)) @ w_out

def rwkv7_mixer(xn, mu, w_in, w0, w1, w2, a0, a1, a2, k_k, k_a, r_k, lnx_w, lnx_b, w_out):
    B, T, D = xn.shape
    H, N = RWKV_HEADS, RWKV_HEAD
    C = H * N
    f32 = jnp.float32
    xx = jnp.pad(xn, ((0, 0), (1, 0), (0, 0)))[:, :-1] - xn
    lerp = xn[None] + xx[None] * mu[:, None, None, :]
    rkvz = jnp.einsum('sbtd,dsc->sbtc', lerp[:4], w_in.reshape(D, 4, C))
    r, k, v, z = rkvz[0], rkvz[1], rkvz[2], rkvz[3]
    w = -jax.nn.softplus(-(w0 + jnp.tanh(lerp[4] @ w1) @ w2)) - 0.5
    a = jax.nn.sigmoid(a0 + (lerp[5] @ a1) @ a2)
    hs = lambda t: t.astype(f32).reshape(B, T, H, N)
    kk = hs(k * k_k)
    kk = kk / jnp.maximum(jnp.sqrt(jnp.sum(kk * kk, axis=-1, keepdims=True)), 1e-12)
    k = hs(k * (1 + (a - 1) * k_a))
    r, v, a = hs(r), hs(v), hs(a)
    decay = jnp.exp(-jnp.exp(hs(w)))
    aa, bb = -kk, kk * a

    def step(S, inp):
        r_t, w_t, k_t, v_t, a_t, b_t = inp
        sa = jnp.einsum('bhij,bhj->bhi', S, a_t)
        S = S * w_t[:, :, None, :] + sa[..., None] * b_t[:, :, None, :] + v_t[..., None] * k_t[:, :, None, :]
        return S, jnp.einsum('bhij,bhj->bhi', S, r_t)

    xs = tuple(jnp.moveaxis(t, 1, 0) for t in (r, decay, k, v, aa, bb))
    _, y = lax.scan(step, jnp.zeros((B, H, N, N), f32), xs)
    y = jnp.moveaxis(y, 0, 1)
    mean = jnp.mean(y, axis=-1, keepdims=True)
    var = jnp.mean(jnp.square(y - mean), axis=-1, keepdims=True)
    y = ((y - mean) * lax.rsqrt(var + RWKV_GN_EPS)).reshape(B, T, C) * lnx_w.astype(f32) + lnx_b.astype(f32)
    bonus = jnp.sum(r * k * r_k.astype(f32), axis=-1, keepdims=True) * v
    y = (y + bonus.reshape(B, T, C)) * jax.nn.silu(z.astype(f32))
    return y.astype(xn.dtype) @ w_out

def nsa_mixer(xn, w_in, cmp_pos_k, cmp_k_w1, cmp_k_w2, cmp_pos_v, cmp_v_w1, cmp_v_w2, w_out, t5_table):
    B, T, _ = xn.shape
    G, R, Dh = KV_HEADS, GQA, HEAD_DIM
    f32 = jnp.float32
    nq, nkv = ATTN_HEADS * Dh, G * Dh
    splits = np.cumsum([nq] + [nkv] * 6 + [3 * ATTN_HEADS]).tolist()
    q, kc, vc, ks, vs, kw, vw, gates, z = jnp.split(xn @ w_in, splits, axis=-1)
    q = q_heads(q, B, T)
    kc, vc, ks, vs, kw, vw = (kv_heads(t, B, T) for t in (kc, vc, ks, vs, kw, vw))
    scale = Dh ** -0.5
    tpos = jnp.arange(T)

    n_cmp = (T - NSA_CMP_LEN) // NSA_CMP_STRIDE + 1
    tok_idx = np.arange(n_cmp)[:, None] * NSA_CMP_STRIDE + np.arange(NSA_CMP_LEN)[None, :]

    def compress(t, pos, w1, w2):
        blk = (t[:, :, tok_idx] + pos).reshape(B, G, n_cmp, NSA_CMP_LEN * Dh)
        return jax.nn.silu(blk @ w1) @ w2

    k_cmp = compress(kc, cmp_pos_k, cmp_k_w1, cmp_k_w2)
    v_cmp = compress(vc, cmp_pos_v, cmp_v_w1, cmp_v_w2)
    cmp_start = jnp.arange(n_cmp) * NSA_CMP_STRIDE
    cmp_end = cmp_start + NSA_CMP_LEN - 1
    cmp_ok = cmp_end[None, :] <= tpos[:, None]
    s_c = jnp.einsum('bgrtd,bgnd->bgrtn', q, k_cmp, preferred_element_type=f32) * scale
    p_c = jax.nn.softmax(jnp.where(cmp_ok, s_c, NEG), axis=-1) * cmp_ok
    o_cmp = jnp.einsum('bgrtn,bgnd->bgrtd', p_c.astype(v_cmp.dtype), v_cmp)

    n_sel = T // NSA_SEL_LEN
    k_top = min(NSA_TOPK, n_sel)
    sel_start = jnp.arange(n_sel) * NSA_SEL_LEN
    overlap = ((cmp_start[:, None] < sel_start[None, :] + NSA_SEL_LEN)
               & (cmp_end[:, None] >= sel_start[None, :])).astype(f32)
    imp = jnp.einsum('bgrtn,ns->bgts', p_c, overlap)
    blk = jnp.arange(n_sel)[None, :]
    cur = (tpos // NSA_SEL_LEN)[:, None]
    forced = (blk == 0) | (blk == cur) | (blk == cur - 1)
    future = sel_start[None, :] > tpos[:, None]
    imp = jnp.where(forced, BIG, jnp.where(future, NEG, imp))
    _, sel_idx = lax.top_k(imp, k_top)

    ks_blk = ks.reshape(B, G, n_sel, NSA_SEL_LEN, Dh)
    vs_blk = vs.reshape(B, G, n_sel, NSA_SEL_LEN, Dh)
    QC = NSA_SEL_QCHUNK
    nch = T // QC
    q_ch = jnp.moveaxis(q.reshape(B, G, R, nch, QC, Dh), 3, 0)
    idx_ch = jnp.moveaxis(sel_idx.reshape(B, G, nch, QC, k_top), 2, 0)
    pos_ch = tpos.reshape(nch, QC)
    bi = jnp.arange(B)[:, None, None, None]
    gi = jnp.arange(G)[None, :, None, None]
    gi5 = jnp.arange(G)[None, :, None, None, None]
    table_g = t5_table.reshape(T5_BUCKETS, G, R)

    def sel_chunk(args):
        qc, ic, pc = args
        kg = ks_blk[bi, gi, ic]
        vg = vs_blk[bi, gi, ic]
        kpos = ic[..., None] * NSA_SEL_LEN + jnp.arange(NSA_SEL_LEN)
        dist = pc[None, None, :, None, None] - kpos
        s = jnp.einsum('bgrqd,bgqskd->bgrqsk', qc, kg, preferred_element_type=f32) * scale
        bias = jnp.moveaxis(table_g[t5_bucket(dist), gi5], -1, 2).astype(f32)
        s = jnp.where((dist >= 0)[:, :, None], s + bias, NEG)
        p = jax.nn.softmax(s.reshape(B, G, R, QC, k_top * NSA_SEL_LEN), axis=-1)
        p = p.reshape(B, G, R, QC, k_top, NSA_SEL_LEN)
        return jnp.einsum('bgrqsk,bgqskd->bgrqd', p.astype(vg.dtype), vg)

    o_sel = lax.map(sel_chunk, (q_ch, idx_ch, pos_ch))
    o_sel = jnp.moveaxis(o_sel, 0, 3).reshape(B, G, R, T, Dh)

    o_win = banded_attention(q, kw, vw, t5_table, NSA_WINDOW)

    g = jax.nn.sigmoid(gates).reshape(B, T, 3, G, R).transpose(2, 0, 3, 4, 1)[..., None]
    o = g[0] * o_cmp + g[1] * o_sel + g[2] * o_win
    return (merge_heads(o, B, T) * jax.nn.silu(z)) @ w_out

def rglru_mixer(xn, w_in, conv_w, conv_b, gate_a_w, gate_a_b, gate_x_w, gate_x_b, lam, w_out):
    B, T, _ = xn.shape
    f32 = jnp.float32
    u, z = jnp.split(xn @ w_in, 2, axis=-1)
    u = lax.conv_general_dilated(u, conv_w[:, None, :], window_strides=(1,),
                                 padding=[(CONV_WIDTH - 1, 0)],
                                 dimension_numbers=('NWC', 'WIO', 'NWC'),
                                 feature_group_count=LRU_WIDTH) + conv_b
    ub = u.reshape(B, T, LRU_BLOCKS, LRU_BLOCK)
    r = jax.nn.sigmoid(jnp.einsum('btnc,ncd->btnd', ub, gate_a_w).reshape(B, T, LRU_WIDTH) + gate_a_b)
    i = jax.nn.sigmoid(jnp.einsum('btnc,ncd->btnd', ub, gate_x_w).reshape(B, T, LRU_WIDTH) + gate_x_b)
    log_a = -LRU_C * r.astype(f32) * jax.nn.softplus(-lam.astype(f32))
    a = jnp.exp(log_a)
    b = jnp.sqrt(-jnp.expm1(2.0 * log_a)) * (i * u).astype(f32)

    def combine(left, right):
        a1, b1 = left
        a2, b2 = right
        return a1 * a2, a2 * b1 + b2

    _, h = lax.associative_scan(combine, (a, b), axis=1)
    return (h.astype(xn.dtype) * jax.nn.silu(z)) @ w_out

def second_inputs(seed: int = 0) -> dict:
    key = jax.random.key(seed)
    keys = iter(jax.random.split(key, 64))
    f32 = jnp.float32

    def nrm(shape, scale):
        return jax.random.normal(next(keys), shape, f32) * scale

    def dense(shape):
        return nrm(shape, shape[-2] ** -0.5)

    def unif(shape, lo, hi):
        return jax.random.uniform(next(keys), shape, f32, lo, hi)

    LA, LB, LC, LD = (_layers_of(m) for m in range(N_MIXERS))
    C = RWKV_HEADS * RWKV_HEAD
    nq, nkv = ATTN_HEADS * HEAD_DIM, KV_HEADS * HEAD_DIM
    a_cols = 2 * nq + 2 * nkv
    c_cols = 2 * nq + 6 * nkv + 3 * ATTN_HEADS
    lam_u = unif((LD, LRU_WIDTH), 0.9, 0.999)
    return {
        "x": nrm((BATCH, SEQ, D_MODEL), 1.0),
        "t5_table": nrm((T5_BUCKETS, ATTN_HEADS), 0.5),
        "norm_g": 1.0 + nrm((DEPTH, D_MODEL), 0.05),
        "final_g": 1.0 + nrm((D_MODEL,), 0.05),
        "a_w_in": dense((LA, D_MODEL, a_cols)),
        "a_sinks": nrm((LA, ATTN_HEADS), 0.5),
        "a_w_out": dense((LA, nq, D_MODEL)),
        "b_mu": unif((LB, 6, D_MODEL), 0.0, 1.0),
        "b_w_in": dense((LB, D_MODEL, 4 * C)),
        "b_w0": unif((LB, C), -6.0, 0.0),
        "b_w1": dense((LB, D_MODEL, RWKV_LORA_W)),
        "b_w2": dense((LB, RWKV_LORA_W, C)),
        "b_a0": nrm((LB, C), 0.5),
        "b_a1": dense((LB, D_MODEL, RWKV_LORA_A)),
        "b_a2": dense((LB, RWKV_LORA_A, C)),
        "b_k_k": 0.85 + nrm((LB, C), 0.1),
        "b_k_a": 1.0 + nrm((LB, C), 0.1),
        "b_r_k": nrm((LB, RWKV_HEADS, RWKV_HEAD), 0.1),
        "b_lnx_w": 1.0 + nrm((LB, C), 0.05),
        "b_lnx_b": nrm((LB, C), 0.01),
        "b_w_out": dense((LB, C, D_MODEL)),
        "c_w_in": dense((LC, D_MODEL, c_cols)),
        "c_cmp_pos_k": nrm((LC, NSA_CMP_LEN, HEAD_DIM), 0.1),
        "c_cmp_k_w1": dense((LC, NSA_CMP_LEN * HEAD_DIM, NSA_CMP_HIDDEN)),
        "c_cmp_k_w2": dense((LC, NSA_CMP_HIDDEN, HEAD_DIM)),
        "c_cmp_pos_v": nrm((LC, NSA_CMP_LEN, HEAD_DIM), 0.1),
        "c_cmp_v_w1": dense((LC, NSA_CMP_LEN * HEAD_DIM, NSA_CMP_HIDDEN)),
        "c_cmp_v_w2": dense((LC, NSA_CMP_HIDDEN, HEAD_DIM)),
        "c_w_out": dense((LC, nq, D_MODEL)),
        "d_w_in": dense((LD, D_MODEL, 2 * LRU_WIDTH)),
        "d_conv_w": nrm((LD, CONV_WIDTH, LRU_WIDTH), CONV_WIDTH ** -0.5),
        "d_conv_b": nrm((LD, LRU_WIDTH), 0.01),
        "d_gate_a_w": dense((LD, LRU_BLOCKS, LRU_BLOCK, LRU_BLOCK)),
        "d_gate_a_b": nrm((LD, LRU_WIDTH), 0.01),
        "d_gate_x_w": dense((LD, LRU_BLOCKS, LRU_BLOCK, LRU_BLOCK)),
        "d_gate_x_b": nrm((LD, LRU_WIDTH), 0.01),
        "d_lambda": jnp.log(lam_u) - jnp.log1p(-lam_u),
        "d_w_out": dense((LD, LRU_WIDTH, D_MODEL)),
    }

def second_block(x, t5_table, norm_g, final_g,
              a_w_in, a_sinks, a_w_out,
              b_mu, b_w_in, b_w0, b_w1, b_w2, b_a0, b_a1, b_a2, b_k_k, b_k_a, b_r_k,
              b_lnx_w, b_lnx_b, b_w_out,
              c_w_in, c_cmp_pos_k, c_cmp_k_w1, c_cmp_k_w2, c_cmp_pos_v, c_cmp_v_w1, c_cmp_v_w2, c_w_out,
              d_w_in, d_conv_w, d_conv_b, d_gate_a_w, d_gate_a_b, d_gate_x_w, d_gate_x_b,
              d_lambda, d_w_out):
    for layer in range(DEPTH):
        m, j = layer % N_MIXERS, layer // N_MIXERS
        xn = rms_norm_2(x, norm_g[layer])
        if m == 0:
            y = swa_sink_mixer(xn, a_w_in[j], a_sinks[j], a_w_out[j], t5_table)
        elif m == 1:
            y = rwkv7_mixer(xn, b_mu[j], b_w_in[j], b_w0[j], b_w1[j], b_w2[j], b_a0[j], b_a1[j],
                            b_a2[j], b_k_k[j], b_k_a[j], b_r_k[j], b_lnx_w[j], b_lnx_b[j], b_w_out[j])
        elif m == 2:
            y = nsa_mixer(xn, c_w_in[j], c_cmp_pos_k[j], c_cmp_k_w1[j], c_cmp_k_w2[j],
                          c_cmp_pos_v[j], c_cmp_v_w1[j], c_cmp_v_w2[j], c_w_out[j], t5_table)
        else:
            y = rglru_mixer(xn, d_w_in[j], d_conv_w[j], d_conv_b[j], d_gate_a_w[j], d_gate_a_b[j],
                            d_gate_x_w[j], d_gate_x_b[j], d_lambda[j], d_w_out[j])
        x = x + y.astype(x.dtype)
    return rms_norm_2(x, final_g)


def setup_inputs(seed=0):
    out = dict(first_inputs(seed))
    for name, value in second_inputs(seed + 1).items():
        if name != "x":
            out[name + "_2"] = value
    return out


def reference(
    x, positions, norm_gain, w_in, b_merge, mla_q_norm, mla_w_uq, mla_kv_norm, mla_w_ukv,
    mla_q_gain, mla_k_gain, dsa_q_gain, dsa_k_gain, w_branch_mla, w_branch_dsa, w_out,
    t5_table_2, norm_g_2, final_g_2, a_w_in_2, a_sinks_2, a_w_out_2, b_mu_2, b_w_in_2, b_w0_2,
    b_w1_2, b_w2_2, b_a0_2, b_a1_2, b_a2_2, b_k_k_2, b_k_a_2, b_r_k_2, b_lnx_w_2, b_lnx_b_2,
    b_w_out_2, c_w_in_2, c_cmp_pos_k_2, c_cmp_k_w1_2, c_cmp_k_w2_2, c_cmp_pos_v_2, c_cmp_v_w1_2,
    c_cmp_v_w2_2, c_w_out_2, d_w_in_2, d_conv_w_2, d_conv_b_2, d_gate_a_w_2, d_gate_a_b_2,
    d_gate_x_w_2, d_gate_x_b_2, d_lambda_2, d_w_out_2,
):
    x = first_block(
        x, positions, norm_gain, w_in, b_merge, mla_q_norm, mla_w_uq, mla_kv_norm, mla_w_ukv,
        mla_q_gain, mla_k_gain, dsa_q_gain, dsa_k_gain, w_branch_mla, w_branch_dsa, w_out,
    )
    return second_block(
        x, t5_table_2, norm_g_2, final_g_2, a_w_in_2, a_sinks_2, a_w_out_2, b_mu_2, b_w_in_2,
        b_w0_2, b_w1_2, b_w2_2, b_a0_2, b_a1_2, b_a2_2, b_k_k_2, b_k_a_2, b_r_k_2, b_lnx_w_2,
        b_lnx_b_2, b_w_out_2, c_w_in_2, c_cmp_pos_k_2, c_cmp_k_w1_2, c_cmp_k_w2_2,
        c_cmp_pos_v_2, c_cmp_v_w1_2, c_cmp_v_w2_2, c_w_out_2, d_w_in_2, d_conv_w_2, d_conv_b_2,
        d_gate_a_w_2, d_gate_a_b_2, d_gate_x_w_2, d_gate_x_b_2, d_lambda_2, d_w_out_2,
    )


_drawn_inputs = setup_inputs


def setup_inputs(seed=0):
    import zlib

    import numpy as np

    out = dict(_drawn_inputs(seed))
    spreads = {}
    factors = {'norm_gain': 8.0,
     'b_merge': 8.0,
     'mla_q_norm': 8.0,
     'mla_kv_norm': 8.0,
     'mla_q_gain': 8.0,
     'mla_k_gain': 8.0,
     'dsa_q_gain': 8.0,
     'dsa_k_gain': 8.0,
     'norm_g_2': 5.798,
     'a_sinks_2': 64.0}
    for name, (base, spread) in spreads.items():
        noise = np.random.default_rng([zlib.crc32(name.encode()), seed]).standard_normal(out[name].shape)
        drawn = base * np.exp(spread * noise) if base else spread * noise
        out[name] = __import__('jax').numpy.asarray(drawn.astype(out[name].dtype))
    for name, factor in factors.items():
        out[name] = (out[name] * factor).astype(out[name].dtype)
    return out
```

```python
import math
from contextlib import ExitStack

import numpy as np
import concourse.bass as bass
from concourse import mybir
from concourse.alu_op_type import AluOpType as ALU

F32 = mybir.dt.float32
F32R = mybir.dt.float32r
BF16 = mybir.dt.bfloat16
I32 = mybir.dt.int32
ACT = mybir.ActivationFunctionType
AX = mybir.AxisListType

P = 128
T = 2048
NT = T // P
D = 1024
KD = D // P
GT = 512
NG = T // GT
EPS = 1e-6

H = 8
QK, NOPE, ROPE_M = 96, 64, 32
HD = 64
KV = 2
IDX = 32
TOPK = min(256, T // 4)
ROT_D, ROT_I = 16, 8
THETA = 500000.0

SPLITS = [256, 128, 32, 512, 512, 128, 128, 512, 256, 32, 8, 1024, 1024]
(C_Q, C_KV, C_PE, C_GA, C_QB, C_KB, C_VB, C_GB, C_QI, C_KI, C_WI, C_MA, C_MB) = (
    sum(SPLITS[:i]) for i in range(len(SPLITS)))
C_END = sum(SPLITS)

TM_PE, TM_QB, TM_KB, TM_VB, TM_QI, TM_KI, TM_WI = 0, 32, 544, 672, 800, 1056, 1088
TM_W = 1096
TM_CHUNK = TM_W // 4

WH, WKV, WG = 16, 4, 4
WINDOW = 128
NEG = -1e30
ND = 257


class Sems:

    def __init__(self, nc):
        self.nc, self.live = nc, []

    def __call__(self, name, count=None):
        if count is None:
            self.live.append(self.nc.alloc_semaphore(name=name))
            return self.live[-1]
        return [self(f"{name}{i}") for i in range(count)]

    def end_stage(self):
        self.nc.clear_and_free_semaphores(self.live)
        self.nc.all_engine_barrier()
        self.live = []


def mm3(pe, out, l, r, start, stop):
    pe.matmul(out, l[0], r[1], start=start, stop=False)
    pe.matmul(out, l[1], r[0], start=False, stop=False)
    return pe.matmul(out, l[0], r[0], start=False, stop=stop)


def stage_norm(nc, sem, tag, x_dram, gain_dram, ident, hT):
    hi, lo = hT
    with ExitStack() as c:
        sb = lambda n, s, d=F32: c.enter_context(nc.sbuf_tensor(f"{tag}_{n}", s, d))
        xt = sb("xt", [P, 3, D])
        h = sb("h", [P, 2, D])
        junk = sb("junk", [P, D])
        g = sb("g", [P, 2, KD, P])
        gain = sb("gain", [P, KD])
        ss = sb("ss", [P, NT])
        ms = sb("ms", [P, NT])
        sd = sb("sd", [P, NT])
        rs = sb("rs", [P, NT])
        tp = c.enter_context(nc.psum_tensor(f"{tag}_tp", [P, 2, KD, P], F32))
        x_in = sem(f"{tag}_x_in", 3)
        gain_in, squared, meaned, rooted, normed, turned, gained, hi_done, lo_done = (
            sem(f"{tag}_{n}") for n in ("gain_in", "squared", "meaned", "rooted", "normed", "turned",
                                        "gained", "hi_done", "lo_done"))
        block = c.enter_context(nc.Block())

        @block.sync
        def _(sp):
            sp.dma_start(gain[:], gain_dram.rearrange("(k p) -> p k", p=P),
                         allow_slow_non_contiguous=True).then_inc(gain_in, 16)
            for t in range(NT):
                if t >= 3:
                    sp.wait_ge(normed, t - 2)
                sp.dma_start(xt[:, t % 3], x_dram[t * P:(t + 1) * P, :]).then_inc(x_in[t % 3], 16)

        @block.scalar
        def _(act):
            def square(t):
                act.wait_ge(x_in[t % 3], 16 * (t // 3 + 1))
                if t >= 1:
                    act.wait_ge(squared, t)
                nc.scalar.activation(junk[:], xt[:, t % 3], ACT.Square,
                                     accum_out=ss[:, t:t + 1]).then_inc(squared, 1)

            square(0)
            for t in range(NT):
                if t + 1 < NT:
                    square(t + 1)
                act.wait_ge(meaned, t + 1)
                nc.scalar.activation(sd[:, t:t + 1], ms[:, t:t + 1], ACT.Sqrt).then_inc(rooted, 1)
                if t >= 1:
                    act.wait_ge(gained, t)
                    nc.scalar.activation(hi[:, :, (t - 1) * P:t * P], g[:, (t - 1) % 2],
                                         ACT.Copy).then_inc(hi_done, 1)
            act.wait_ge(gained, NT)
            nc.scalar.activation(hi[:, :, (NT - 1) * P:NT * P], g[:, (NT - 1) % 2],
                                 ACT.Copy).then_inc(hi_done, 1)

        @block.vector
        def _(dve):
            def mean(t):
                dve.wait_ge(squared, t + 1)
                nc.vector.tensor_scalar(ms[:, t:t + 1], ss[:, t:t + 1], 1.0 / D, EPS, ALU.mult,
                                        ALU.add).then_inc(meaned, 1)

            def norm(t):
                dve.wait_ge(rooted, t + 1)
                nc.vector.reciprocal(rs[:, t:t + 1], sd[:, t:t + 1])
                dve.drain()
                if t >= 2:
                    dve.wait_ge(turned, t - 1)
                nc.vector.tensor_scalar(h[:, t % 2], xt[:, t % 3], rs[:, t:t + 1], None,
                                        ALU.mult).then_inc(normed, 1)

            def gains(t):
                dve.wait_ge(turned, t + 1)
                if t >= 2:
                    dve.wait_ge(lo_done, t - 1)
                nc.vector.tensor_tensor(g[:, t % 2], tp[:, t % 2],
                                        gain[:].unsqueeze(2).broadcast_to([P, KD, P]),
                                        ALU.mult).then_inc(gained, 1)

            dve.wait_ge(gain_in, 16)
            mean(0)
            for t in range(NT):
                norm(t)
                if t + 1 < NT:
                    mean(t + 1)
                if t >= 1:
                    gains(t - 1)
            gains(NT - 1)

        @block.gpsimd
        def _(pool):
            for t in range(NT):
                pool.wait_ge(hi_done, t + 1)
                s = slice(t * P, (t + 1) * P)
                nc.gpsimd.tensor_tensor(lo[:, :, s], g[:, t % 2], hi[:, :, s].bitcast(F32),
                                        ALU.subtract).then_inc(lo_done, 1)

        @block.tensor
        def _(pe):
            for t in range(NT):
                pe.wait_ge(normed, t + 1)
                if t >= 2:
                    pe.wait_ge(gained, t - 1)
                for k in range(KD):
                    last = nc.tensor.transpose(tp[:, t % 2, k], h[:, t % 2, k * P:(k + 1) * P], ident[:])
                last.then_inc(turned, 1)


class Run:

    def __init__(self, kind, count, columns, store, func=ACT.Copy, bias=False):
        self.kind, self.count, self.columns, self.store = kind, count, columns, store
        self.func, self.bias = func, bias


def each_chunk(eng, runs, body):
    n = 0
    for run in runs:
        if run.kind == "fm" and run.count >= 4:
            with eng.Fori(0, run.count // 2) as i:
                for p in (0, 1):
                    body(n + p + 2 * i, (n + p) % 2, (n + p) // 2 + i, p + 2 * i, run)
        else:
            for j in range(run.count):
                body(n + j, (n + j) % 2, (n + j) // 2, j, run)
        n += run.count


def stage_project(nc, sem, tag, hT, weight, width, runs, bias_dram=None):
    n_tm = sum(r.count for r in runs if r.kind == "tm")
    total = sum(r.count for r in runs)
    w_view = weight.rearrange("(k p) n -> p k n", p=P)
    parts = [len(r.columns(j if r.kind == "tm" else 0)) for r in runs for j in range(r.count)]
    assert all(x == 1 for x in parts[n_tm:])

    def first_step(n):
        if isinstance(n, int) and n <= n_tm:
            return NT * n
        return NG * n + (NT - NG) * n_tm

    def loaded(n, par, use):
        if isinstance(n, int):
            return 16 * sum(parts[m] for m in range(par, n + 1, 2))
        return 16 * (use + 1 + sum(parts[m] - 1 for m in range(par, n_tm, 2)))

    def steps(n, par, run):
        if run.kind == "tm":
            return [(first_step(n) + t, t % 8, t % 4, t, width) for t in range(NT)]
        return [(first_step(n) + g, g + NG * ((par + n_tm) % 2), g, g, GT) for g in range(NG)]

    def stores_before(n, g):
        if isinstance(n, int) and n < n_tm:
            return 4 * n + g // 4
        return n + 3 * n_tm

    with ExitStack() as c:
        sb = lambda n, s, d=F32: c.enter_context(nc.sbuf_tensor(f"{tag}_{n}", s, d))
        ws = sb("ws", [P, 2, KD, width])
        wh = sb("wh", [P, 2, KD, width], F32R)
        wl = sb("wl", [P, 2, KD, width], F32R)
        ob = sb("ob", [P, 4, GT])
        bias_sb = sb("bias", [P, bias_dram.shape[0] // P]) if bias_dram is not None else None
        bias_now = sb("bias_now", [P, 2])
        ps = c.enter_context(nc.psum_tensor(f"{tag}_ps", [P, 8, GT], F32))
        w_in = sem(f"{tag}_w_in", 2)
        stored = sem(f"{tag}_stored", 4)
        bias_in, w_split, filled, evacuated = (
            sem(f"{tag}_{n}") for n in ("bias_in", "w_split", "filled", "evacuated"))
        block = c.enter_context(nc.Block())

        @block.sync
        def _(sp):
            if bias_sb is not None:
                sp.dma_start(bias_sb[:], bias_dram.rearrange("(j p) -> p j", p=P),
                             allow_slow_non_contiguous=True).then_inc(bias_in, 16)

            def load(n, par, use, j, run):
                if not isinstance(n, int) or n >= 2:
                    sp.wait_ge(w_split, n - 1)
                for at, c0, w in run.columns(j):
                    sp.dma_start(ws[:, par, :, at:at + w],
                                 w_view[:, :, bass.ds(c0, w)]).then_inc(w_in[par], 16)

            each_chunk(sp, runs, load)

        @block.vector
        def _(dve):
            def split(n, par, use, j, run):
                w = width if run.kind == "tm" else P
                dve.wait_ge(w_in[par], loaded(n, par, use))
                if not isinstance(n, int) or n >= 2:
                    dve.wait_ge(filled, first_step(n - 1))
                nc.vector.tensor_copy(wh[:, par, :, 0:w], ws[:, par, :, 0:w])
                dve.drain()
                nc.vector.tensor_tensor(wl[:, par, :, 0:w], ws[:, par, :, 0:w],
                                        wh[:, par, :, 0:w].bitcast(F32), ALU.subtract).then_inc(w_split, 1)

            each_chunk(dve, runs, split)

        @block.tensor
        def _(pe):
            hi, lo = hT

            def multiply(n, par, use, j, run):
                pe.wait_ge(w_split, n + 1)
                for u, bank, _, g, w in steps(n, par, run):
                    if not isinstance(u, int) or u >= 8:
                        pe.wait_ge(evacuated, u - 7)
                    for k in range(KD):
                        if run.kind == "tm":
                            s = slice(g * P, (g + 1) * P)
                            l, r = (hi[:, k, s], lo[:, k, s]), (wh[:, par, k, 0:w], wl[:, par, k, 0:w])
                        else:
                            s = slice(g * GT, (g + 1) * GT)
                            l, r = (wh[:, par, k, 0:P], wl[:, par, k, 0:P]), (hi[:, k, s], lo[:, k, s])
                        last = mm3(nc.tensor, ps[:, bank, 0:w], l, r, start=k == 0, stop=k == KD - 1)
                    last.then_inc(filled, 1)

            each_chunk(pe, runs, multiply)

        @block.scalar
        def _(act):
            if bias_sb is not None:
                act.wait_ge(bias_in, 16)

            def evacuate(n, par, use, j, run):
                if run.bias:
                    nc.scalar.activation(bias_now[:, par:par + 1], bias_sb[:, bass.ds(j, 1)], ACT.Copy)
                    act.drain()
                for u, bank, slot, g, w in steps(n, par, run):
                    target = ob[:, slot, 0:w]
                    if not isinstance(n, int) or stores_before(n, g) >= 1:
                        act.wait_ge(stored[slot], 16 * stores_before(n, g))
                    act.wait_ge(filled, u + 1)
                    if run.bias:
                        nc.scalar.activation(target, ps[:, bank, 0:w], run.func,
                                             bias=bias_now[:, par:par + 1]).then_inc(evacuated, 1)
                    else:
                        nc.scalar.activation(target, ps[:, bank, 0:w], run.func).then_inc(evacuated, 1)
                    act.wait_ge(evacuated, u + 1)
                    act.dma_start(run.store(j, g), target).then_inc(stored[slot], 16)

            each_chunk(act, runs, evacuate)
            for g in range(4):
                act.wait_ge(stored[g], 16 * (total + 3 * n_tm))


FREQS = [(ROPE_M, 0), (ROT_D, ROPE_M // 2), (ROT_I, ROPE_M // 2 + ROT_D // 2)]
NF = (ROPE_M + ROT_D + ROT_I) // 2
TWO_PI = 2 * math.pi
PI_A = 6.28125
PI_B = float(np.float32(np.round((TWO_PI - PI_A) * 2.0 ** 19) / 2.0 ** 19))
PI_C = float(TWO_PI - PI_A - PI_B)
ROUNDER = 1.5 * 2.0 ** 23


def stage_qkv(nc, sem, ident, a, cqT, tm, qkT, qbT, kbT, qiT, kiT, va, vb, wi):
    with ExitStack() as c:
        sb = lambda n, s, d=F32: c.enter_context(nc.sbuf_tensor(f"b_{n}", s, d))
        pos_i = sb("pos_i", [P, NT], I32)
        pos = sb("pos", [P, NT])
        freq = sb("freq", [P, NF])
        ang = sb("ang", [P, NT, NF])
        turns = sb("turns", [P, NT, NF])
        red = sb("red", [P, 2, NT, NF])
        cos2 = sb("cos2", [P, NT, 2 * NF])
        sin2 = sb("sin2", [P, NT, 2 * NF])
        c_gain = sb("c_gain", [P, 3])
        qk_gain = sb("qk_gain", [P, 2, QK])
        b_gain = sb("b_gain", [P, 2, HD])
        ones = sb("ones", [P, 2])
        uq = sb("uq", [P, 2, H * QK])
        uqs = [sb(f"uq_{n}", [P, 2, H * QK], F32R) for n in ("hi", "lo")]
        ukv = sb("ukv", [P, D])
        ukvs = [sb(f"ukv_{n}", [P, D], F32R) for n in ("hi", "lo")]
        tmb = sb("tmb", [P, 3, TM_W])
        cq = sb("cq", [P, 2, 3, P])
        csq = sb("csq", [P, 2, 3, P])
        cg = sb("cg", [P, 2, 3, P])
        ch = sb("ch", [P, 2, 3, P], F32R)
        cl = sb("cl", [P, 2, 3, P], F32R)
        st1 = sb("st1", [P, NT, 2])
        sd1 = sb("sd1", [P, NT, 2])
        rs1 = sb("rs1", [P, NT, 2])
        qk = sb("qk", [P, 3, 2 * H, QK])
        qb = sb("qb", [P, 2, H + KV, HD])
        sq = sb("sq", [P, 2 * H * QK + (H + KV) * HD])
        st2 = sb("st2", [P, 26])
        ms2 = sb("ms2", [P, 26])
        sd2 = sb("sd2", [P, 26])
        rs2 = sb("rs2", [P, 26])
        rot = sb("rot", [P, 2, 2 * H, ROPE_M])
        rot_p = sb("rot_p", [P, 2, H + KV, ROT_D])
        v = sb("v", [P, 3, 640])
        vh = sb("vh", [P, 2, 640], F32R)
        vl = sb("vl", [P, 2, 640], F32R)
        th = sb("th", [P, 3, GT], F32R)
        tl = sb("tl", [P, 3, GT], F32R)
        p_ss = c.enter_context(nc.psum_tensor("b_ps_ss", [P, 4], F32))
        p_up = c.enter_context(nc.psum_tensor("b_ps_up", [P, 4, GT], F32))
        p_t = c.enter_context(nc.psum_tensor("b_ps_t", [P, 3, GT], F32))
        const_in, w_ready, trig_r, trig, filled_c = (
            sem(f"b_{n}") for n in ("const_in", "w_ready", "trig_r", "trig", "ones_made"))
        tile_in = sem("b_tile_in", 3)
        (c_squared, c_gained, c_hi, c_lo, summed, meaned1, rooted1, scaled1, up, up_read, pe_spread,
         squared2, meaned2, rooted2, normed, gained, roped, roped_p, v_hi, v_lo, turned, t_hi, t_lo) = (
            sem(f"b_{n}") for n in
            ("c_squared", "c_gained", "c_hi", "c_lo", "summed", "meaned1", "rooted1", "scaled1", "up",
             "up_read", "pe_spread", "squared2", "meaned2", "rooted2", "normed", "gained", "roped",
             "roped_p", "v_hi", "v_lo", "turned", "t_hi", "t_lo"))
        t_stored = sem("b_t_stored", 3)
        v_stored = sem("b_v_stored", 2)
        wi_stored = sem("b_wi_stored", 3)
        block = c.enter_context(nc.Block())
        NB = 6

        def staged(parts):
            for i in range(NT + len(parts) - 1):
                for k in reversed(range(len(parts))):
                    if 0 <= i - k < NT:
                        parts[k](i - k)

        def stored_of(u, slot):
            return sum(96 if w % NB == 5 else 32 for w in range(slot, u, 3))

        def rotate(ops, eng, x, table, t, tmp, done):
            rd, f0 = FREQS[table]
            n, h = x.shape[1], rd // 2
            spread = lambda tab, a0, a1: tab[:, t, 2 * f0 + a0:2 * f0 + a1].unsqueeze(1)\
                .broadcast_to([P, n, a1 - a0])
            ops.tensor_tensor(tmp[:, 1, 0:n, 0:h], x[:, :, h:rd], spread(sin2, 0, h), ALU.mult)
            ops.tensor_tensor(tmp[:, 1, 0:n, h:rd], x[:, :, 0:h], spread(sin2, h, rd), ALU.mult)
            ops.tensor_tensor(tmp[:, 0, 0:n, 0:rd], x, spread(cos2, 0, rd), ALU.mult)
            eng.drain()
            last = ops.tensor_tensor(x, tmp[:, 0, 0:n, 0:rd], tmp[:, 1, 0:n, 0:rd], ALU.add)
            if done is not None:
                last.then_inc(done, 1)
            return last

        @block.sync
        def _(sp):
            sp.dma_start(pos_i[:], a["positions"][0].rearrange("(t p) -> p t", p=P),
                         allow_slow_non_contiguous=True).then_inc(const_in, 16)
            sp.dma_start(c_gain[:, 0:2], a["mla_q_norm"][0].rearrange("(k p) -> p k", p=P),
                         allow_slow_non_contiguous=True).then_inc(const_in, 16)
            sp.dma_start(c_gain[:, 2:3], a["mla_kv_norm"].rearrange("a p -> p a"),
                         allow_slow_non_contiguous=True).then_inc(const_in, 16)
            for dst, name in ((qk_gain[:, 0], "mla_q_gain"), (qk_gain[:, 1], "mla_k_gain"),
                              (b_gain[:, 0], "dsa_q_gain"), (b_gain[:, 1], "dsa_k_gain")):
                sp.dma_start(dst, a[name][0].partition_broadcast(P)).then_inc(const_in, 16)
            sp.dma_start(uq[:], a["mla_w_uq"][0].rearrange("(k p) n -> p k n", p=P)).then_inc(const_in, 16)
            sp.dma_start(ukv[:], a["mla_w_ukv"][0]).then_inc(const_in, 16)

            def load(t):
                if t >= 3:
                    sp.wait_ge(turned, NB * (t - 2))
                    sp.wait_ge(v_lo, t - 2)
                    sp.wait_ge(wi_stored[t % 3], 16 * (t // 3))
                if t >= 2:
                    sp.wait_ge(c_gained, t - 1)
                    sp.wait_ge(c_squared, t - 1)
                s = slice(t * P, (t + 1) * P)
                sp.dma_start(tmb[:, t % 3], tm[s, :]).then_inc(tile_in[t % 3], 16)
                sp.dma_start(cq[:, t % 2], cqT.rearrange("(k p) t -> p k t", p=P)[:, :, s])\
                    .then_inc(tile_in[t % 3], 16)

            def store_values(t):
                s = slice(t * P, (t + 1) * P)
                sp.wait_ge(v_lo, t + 1)
                for half, src in ((0, vh), (1, vl)):
                    sp.dma_start(va[half, s, :], src[:, t % 2, 0:512].bitcast(F32)).then_inc(v_stored[t % 2], 16)
                    sp.dma_start(vb[half, s, :], src[:, t % 2, 512:640].bitcast(F32)).then_inc(v_stored[t % 2], 16)
                sp.wait_ge(roped_p, t + 1)
                sp.dma_start(wi[s, :], tmb[:, t % 3, TM_WI:TM_W]).then_inc(wi_stored[t % 3], 16)

            def store_turned(t):
                s = slice(t * P, (t + 1) * P)
                for b in range(NB):
                    u = NB * t + b
                    sp.wait_ge(t_lo, u + 1)
                    for half, src in ((0, th), (1, tl)):
                        x = src[:, u % 3].bitcast(F32).rearrange("p (j t) -> p j t", t=P)
                        done = t_stored[u % 3]
                        if b < 4:
                            sp.dma_start(qkT[half, 4 * b:4 * b + 4, :, s].rearrange("h d t -> d h t"),
                                         x[0:QK]).then_inc(done, 16)
                        elif b == 4:
                            sp.dma_start(qbT[half, :, :, s].rearrange("j p t -> p j t"), x).then_inc(done, 16)
                        else:
                            sp.dma_start(kbT[half, :, s], x[:, 0]).then_inc(done, 16)
                            sp.dma_start(qiT[half, :, :, s].rearrange("j p t -> p j t"),
                                         x[:, 1:3]).then_inc(done, 16)
                            sp.dma_start(kiT[half, :, s], x[0:IDX, 3]).then_inc(done, 16)

            staged([load, store_values, store_turned])
            for n in range(3):
                sp.wait_ge(t_stored[n], stored_of(NB * NT, n))
                sp.wait_ge(wi_stored[n], 16 * len(range(n, NT, 3)))
            for n in range(2):
                sp.wait_ge(v_stored[n], 64 * (NT // 2))

        @block.scalar
        def _(act):
            act.wait_ge(trig_r, 1)
            nc.scalar.activation(red[:], red[:], ACT.Sin).then_inc(trig_r, 1)

            def part1(t):
                act.wait_ge(tile_in[t % 3], 32 * (t // 3 + 1))
                if t >= 2:
                    act.wait_ge(summed, t - 1)
                nc.scalar.activation(csq[:, t % 2], cq[:, t % 2], ACT.Square).then_inc(c_squared, 1)
                act.wait_ge(c_gained, t + 1)
                if t >= 2:
                    act.wait_ge(up, 2 * (t - 1))
                nc.scalar.activation(ch[:, t % 2], cg[:, t % 2], ACT.Copy).then_inc(c_hi, 1)
                act.wait_ge(meaned1, t + 1)
                nc.scalar.activation(sd1[:, t], st1[:, t], ACT.Sqrt).then_inc(rooted1, 1)
                act.wait_ge(scaled1, t + 1)
                act.wait_ge(up, 2 * t + 2)
                if t >= 3:
                    act.wait_ge(turned, NB * (t - 2))
                    act.wait_ge(v_lo, t - 2)
                for b in range(2):
                    nc.scalar.activation(qk[:, t % 3, 4 * b:4 * b + 4],
                                         p_up[:, b, 0:4 * QK].rearrange("p (h d) -> p h d", d=QK),
                                         ACT.Copy, scale=rs1[:, t, 0:1])
                for b in range(2):
                    kv = p_up[:, 2 + b].rearrange("p (h d) -> p h d", d=NOPE + HD)
                    nc.scalar.activation(qk[:, t % 3, H + 4 * b:H + 4 * b + 4, 0:NOPE], kv[:, :, 0:NOPE],
                                         ACT.Copy, scale=rs1[:, t, 1:2])
                    last = nc.scalar.activation(
                        v[:, t % 3, 256 * b:256 * b + 256].rearrange("p (h d) -> p h d", d=HD),
                        kv[:, :, NOPE:], ACT.Copy, scale=rs1[:, t, 1:2])
                last.then_inc(up_read, 1)

            def part2(t):
                act.wait_ge(up_read, t + 1)
                act.wait_ge(pe_spread, t + 1)
                if t >= 1:
                    act.wait_ge(meaned2, t)
                n = 2 * H * QK
                nc.scalar.activation(sq[:, 0:n], qk[:, t % 3].rearrange("p h d -> p (h d)"), ACT.Square)
                nc.scalar.activation(sq[:, n:], tmb[:, t % 3, TM_QB:TM_VB], ACT.Square).then_inc(squared2, 1)
                if t >= 2:
                    act.wait_ge(v_stored[t % 2], 64 * (t // 2))
                    act.wait_ge(v_lo, t - 1)
                nc.scalar.activation(vh[:, t % 2], v[:, t % 3], ACT.Copy).then_inc(v_hi, 1)
                act.wait_ge(meaned2, t + 1)
                if t >= 1:
                    act.wait_ge(normed, t)
                nc.scalar.activation(sd2[:], ms2[:], ACT.Sqrt).then_inc(rooted2, 1)

            def part3(t):
                for b in range(NB):
                    u = NB * t + b
                    act.wait_ge(turned, u + 1)
                    if u >= 3:
                        act.wait_ge(t_stored[u % 3], stored_of(u - 2, u % 3))
                        act.wait_ge(t_lo, u - 2)
                    rows = QK if b < 4 else P
                    parts = [(rows, 0, GT)] if b < 5 else [(P, 0, 3 * P), (IDX, 3 * P, GT)]
                    for r, x0, x1 in parts:
                        last = nc.scalar.activation(th[0:r, u % 3, x0:x1], p_t[0:r, u % 3, x0:x1], ACT.Copy)
                    last.then_inc(t_hi, 1)

            staged([part1, part2, part3])

        @block.vector
        def _(dve):
            for n, (rd, f0) in enumerate(FREQS):
                for f in range(rd // 2):
                    value = float(np.float32(THETA) ** (-np.float32(2 * f) / np.float32(rd)))
                    nc.vector.memset(freq[:, f0 + f:f0 + f + 1], value)
            nc.vector.memset(ones[:], 1.0).then_inc(filled_c, 1)
            dve.wait_ge(const_in, 16 * 9)
            nc.vector.tensor_copy(pos[:], pos_i[:])
            nc.vector.tensor_copy(uqs[0][:], uq[:])
            nc.vector.tensor_copy(ukvs[0][:], ukv[:])
            dve.drain()
            nc.vector.tensor_tensor(uqs[1][:], uq[:], uqs[0][:].bitcast(F32), ALU.subtract)
            nc.vector.tensor_tensor(ukvs[1][:], ukv[:], ukvs[0][:].bitcast(F32), ALU.subtract)\
                .then_inc(w_ready, 1)
            nc.vector.tensor_tensor(ang[:], pos[:].unsqueeze(2).broadcast_to([P, NT, NF]),
                                    freq[:].unsqueeze(1).broadcast_to([P, NT, NF]), ALU.mult)
            dve.drain()
            for which, quarter in ((0, 0.25), (1, 0.0)):
                nc.vector.tensor_scalar(turns[:], ang[:], 1 / TWO_PI, quarter, ALU.mult, ALU.add)
                dve.drain()
                nc.vector.tensor_scalar(turns[:], turns[:], ROUNDER, None, ALU.add)
                dve.drain()
                nc.vector.tensor_scalar(turns[:], turns[:], ROUNDER, None, ALU.subtract)
                dve.drain()
                src = ang[:]
                for part in (PI_A, PI_B, PI_C):
                    nc.vector.scalar_tensor_tensor(out=red[:, which], in0=turns[:], scalar=-part, in1=src,
                                                   op0=ALU.mult, op1=ALU.add)
                    dve.drain()
                    src = red[:, which]
                if quarter:
                    nc.vector.tensor_scalar(red[:, which], red[:, which], math.pi / 2, None, ALU.add)
                    dve.drain()
            last = nc.vector.tensor_scalar(red[:], red[:], 3.1415925, -3.1415925, ALU.min, ALU.max)
            last.then_inc(trig_r, 1)
            dve.wait_ge(trig_r, 2)
            for rd, f0 in FREQS:
                h = rd // 2
                for half in range(2):
                    at = slice(2 * f0 + half * h, 2 * f0 + half * h + h)
                    nc.vector.tensor_copy(cos2[:, :, at], red[:, 0, :, f0:f0 + h])
                    last = nc.vector.tensor_scalar(sin2[:, :, at], red[:, 1, :, f0:f0 + h],
                                                   1.0 if half else -1.0, None, ALU.mult)
            last.then_inc(trig, 1)

            def part1(t):
                dve.wait_ge(tile_in[t % 3], 32 * (t // 3 + 1))
                if t >= 2:
                    dve.wait_ge(c_lo, t - 1)
                    dve.wait_ge(c_hi, t - 1)
                nc.vector.tensor_tensor(cg[:, t % 2], cq[:, t % 2],
                                        c_gain[:].unsqueeze(2).broadcast_to([P, 3, P]),
                                        ALU.mult).then_inc(c_gained, 1)
                dve.wait_ge(c_hi, t + 1)
                nc.vector.tensor_tensor(cl[:, t % 2], cg[:, t % 2], ch[:, t % 2].bitcast(F32),
                                        ALU.subtract).then_inc(c_lo, 1)
                dve.wait_ge(summed, t + 1)
                nc.vector.tensor_scalar(st1[:, t, 0:1], p_ss[:, 0:1], 1.0 / 256, EPS, ALU.mult, ALU.add)
                nc.vector.tensor_scalar(st1[:, t, 1:2], p_ss[:, 2:3], 1.0 / 128, EPS, ALU.mult,
                                        ALU.add).then_inc(meaned1, 1)
                dve.wait_ge(rooted1, t + 1)
                nc.vector.reciprocal(rs1[:, t], sd1[:, t]).then_inc(scaled1, 1)

            def part2(t):
                dve.wait_ge(squared2, t + 1)
                n = 2 * H * QK
                nc.vector.tensor_reduce(st2[:, 0:16], sq[:, 0:n].rearrange("p (h d) -> p h d", d=QK),
                                        AX.X, ALU.add)
                nc.vector.tensor_reduce(st2[:, 16:26], sq[:, n:].rearrange("p (h d) -> p h d", d=HD),
                                        AX.X, ALU.add)
                dve.drain()
                if t >= 1:
                    dve.wait_ge(rooted2, t)
                nc.vector.tensor_scalar(ms2[:, 0:16], st2[:, 0:16], 1.0 / QK, EPS, ALU.mult, ALU.add)
                nc.vector.tensor_scalar(ms2[:, 16:26], st2[:, 16:26], 1.0 / HD, EPS, ALU.mult,
                                        ALU.add).then_inc(meaned2, 1)
                dve.wait_ge(rooted2, t + 1)
                nc.vector.reciprocal(rs2[:], sd2[:])
                dve.drain()
                if t >= 2:
                    dve.wait_ge(turned, NB * (t - 1))
                nc.vector.tensor_tensor(qk[:, t % 3], qk[:, t % 3],
                                        rs2[:, 0:16].unsqueeze(2).broadcast_to([P, 16, QK]), ALU.mult)
                nc.vector.tensor_tensor(qb[:, t % 2],
                                        tmb[:, t % 3, TM_QB:TM_VB].rearrange("p (h d) -> p h d", d=HD),
                                        rs2[:, 16:26].unsqueeze(2).broadcast_to([P, 10, HD]),
                                        ALU.mult).then_inc(normed, 1)
                dve.wait_ge(gained, t + 1)
                rotate(nc.vector, dve, qk[:, t % 3, :, NOPE:QK], 0, t, rot, roped)

            def part3(t):
                for b in range(NB):
                    u = NB * t + b
                    dve.wait_ge(t_hi, u + 1)
                    parts = [(QK if b < 4 else P, 0, GT)] if b < 5 else [(P, 0, 3 * P), (IDX, 3 * P, GT)]
                    for r, x0, x1 in parts:
                        last = nc.vector.tensor_tensor(tl[0:r, u % 3, x0:x1], p_t[0:r, u % 3, x0:x1],
                                                       th[0:r, u % 3, x0:x1].bitcast(F32), ALU.subtract)
                    last.then_inc(t_lo, 1)

            staged([part1, part2, part3])

        @block.gpsimd
        def _(pool):
            pool.wait_ge(const_in, 16 * 9)
            pool.wait_ge(trig, 1)

            def part1(t):
                pool.wait_ge(tile_in[t % 3], 32 * (t // 3 + 1))
                if t >= 3:
                    pool.wait_ge(turned, NB * (t - 2))
                nc.gpsimd.tensor_copy(qk[:, t % 3, H:2 * H, NOPE:QK],
                                      tmb[:, t % 3, 0:ROPE_M].unsqueeze(1).broadcast_to([P, H, ROPE_M]))
                nc.gpsimd.tensor_copy(v[:, t % 3, 512:640], tmb[:, t % 3, TM_VB:TM_QI]).then_inc(pe_spread, 1)

            def part2(t):
                pool.wait_ge(v_hi, t + 1)
                nc.gpsimd.tensor_tensor(vl[:, t % 2], v[:, t % 3], vh[:, t % 2].bitcast(F32),
                                        ALU.subtract).then_inc(v_lo, 1)
                ix = tmb[:, t % 3, TM_QI:TM_WI].rearrange("p (h d) -> p h d", d=IDX)
                rotate(nc.gpsimd, pool, ix[:, :, 0:ROT_I], 2, t, rot_p, None)
                nc.gpsimd.tensor_scalar(tmb[:, t % 3, TM_WI:TM_W], tmb[:, t % 3, TM_WI:TM_W],
                                        H ** -0.5 * IDX ** -0.5, None, ALU.mult)
                pool.wait_ge(normed, t + 1)
                for n in range(2):
                    x = qk[:, t % 3, H * n:H * n + H]
                    last = nc.gpsimd.tensor_tensor(x, x, qk_gain[:, n].unsqueeze(1)
                                                   .broadcast_to([P, H, QK]), ALU.mult)
                last.then_inc(gained, 1)
                for n, (h0, h1) in enumerate(((0, H), (H, H + KV))):
                    x = qb[:, t % 2, h0:h1]
                    nc.gpsimd.tensor_tensor(x, x, b_gain[:, n].unsqueeze(1)
                                            .broadcast_to([P, h1 - h0, HD]), ALU.mult)
                pool.drain()
                rotate(nc.gpsimd, pool, qb[:, t % 2, :, 0:ROT_D], 1, t, rot_p, roped_p)

            staged([part1, part2])

        @block.tensor
        def _(pe):
            pe.wait_ge(filled_c, 1)
            pe.wait_ge(w_ready, 1)

            def part1(t):
                pe.wait_ge(c_squared, t + 1)
                if t >= 1:
                    pe.wait_ge(meaned1, t)
                for k in range(2):
                    nc.tensor.matmul(p_ss[:, 0:2], csq[:, t % 2, k], ones[:], start=k == 0, stop=k == 1)
                nc.tensor.matmul(p_ss[:, 2:4], csq[:, t % 2, 2], ones[:], start=True, stop=True)\
                    .then_inc(summed, 1)
                pe.wait_ge(c_lo, t + 1)
                if t >= 1:
                    pe.wait_ge(up_read, t)
                for b in range(2):
                    for k in range(2):
                        s = slice(4 * QK * b, 4 * QK * (b + 1))
                        last = mm3(nc.tensor, p_up[:, b, 0:4 * QK], (ch[:, t % 2, k], cl[:, t % 2, k]),
                                   (uqs[0][:, k, s], uqs[1][:, k, s]), start=k == 0, stop=k == 1)
                last.then_inc(up, 1)
                for b in range(2):
                    s = slice(GT * b, GT * (b + 1))
                    last = mm3(nc.tensor, p_up[:, 2 + b], (ch[:, t % 2, 2], cl[:, t % 2, 2]),
                               (ukvs[0][:, s], ukvs[1][:, s]), start=True, stop=True)
                last.then_inc(up, 1)

            def part3(t):
                pe.wait_ge(roped, t + 1)
                pe.wait_ge(roped_p, t + 1)
                for b in range(NB):
                    u = NB * t + b
                    if u >= 3:
                        pe.wait_ge(t_lo, u - 2)
                    if b < 4:
                        blocks = [(QK, qk[:, t % 3, 4 * b + j]) for j in range(4)]
                    elif b == 4:
                        blocks = [(P, qb[:, t % 2, 2 * j:2 * j + 2]) for j in range(4)]
                    else:
                        x = tmb[:, t % 3]
                        blocks = [(P, qb[:, t % 2, H:H + KV]), (P, x[:, TM_QI:TM_QI + P]),
                                  (P, x[:, TM_QI + P:TM_KI]), (IDX, x[:, TM_KI:TM_WI])]
                    for j, (rows, src) in enumerate(blocks):
                        last = nc.tensor.transpose(p_t[0:rows, u % 3, j * P:(j + 1) * P], src, ident[:])
                    last.then_inc(turned, 1)

            staged([part1, lambda t: None, part3])


class Attention:
    width = T

    def pe_start(self, pe): ...
    def dve_start(self, dve): ...
    def act_start(self, act): ...
    def pool_start(self, pool): ...
    def wait_bias(self, dve, n, s): ...
    def act_sub(self, act, n, s, shift): ...

    def least_max(self, n, s):
        return -3e38

    def is_sink(self, n, j):
        return False

    def column(self, n, j):
        return slice(j * P, (j + 1) * P)

    def turned_before(self, n):
        return self.sems["n_b"][n]


def schedule(units):
    steps, late = [], []
    blocks = 0
    for n in range(len(units) + 1):
        s_steps = []
        if n < len(units):
            for s in range(4):
                keys = units[n]["keys"][s]
                for c, k0 in enumerate(range(0, keys, GT)):
                    s_steps.append(("S", n, s, c, k0, min(GT, keys - k0), k0 + GT >= keys))
        b_steps = [("B", n - 1, i, j, s0) for i, (j, s0) in enumerate(units[n - 1]["blocks"])] if n else []
        total = max(len(s_steps), len(b_steps))
        done_s = done_b = 0
        pending = []
        for x in range(1, total + 1):
            while done_s * total < x * len(s_steps):
                step = s_steps[done_s]
                steps.append(step)
                done_s += 1
                for e in pending:
                    steps.append(e)
                pending = [("E", n, step[2])] if step[6] else []
            while done_b * total < x * len(b_steps):
                steps.append(b_steps[done_b])
                done_b += 1
                blocks += 1
                while late and late[0][1] <= blocks:
                    steps.append(("O", late.pop(0)[0]))
        steps += pending
        if n:
            late.append((n - 1, blocks + 3))
    return steps + [("O", n) for n, _ in late]


def stage_attention(nc, sem, tag, ident, layer):
    units = layer.units
    steps = schedule(units)
    n_b = [sum(len(u["blocks"]) for u in units[:n]) for n in range(len(units) + 1)]
    n_sub = lambda n, s: 4 * n + s
    with ExitStack() as c:
        sb = lambda n, s, d=F32: c.enter_context(nc.sbuf_tensor(f"{tag}_{n}", s, d))
        probs = sb("probs", [P, 2, 4, layer.width])
        maxes = sb("maxes", [P, 2, 4, 4])
        top = sb("top", [P, 2, 4])
        shift = sb("shift", [P, 2, 4])
        th = sb("th", [P, 3, GT], F32R)
        tl = sb("tl", [P, 3, GT], F32R)
        inv = sb("inv", [HD, GT])
        ot = sb("ot", [HD, 2, GT])
        p_s = c.enter_context(nc.psum_tensor(f"{tag}_p_s", [P, 3, GT], F32))
        p_t = c.enter_context(nc.psum_tensor(f"{tag}_p_t", [P, 3, GT], F32))
        p_o = c.enter_context(nc.psum_tensor(f"{tag}_p_o", [P, 2, GT], F32))
        scored, moved, shifted, exped, turned, hi_done, lo_done, multiplied, inverted, out_done = (
            sem(f"{tag}_{n}") for n in ("scored", "moved", "shifted", "exped", "turned", "hi_done",
                                        "lo_done", "multiplied", "inverted", "out_done"))
        stored = sem(f"{tag}_stored", 2)
        n_s = [sum(-(-k // GT) for u in units[:n] for k in u["keys"]) for n in range(len(units) + 1)]
        layer.setup(nc, sem, ident, c, dict(exped=exped, multiplied=multiplied, moved=moved,
                                            lo_done=lo_done, n_b=n_b, n_s=n_s))
        block = c.enter_context(nc.Block())

        @block.sync
        def _(sp):
            ahead = 4
            for n in range(ahead):
                layer.load(sp, n)
            for n in range(len(units)):
                if n + ahead < len(units):
                    layer.load(sp, n + ahead)
                if n >= 1:
                    sp.wait_ge(out_done, n)
                    sp.dma_start(layer.store(n - 1), ot[:, (n - 1) % 2]).then_inc(stored[(n - 1) % 2], 16)
            n = len(units) - 1
            sp.wait_ge(out_done, n + 1)
            sp.dma_start(layer.store(n), ot[:, n % 2]).then_inc(stored[n % 2], 16)
            for p in range(2):
                sp.wait_ge(stored[p], 16 * len(range(p, len(units), 2)))

        @block.tensor
        def _(pe):
            layer.pe_start(pe)
            i = 0
            behind = []

            def multiply():
                n, place, j, s0 = behind.pop(0)
                b = n_b[n] + place
                if place == 0:
                    layer.wait_values(pe, n)
                    if n >= 2:
                        pe.wait_ge(out_done, n - 1)
                pe.wait_ge(lo_done, b + 1)
                last = place == len(units[n]["blocks"]) - 1
                out = p_o[:, n % 2, s0 * P:GT]
                pair = (th[:, b % 3, s0 * P:GT], tl[:, b % 3, s0 * P:GT])
                if layer.is_sink(n, j):
                    hi = layer.values(n, j)[0]
                    nc.tensor.matmul(out, hi, pair[1], start=False, stop=False)
                    nc.tensor.matmul(out, hi, pair[0], start=False, stop=last).then_inc(multiplied, 1)
                else:
                    mm3(nc.tensor, out, layer.values(n, j), pair, start=place == 0,
                        stop=last).then_inc(multiplied, 1)

            for step in steps:
                if step[0] == "S":
                    _, n, s, ch, k0, w, last = step
                    if s == 0 and ch == 0:
                        layer.wait_scores(pe, n)
                    if i >= 3:
                        pe.wait_ge(moved, i - 2)
                    layer.scores(p_s[:, i % 3, 0:w], n, s, k0, w).then_inc(scored, 1)
                    i += 1
                elif step[0] == "B":
                    _, n, place, j, s0 = step
                    b = n_b[n] + place
                    pe.wait_ge(exped, n_sub(n, 3) + 1)
                    if b >= 3:
                        pe.wait_ge(lo_done, b - 2)
                    if not layer.is_sink(n, j):
                        for s in range(s0, 4):
                            last = nc.tensor.transpose(p_t[:, b % 3, s * P:(s + 1) * P],
                                                       probs[:, n % 2, s, layer.column(n, j)], ident[:])
                        last.then_inc(turned, 1)
                    behind.append((n, place, j, s0))
                    if len(behind) > 2:
                        multiply()
            while behind:
                multiply()

        @block.vector
        def _(dve):
            layer.dve_start(dve)
            i = 0
            for step in steps:
                if step[0] == "S":
                    _, n, s, ch, k0, w, last = step
                    if ch == 0:
                        layer.wait_bias(dve, n, s)
                        if n >= 2 and s == 0:
                            dve.wait_ge(turned, layer.turned_before(n - 1))
                    dve.wait_ge(scored, i + 1)
                    nc.vector.tensor_tensor_reduce(
                        out=probs[:, n % 2, s, k0:k0 + w], in0=p_s[:, i % 3, 0:w],
                        in1=layer.bias(n, s, k0, w), scale=1.0, scalar=layer.least_max(n, s),
                        op0=ALU.add, op1=ALU.max, accum_out=maxes[:, n % 2, s, ch:ch + 1]).then_inc(moved, 1)
                    i += 1
                    if last:
                        m = maxes[:, n % 2, s, 0:1]
                        dve.wait_ge(moved, i)
                        if ch > 0:
                            m = top[:, n % 2, s:s + 1]
                            nc.vector.tensor_reduce(m, maxes[:, n % 2, s, 0:ch + 1], AX.X, ALU.max)
                            dve.drain()
                        if n >= 2:
                            dve.wait_ge(exped, n_sub(n - 2, s) + 1)
                        nc.vector.tensor_scalar(shift[:, n % 2, s:s + 1], m, -layer.scale, None,
                                                ALU.mult).then_inc(shifted, 1)
                elif step[0] == "B":
                    _, n, place, j, s0 = step
                    b = n_b[n] + place
                    if b >= 3:
                        dve.wait_ge(multiplied, b - 2)
                    if layer.is_sink(n, j):
                        dve.wait_ge(exped, n_sub(n, 3) + 1)
                        layer.sink_block(dve, n, th[:, b % 3], tl[:, b % 3]).then_inc(lo_done, 1)
                    else:
                        dve.wait_ge(hi_done, layer.turned_before(n) + place + 1)
                        nc.vector.tensor_tensor(tl[:, b % 3, s0 * P:GT], p_t[:, b % 3, s0 * P:GT],
                                                th[:, b % 3, s0 * P:GT].bitcast(F32),
                                                ALU.subtract).then_inc(lo_done, 1)
                elif step[0] == "O":
                    n = step[1]
                    dve.wait_ge(multiplied, n_b[n + 1])
                    if n >= 1:
                        dve.wait_ge(out_done, n)
                    nc.vector.reciprocal(inv[:], p_o[HD:P, n % 2]).then_inc(inverted, 1)
                    dve.wait_ge(inverted, n + 1)
                    if n >= 2:
                        dve.wait_ge(stored[n % 2], 16 * (n // 2))
                    nc.vector.tensor_tensor(ot[:, n % 2], p_o[0:HD, n % 2], inv[:],
                                            ALU.mult).then_inc(out_done, 1)

        @block.scalar
        def _(act):
            layer.act_start(act)
            for step in steps:
                if step[0] == "E":
                    _, n, s = step
                    act.wait_ge(shifted, n_sub(n, s) + 1)
                    x = probs[:, n % 2, s, 0:units[n]["keys"][s]]
                    layer.act_sub(act, n, s, shift[:, n % 2, s:s + 1])
                    nc.scalar.activation(x, x, ACT.Exp, bias=shift[:, n % 2, s:s + 1],
                                         scale=layer.scale).then_inc(exped, 1)
                elif step[0] == "B":
                    _, n, place, j, s0 = step
                    b = n_b[n] + place
                    if layer.is_sink(n, j):
                        continue
                    act.wait_ge(turned, layer.turned_before(n) + place + 1)
                    if b >= 3:
                        act.wait_ge(multiplied, b - 2)
                    nc.scalar.activation(th[:, b % 3, s0 * P:GT], p_t[:, b % 3, s0 * P:GT],
                                         ACT.Copy).then_inc(hi_done, 1)

        @block.gpsimd
        def _(pool):
            layer.pool_start(pool)


class Mla(Attention):
    scale = QK ** -0.5

    def __init__(self, qkT, va, oT):
        self.qkT, self.va, self.oT = qkT, va, oT
        self.units = [dict(keys=[P * (NG * g + s + 1) for s in range(4)],
                           blocks=[(j, max(0, j - 4 * g)) for j in range(4 * g + 4)])
                      for h in range(H) for g in range(NG)]

    def setup(self, nc, sem, ident, ctx, sems):
        sb = lambda n, s, d=F32: ctx.enter_context(nc.sbuf_tensor(f"mla_{n}", s, d))
        self.nc, self.sems = nc, sems
        self.q = [sb(f"q_{n}", [QK, 2, T], F32R) for n in ("hi", "lo")]
        self.k = [sb(f"k_{n}", [QK, 2, T], F32R) for n in ("hi", "lo")]
        self.v = [sb(f"v_{n}", [P, 2, NT, P], F32R) for n in ("hi", "lo")]
        self.none = sb("none", [P, GT])
        self.causal = sb("causal", [P, GT])
        self.qk_in, self.v_in = sem("mla_qk_in", 2), sem("mla_v_in", 2)
        self.ones_made, self.bias_made = sem("mla_ones_made"), sem("mla_bias_made")

    def pool_start(self, pool):
        g = self.nc.gpsimd
        g.memset(self.v[0][:, :, :, HD:P].bitcast(F32), 1.0)
        g.memset(self.v[1][:, :, :, HD:P].bitcast(F32), 0.0).then_inc(self.ones_made, 1)
        g.memset(self.none[:], 0.0)
        g.memset(self.causal[:], 0.0)
        pool.drain()
        g.affine_select(out=self.causal[:, GT - P:GT], in_=self.causal[:, GT - P:GT],
                        compare_op=ALU.is_ge, fill=NEG, base=0, pattern=[[-1, P]],
                        channel_multiplier=1).then_inc(self.bias_made, 1)

    def pe_start(self, pe):
        pe.wait_ge(self.ones_made, 1)

    def dve_start(self, dve):
        dve.wait_ge(self.bias_made, 1)

    def load(self, sp, n):
        h, g = n // NG, n % NG
        if g:
            return
        p = h % 2
        if h >= 2:
            sp.wait_ge(self.sems["multiplied"], self.sems["n_b"][NG * (h - 1)])
        for half in range(2):
            sp.dma_start(self.q[half][:, p].bitcast(F32), self.qkT[half, h]).then_inc(self.qk_in[p], 16)
            sp.dma_start(self.k[half][:, p].bitcast(F32), self.qkT[half, H + h]).then_inc(self.qk_in[p], 16)
        for half in range(2):
            sp.dma_start(self.v[half][:, p, :, 0:HD].bitcast(F32),
                         self.va[half, :, h * HD:(h + 1) * HD].rearrange("(j p) d -> p j d", p=P))\
                .then_inc(self.v_in[p], 16)

    def wait_scores(self, pe, n):
        pe.wait_ge(self.qk_in[n // NG % 2], 64 * (n // NG // 2 + 1))

    def wait_values(self, pe, n):
        pe.wait_ge(self.v_in[n // NG % 2], 32 * (n // NG // 2 + 1))

    def scores(self, out, n, s, k0, w):
        p, t = n // NG % 2, n % NG * 4 + s
        q = [x[:, p, t * P:(t + 1) * P] for x in self.q]
        k = [x[:, p, k0:k0 + w] for x in self.k]
        return mm3(self.nc.tensor, out, q, k, start=True, stop=True)

    def bias(self, n, s, k0, w):
        if k0 + w == self.units[n]["keys"][s]:
            return self.causal[:, GT - w:GT]
        return self.none[:, 0:w]

    def values(self, n, j):
        return [x[:, n // NG % 2, j] for x in self.v]

    def store(self, n):
        h, g = n // NG, n % NG
        return self.oT[h * HD:(h + 1) * HD, g * GT:(g + 1) * GT]

SENTINEL = -3.2e38
FUTURE = -3e38
HALVINGS = 10
WIDE = 2 * GT


def stage_index(nc, sem, ident, qiT, kiT, wi, mask):
    with ExitStack() as c:
        sb = lambda n, s, d=F32: c.enter_context(nc.sbuf_tensor(f"i_{n}", s, d))
        q = sb("q", [P, 2, H, P], F32R)
        k = sb("k", [P, T], F32R)
        w = sb("w", [P, NT, H])
        relu = sb("relu", [P, 4, WIDE])
        score = sb("score", [P, 2, T + 8])
        junk = sb("junk", [P, T])
        bias = sb("bias", [P, 2, T], BF16)
        halves = sb("halves", [P, HALVINGS + 1])
        steps8 = sb("steps8", [P, 8])
        lim = sb("lim", [P, 2])
        rng = sb("rng", [P, 1])
        mid = sb("mid", [P, 1])
        widths = sb("widths", [P, HALVINGS + 1])
        count = sb("count", [P, 1])
        side = sb("side", [P, 1])
        few = sb("few", [P, 1])
        off = sb("off", [P, 1])
        left = sb("left", [P, 1])
        rounds = sb("rounds", [1, 1])
        rounds_i = sb("rounds_i", [1, 1], I32)
        best = sb("best", [P, 8])
        taken = sb("taken", [P, 8])
        gone = sb("gone", [P, 8])
        p_s = c.enter_context(nc.psum_tensor("i_p_s", [P, 3, WIDE], F32))
        p_l = c.enter_context(nc.psum_tensor("i_p_l", [P, GT], F32))
        k_in = sem("i_k_in")
        q_in, stored = sem("i_q_in", 2), sem("i_stored", 2)
        consts, scored, relued, summed, masked, counted, turned, made, fixed = (
            sem(f"i_{n}") for n in ("consts", "scored", "relued", "summed", "masked", "counted", "turned",
                                    "made", "fixed"))
        block = c.enter_context(nc.Block())

        def chunks(t):
            keys = P * (t + 1)
            return [(k0, min(WIDE, keys - k0)) for k0 in range(0, keys, WIDE)]

        tiles = range(TOPK // P, NT)
        n_at, n = {}, 0
        for t in tiles:
            n_at[t] = n
            n += H * len(chunks(t))
        n_at[NT] = n

        @block.sync
        def _(sp):
            sp.dma_start(w[:], wi.rearrange("(t p) h -> p t h", p=P)).then_inc(k_in, 16)
            for r in range(4):
                sp.dma_start(k[IDX * r:IDX * (r + 1)].bitcast(F32), kiT[r % 2]).then_inc(k_in, 16)

            def load(t):
                if t - 2 in n_at:
                    sp.wait_ge(scored, n_at[t - 1])
                for r in range(4):
                    src = qiT[r // 2].rearrange("j (r d) t -> d (j r) t", d=IDX)
                    sp.dma_start(q[IDX * r:IDX * (r + 1), t % 2].bitcast(F32),
                                 src[:, :, t * P:(t + 1) * P]).then_inc(q_in[t % 2], 16)

            def store(t):
                keys = P * (t + 1)
                sp.wait_ge(fixed, t + 1)
                sp.dma_start(mask[t * P:(t + 1) * P, 0:keys], bias[:, t % 2, 0:keys])\
                    .then_inc(stored[t % 2], 16)

            load(tiles[0])
            for t in range(NT):
                if t + 1 in n_at and t + 1 < NT and t + 1 > tiles[0]:
                    load(t + 1)
                store(t)
            for p in range(2):
                sp.wait_ge(stored[p], 16 * (NT // 2))

        @block.tensor
        def _(pe):
            pe.wait_ge(k_in, 80)
            n = 0
            for t in tiles:
                pe.wait_ge(q_in[t % 2], 64 * ((t - tiles[0]) // 2 + 1))
                for h in range(H):
                    for k0, width in chunks(t):
                        if n >= 3:
                            pe.wait_ge(relued, n - 2)
                        for x in range(0, width, GT):
                            y = min(GT, width - x)
                            last = nc.tensor.matmul(p_s[:, n % 3, x:x + y], q[:, t % 2, h],
                                                    k[:, k0 + x:k0 + x + y], start=True, stop=True)
                        last.then_inc(scored, 1)
                        n += 1
                pe.wait_ge(counted, t - tiles[0] + 1)
                nc.tensor.transpose(p_l[0:1, 0:P], left[:], ident[:]).then_inc(turned, 1)

        @block.scalar
        def _(act):
            n = 0
            for t in tiles:
                for h in range(H):
                    for k0, width in chunks(t):
                        act.wait_ge(scored, n + 1)
                        if n >= 4:
                            act.wait_ge(summed, n - 3)
                        nc.scalar.activation(relu[:, n % 4, 0:width], p_s[:, n % 3, 0:width],
                                             ACT.Relu).then_inc(relued, 1)
                        n += 1

        @block.gpsimd
        def _(pool):
            nc.gpsimd.iota(steps8[:], pattern=[[1, 8]], base=0, channel_multiplier=0,
                           allow_small_or_imprecise_dtypes=True).then_inc(consts, 1)
            for t in range(NT):
                keys = P * (t + 1)
                if t in n_at:
                    pool.wait_ge(summed, n_at[t + 1])
                    d = score[:, t % 2, keys - P:keys]
                    nc.gpsimd.affine_select(out=d, in_=d, compare_op=ALU.is_ge, fill=FUTURE, base=0,
                                            pattern=[[-1, P]], channel_multiplier=1).then_inc(masked, 1)
                    pool.wait_ge(made, t - tiles[0] + 1)
                else:
                    nc.gpsimd.memset(bias[:, t % 2, 0:keys], 0.0)
                    pool.drain()
                d = bias[:, t % 2, keys - P:keys]
                nc.gpsimd.affine_select(out=d, in_=d, compare_op=ALU.is_ge, fill=NEG, base=0,
                                        pattern=[[-1, P]], channel_multiplier=1).then_inc(fixed, 1)

        @block.vector
        def _(dve):
            for i in range(HALVINGS + 1):
                nc.vector.memset(halves[:, i:i + 1], 2.0 ** -(i + 1))
            dve.wait_ge(k_in, 80)
            dve.wait_ge(consts, 1)
            n = 0
            for t in tiles:
                keys = P * (t + 1)
                s = score[:, t % 2, 0:keys]
                for h in range(H):
                    for k0, width in chunks(t):
                        dve.wait_ge(relued, n + 1)
                        r, acc = relu[:, n % 4, 0:width], score[:, t % 2, k0:k0 + width]
                        if h == 0:
                            nc.vector.tensor_scalar(acc, r, w[:, t, 0:1], None, ALU.mult).then_inc(summed, 1)
                        else:
                            dve.wait_ge(summed, n + 1 - len(chunks(t)))
                            nc.vector.scalar_tensor_tensor(out=acc, in0=r, scalar=w[:, t, h:h + 1], in1=acc,
                                                           op0=ALU.mult, op1=ALU.add).then_inc(summed, 1)
                        n += 1
                dve.wait_ge(masked, t - tiles[0] + 1)
                sample = score[:, t % 2, 0:keys - P:(keys - P) // 256]
                nc.vector.tensor_reduce(lim[:, 0:1], sample, AX.X, ALU.max)
                nc.vector.tensor_reduce(lim[:, 1:2], sample, AX.X, ALU.min)
                dve.drain()
                nc.vector.tensor_tensor(rng[:], lim[:, 0:1], lim[:, 1:2], ALU.subtract)
                dve.drain()
                nc.vector.tensor_scalar(widths[:], halves[:], rng[:], 1.25, ALU.mult, ALU.mult)
                dve.drain()
                nc.vector.tensor_tensor(mid[:], lim[:, 0:1], widths[:, 0:1], ALU.subtract)
                dve.drain()
                for i in range(HALVINGS):
                    nc.vector.tensor_scalar(junk[:, 0:keys], s, mid[:], None, ALU.is_ge, ALU.add,
                                            accum_out=count[:])
                    dve.drain()
                    nc.vector.tensor_scalar(side[:], count[:], TOPK - 0.5, 0.5, ALU.is_ge, ALU.subtract)
                    dve.drain()
                    nc.vector.scalar_tensor_tensor(out=mid[:], in0=side[:], scalar=widths[:, i:i + 1],
                                                   in1=mid[:], op0=ALU.mult, op1=ALU.add)
                    dve.drain()
                nc.vector.tensor_tensor(mid[:], mid[:], widths[:, HALVINGS - 1:HALVINGS], ALU.add)
                dve.drain()
                nc.vector.tensor_scalar(junk[:, 0:keys], s, mid[:], None, ALU.is_ge, ALU.add,
                                        accum_out=count[:])
                dve.drain()
                nc.vector.tensor_scalar(few[:], count[:], TOPK - 0.5, None, ALU.is_lt)
                dve.drain()
                nc.vector.tensor_scalar(off[:], few[:], NEG, None, ALU.mult)
                nc.vector.tensor_tensor(left[:], few[:], count[:], ALU.mult)
                dve.drain()
                nc.vector.tensor_scalar(left[:], left[:], -1.0, float(TOPK), ALU.mult, ALU.add)\
                    .then_inc(counted, 1)
                nc.vector.scalar_tensor_tensor(out=s, in0=junk[:, 0:keys], scalar=off[:], in1=s,
                                               op0=ALU.mult, op1=ALU.add)
                dve.wait_ge(turned, t - tiles[0] + 1)
                nc.vector.tensor_reduce(rounds[:], p_l[0:1, 0:P], AX.X, ALU.max)
                dve.drain()
                nc.vector.tensor_scalar(rounds[:], rounds[:], 3.5, 0.125, ALU.add, ALU.mult)
                dve.drain()
                nc.vector.tensor_scalar(rounds[:], rounds[:], ROUNDER, None, ALU.add)
                dve.drain()
                nc.vector.tensor_scalar(rounds[:], rounds[:], ROUNDER, None, ALU.subtract)
                dve.drain()
                nc.vector.tensor_copy(rounds_i[:], rounds[:])
                dve.drain()
                n_rounds = dve.value_load(rounds_i[0:1, 0:1], min_val=1, max_val=TOPK // 8)
                whole = score[:, t % 2, 0:keys + 8]
                with dve.Fori(0, n_rounds) as _i:
                    nc.vector.memset(score[:, t % 2, keys:keys + 8], SENTINEL)
                    nc.vector.max(out=best[:], in_=s)
                    nc.vector.tensor_scalar(taken[:], steps8[:], left[:], None, ALU.is_lt)
                    dve.drain()
                    nc.vector.tensor_scalar(left[:], left[:], 8.0, None, ALU.subtract)
                    nc.vector.tensor_tensor(best[:], best[:], taken[:], ALU.mult)
                    nc.vector.tensor_scalar(gone[:], taken[:], 1.0, -SENTINEL, ALU.subtract, ALU.mult)
                    dve.drain()
                    nc.vector.tensor_tensor(best[:], best[:], gone[:], ALU.add)
                    dve.drain()
                    nc.vector.match_replace(out=whole, in_to_replace=best[:], in_values=whole, imm_value=NEG)
                    dve.drain()
                if t >= 2:
                    dve.wait_ge(stored[t % 2], 16 * (t // 2))
                nc.vector.tensor_scalar(bias[:, t % 2, 0:keys], s, NEG / 2, NEG, ALU.is_ge,
                                        ALU.mult).then_inc(made, 1)


class Dsa(Attention):
    scale = HD ** -0.5

    def __init__(self, qbT, kbT, vb, mask, oT):
        self.qbT, self.kbT, self.vb, self.mask, self.oT = qbT, kbT, vb, mask, oT
        self.units = [dict(keys=[P * (t + 1)] * 4, blocks=[(j, 0) for j in range(t + 1)])
                      for t in range(NT) for g in range(KV)]

    def setup(self, nc, sem, ident, ctx, sems):
        sb = lambda n, s, d=F32: ctx.enter_context(nc.sbuf_tensor(f"dsa_{n}", s, d))
        self.nc, self.sems = nc, sems
        self.q = sb("q", [P, 2, H, P], F32R)
        self.k_hi = sb("k_hi", [P, KV, T], F32R)
        self.k_lo = sb("k_lo", [HD, KV, T], F32R)
        self.v = [sb(f"v_{n}", [P, NT, KV, P], F32R) for n in ("hi", "lo")]
        self.m = sb("mask", [P, 2, T], BF16)
        self.q_in, self.m_in = sem("dsa_q_in", 2), sem("dsa_m_in", 2)
        self.kv_in, self.ones_made = sem("dsa_kv_in"), sem("dsa_ones_made")

    def pool_start(self, pool):
        g = self.nc.gpsimd
        g.memset(self.v[0][:, :, :, HD:P].bitcast(F32), 1.0)
        g.memset(self.v[1][:, :, :, HD:P].bitcast(F32), 0.0).then_inc(self.ones_made, 1)

    def pe_start(self, pe):
        pe.wait_ge(self.ones_made, 1)
        pe.wait_ge(self.kv_in, 16 * 7)

    def load(self, sp, n):
        t, g = n // KV, n % KV
        if g:
            return
        if t >= 2:
            sp.wait_ge(self.sems["moved"], self.sems["n_s"][KV * (t - 1)])
        at = slice(t * P, (t + 1) * P)
        for half in range(2):
            sp.dma_start(self.q[half * HD:(half + 1) * HD, t % 2].bitcast(F32),
                         self.qbT[half].rearrange("j (r d) t -> d (j r) t", d=HD)[:, :, at])\
                .then_inc(self.q_in[t % 2], 16)
        keys = P * (t + 1)
        sp.dma_start(self.m[:, t % 2, 0:keys], self.mask[at, 0:keys]).then_inc(self.m_in[t % 2], 16)
        if n == 0:
            k = [self.kbT[half].rearrange("(g d) t -> d g t", d=HD) for half in range(2)]
            for dst, src in ((self.k_hi[0:HD], k[0]), (self.k_hi[HD:P], k[0]), (self.k_lo[:], k[1])):
                sp.dma_start(dst.bitcast(F32), src).then_inc(self.kv_in, 16)
            for half in range(2):
                for g in range(KV):
                    sp.dma_start(self.v[half][:, :, g, 0:HD].bitcast(F32),
                                 self.vb[half, :, g * HD:(g + 1) * HD].rearrange("(j p) d -> p j d", p=P))\
                        .then_inc(self.kv_in, 16)

    def wait_scores(self, pe, n):
        pe.wait_ge(self.q_in[n // KV % 2], 32 * (n // KV // 2 + 1))

    def wait_values(self, pe, n): ...

    def wait_bias(self, dve, n, s):
        dve.wait_ge(self.m_in[n // KV % 2], 16 * (n // KV // 2 + 1))

    def scores(self, out, n, s, k0, w):
        t, g = n // KV, n % KV
        q = self.q[:, t % 2, 4 * g + s]
        self.nc.tensor.matmul(out, q, self.k_hi[:, g, k0:k0 + w], start=True, stop=False)
        return self.nc.tensor.matmul(out, q[0:HD], self.k_lo[:, g, k0:k0 + w], start=False, stop=True)

    def bias(self, n, s, k0, w):
        return self.m[:, n // KV % 2, k0:k0 + w]

    def values(self, n, j):
        return [x[:, j, n % KV] for x in self.v]

    def store(self, n):
        t, g = n // KV, n % KV
        rows = self.oT[g * 4 * HD:(g + 1) * 4 * HD, t * P:(t + 1) * P]
        return rows.rearrange("(h d) t -> d h t", d=HD)


def t5_one_hot():
    out = np.zeros((32, 3 * P), np.float32)
    for dist in range(WINDOW):
        if dist < 16:
            bucket = dist
        else:
            ratio = np.log(np.float32(dist) / np.float32(16)) / np.float32(math.log(8.0))
            bucket = min(31, 16 + int(np.float32(ratio) * np.float32(16)))
        out[bucket, 2 * P - 1 - dist] = 1.0
    return out


def stage_bias(nc, sem, one_hot, table, spread):
    with ExitStack() as c:
        sb = lambda n, s: c.enter_context(nc.sbuf_tensor(f"t_{n}", s, F32))
        hot = sb("hot", [32, 3 * P])
        tab = sb("tab", [32, WH])
        row = sb("row", [WH, 3 * P])
        ps = c.enter_context(nc.psum_tensor("t_ps", [WH, 3 * P], F32))
        loaded, product, filled, stored = (sem(f"t_{n}") for n in ("loaded", "product", "filled", "stored"))
        block = c.enter_context(nc.Block())

        @block.sync
        def _(sp):
            sp.dma_start(hot[:], one_hot).then_inc(loaded, 16)
            sp.dma_start(tab[:], table).then_inc(loaded, 16)
            sp.wait_ge(filled, 2)
            sp.dma_start(spread, row[:].unsqueeze(1).broadcast_to([WH, P, 3 * P])).then_inc(stored, 16)
            sp.wait_ge(stored, 16)

        @block.tensor
        def _(pe):
            pe.wait_ge(loaded, 32)
            nc.tensor.matmul(ps[:], tab[:], hot[:], start=True, stop=True).then_inc(product, 1)

        @block.vector
        def _(dve):
            nc.vector.memset(row[:], NEG).then_inc(filled, 1)
            dve.wait_ge(filled, 1)
            dve.wait_ge(product, 1)
            nc.vector.tensor_scalar(row[:, P:2 * P], ps[:, P:2 * P], 1 / Window.scale, None,
                                    ALU.mult).then_inc(filled, 1)


class Window(Attention):
    scale = HD ** -0.5
    width = 2 * P

    def __init__(self, qT, kT, v, spread, sinks, oT):
        self.qT, self.kT, self.v_dram, self.spread, self.sinks, self.oT = qT, kT, v, spread, sinks, oT
        self.units = [dict(keys=[P * min(2, t + 1)] * 4, blocks=[(j, 0) for j in range(min(2, t + 1) + 1)])
                      for t in range(NT) for g in range(WKV)]

    def setup(self, nc, sem, ident, ctx, sems):
        sb = lambda n, s, d=F32: ctx.enter_context(nc.sbuf_tensor(f"win_{n}", s, d))
        self.nc, self.sems, self.ident = nc, sems, ident
        self.q_raw = sb("q_raw", [P, 2, WH, P])
        self.k_raw = sb("k_raw", [P, 2, WKV, P])
        self.v_raw = sb("v_raw", [P, 2, WKV * HD])
        self.q = sb("q", [P, 2, WH, P], F32R)
        self.k_hi = sb("k_hi", [P, WKV, 4, P], F32R)
        self.k_lo = sb("k_lo", [HD, WKV, 4, P], F32R)
        self.v = [sb(f"v_{n}", [P, 4, WKV, P], F32R) for n in ("hi", "lo")]
        self.sink_v = sb("sink_v", [P, P], F32R)
        self.b = sb("bias", [P, WH, 2 * P])
        self.sink8 = sb("sink8", [P, WH])
        self.e_sink = sb("e_sink", [P, 2, 4])
        self.tile_in = sem("win_tile_in", 2)
        self.const_in, self.consts, self.sink_made, self.q_split, self.kv_split, self.k_split = (
            sem(f"win_{n}") for n in ("const_in", "consts", "sink_made", "q_split", "kv_split", "k_split"))

    def load(self, sp, n):
        t, g = n // WKV, n % WKV
        if n == 0:
            sp.dma_start(self.sink8[:], self.sinks.partition_broadcast(P)).then_inc(self.const_in, 16)
            flat = self.spread.rearrange("h r u -> h (r u)")[:, P - 1:P - 1 + P * (3 * P - 1)]
            toeplitz = flat.rearrange("h (q u) -> q h u", u=3 * P - 1)[:, :, 0:2 * P]
            sp.dma_start(self.b[:], toeplitz).then_inc(self.const_in, 16)
        if g:
            return
        at = slice(t * P, (t + 1) * P)
        if t >= 2:
            sp.wait_ge(self.kv_split, t - 1)
        done = self.tile_in[t % 2]
        for rows in (slice(0, HD), slice(HD, P)):
            sp.dma_start(self.q_raw[rows, t % 2],
                         self.qT.rearrange("(h d) t -> d h t", d=HD)[:, :, at]).then_inc(done, 16)
            sp.dma_start(self.k_raw[rows, t % 2],
                         self.kT.rearrange("(h d) t -> d h t", d=HD)[:, :, at]).then_inc(done, 16)
        sp.dma_start(self.v_raw[:, t % 2], self.v_dram[at, :]).then_inc(done, 16)

    def pool_start(self, pool):
        g = self.nc.gpsimd
        g.memset(self.v[0][:, :, :, HD:P].bitcast(F32), 1.0)
        g.memset(self.v[1][:, :, :, HD:P].bitcast(F32), 0.0)
        g.memset(self.sink_v[:, 0:HD].bitcast(F32), 0.0)
        g.memset(self.sink_v[:, HD:P].bitcast(F32), 1.0).then_inc(self.consts, 1)
        for t in range(NT):
            p, r = t % 2, t % 4
            pool.wait_ge(self.tile_in[p], 80 * (t // 2 + 1))
            if t >= 2:
                pool.wait_ge(self.sems["multiplied"], self.sems["n_b"][WKV * (t - 1)])
            v_raw = self.v_raw[:, p].rearrange("p (g d) -> p g d", d=HD)
            g.tensor_copy(self.k_hi[:, :, r], self.k_raw[:, p])
            g.tensor_copy(self.v[0][:, r, :, 0:HD], v_raw)
            g.tensor_copy(self.q[:, p], self.q_raw[:, p])
            pool.drain()
            g.tensor_tensor(self.k_lo[:, :, r], self.k_raw[0:HD, p], self.k_hi[0:HD, :, r].bitcast(F32),
                            ALU.subtract)
            pool.drain()
            g.tensor_tensor(self.v[1][:, r, :, 0:HD], v_raw, self.v[0][:, r, :, 0:HD].bitcast(F32),
                            ALU.subtract)
            pool.drain()
            g.tensor_tensor(self.q[HD:P, p], self.q_raw[HD:P, p], self.q[HD:P, p].bitcast(F32),
                            ALU.subtract).then_inc(self.kv_split, 1)
            pool.drain()

    def pe_start(self, pe):
        pe.wait_ge(self.consts, 1)

    def dve_start(self, dve):
        dve.wait_ge(self.const_in, 32)
        self.nc.vector.tensor_scalar(self.sink8[:], self.sink8[:], 1 / self.scale, None,
                                     ALU.mult).then_inc(self.sink_made, 1)
        dve.drain()

    def act_start(self, act):
        act.wait_ge(self.sink_made, 1)

    def act_sub(self, act, n, s, shift):
        if n >= 2 and s == 0:
            act.wait_ge(self.sems["lo_done"], self.sems["n_b"][n - 1])
        h = 4 * (n % WKV) + s
        self.nc.scalar.activation(self.e_sink[:, n % 2, s:s + 1], self.sink8[:, h:h + 1], ACT.Exp,
                                  bias=shift, scale=self.scale)

    def least_max(self, n, s):
        h = 4 * (n % WKV) + s
        return self.sink8[:, h:h + 1]

    def is_sink(self, n, j):
        return j == len(self.units[n]["blocks"]) - 1

    def turned_before(self, n):
        return self.sems["n_b"][n] - n

    def sink_block(self, dve, n, th, tl):
        v = self.nc.vector
        for s in range(4):
            v.tensor_scalar(th[:, s * P:(s + 1) * P], self.ident[:], self.e_sink[:, n % 2, s:s + 1], None,
                            ALU.mult)
        dve.drain()
        for s in range(4):
            x = slice(s * P, (s + 1) * P)
            last = v.scalar_tensor_tensor(out=tl[:, x], in0=self.ident[:],
                                          scalar=self.e_sink[:, n % 2, s:s + 1], in1=th[:, x].bitcast(F32),
                                          op0=ALU.mult, op1=ALU.subtract)
        return last

    def wait_scores(self, pe, n):
        pe.wait_ge(self.kv_split, n // WKV + 1)

    def wait_values(self, pe, n): ...

    def scores(self, out, n, s, k0, w):
        t, g = n // WKV, n % WKV
        q = self.q[:, t % 2, 4 * g + s]
        for i in range(w // P):
            r = (t - w // P + 1 + i) % 4
            o = out[:, i * P:(i + 1) * P]
            self.nc.tensor.matmul(o, q, self.k_hi[:, g, r], start=True, stop=False)
            last = self.nc.tensor.matmul(o, q[0:HD], self.k_lo[:, g, r], start=False, stop=True)
        return last

    def bias(self, n, s, k0, w):
        return self.b[:, 4 * (n % WKV) + s, 2 * P - w:2 * P]

    def values(self, n, j):
        if self.is_sink(n, j):
            return [self.sink_v[:]]
        t, g = n // WKV, n % WKV
        r = (t - (len(self.units[n]["blocks"]) - 2) + j) % 4
        return [x[:, r, g] for x in self.v]

    def store(self, n):
        t, g = n // WKV, n % WKV
        rows = self.oT[g * 4 * HD:(g + 1) * 4 * HD, t * P:(t + 1) * P]
        return rows.rearrange("(h d) t -> d h t", d=HD)


def stage_branch(nc, sem, oaT, obT, gates, w_mla, w_dsa, mergedT):
    KO = 4
    with ExitStack() as c:
        sb = lambda n, s, d=F32: c.enter_context(nc.sbuf_tensor(f"m_{n}", s, d))
        raw = sb("raw", [P, 2, KO, D])
        w = [[sb(f"w{x}_{n}", [P, KO, D], F32R) for n in ("hi", "lo")] for x in "ab"]
        o = sb("o", [P, 2, KO, GT])
        gate = sb("gate", [P, 2, KO, GT])
        oh = sb("oh", [P, 2, KO, GT], F32R)
        ol = sb("ol", [P, 2, KO, GT], F32R)
        m = sb("m", [P, 2, 2, GT])
        part = sb("part", [P, 2, GT])
        total = sb("total", [P, 2, GT])
        ps = c.enter_context(nc.psum_tensor("m_ps", [P, 4, 2, GT], F32))
        w_in = sem("m_w_in")
        o_in, m_in, stored = sem("m_o_in", 2), sem("m_m_in", 2), sem("m_stored", 2)
        w_hi, w_lo, gated, hi_done, lo_done, filled, weighed, added = (
            sem(f"m_{n}") for n in ("w_hi", "w_lo", "gated", "hi_done", "lo_done", "filled", "weighed",
                                    "added"))
        block = c.enter_context(nc.Block())
        view = lambda x: x.rearrange("(k p) t -> p k t", p=P)
        tok = lambda g: slice(g * GT, (g + 1) * GT)

        @block.sync
        def _(sp):
            for x, src in enumerate((w_mla, w_dsa)):
                sp.dma_start(raw[:, x], view(src)).then_inc(w_in, 16)

            def load(g):
                for x, src in enumerate((oaT, obT)):
                    if g:
                        sp.wait_ge(lo_done, 2 * g - 1 + x)
                    sp.dma_start(o[:, x], view(src)[:, :, tok(g)]).then_inc(o_in[x], 16)
                    sp.dma_start(gate[:, x], view(gates[x * 512:(x + 1) * 512])[:, :, tok(g)])\
                        .then_inc(o_in[x], 16)

            def load_m(n):
                g, f = n // KD, n % KD
                if n >= 2:
                    sp.wait_ge(weighed, 2 * (n - 1))
                for x in range(2):
                    r = 1024 * (x + 1) + f * P
                    sp.dma_start(m[:, n % 2, x], gates[r:r + P, tok(g)]).then_inc(m_in[n % 2], 16)

            def store(n):
                g, f = n // KD, n % KD
                sp.wait_ge(added, n + 1)
                sp.dma_start(mergedT[f * P:(f + 1) * P, tok(g)], total[:, n % 2]).then_inc(stored[n % 2], 16)

            load(0)
            load_m(0)
            for n in range(NG * KD):
                if n % KD == 0 and n // KD + 1 < NG:
                    load(n // KD + 1)
                if n + 1 < NG * KD:
                    load_m(n + 1)
                store(n)
            for p in range(2):
                sp.wait_ge(stored[p], 16 * (NG * KD // 2))

        @block.scalar
        def _(act):
            act.wait_ge(w_in, 32)
            for x in range(2):
                nc.scalar.activation(w[x][0][:], raw[:, x], ACT.Copy).then_inc(w_hi, 1)
            for g in range(NG):
                for x in range(2):
                    act.wait_ge(gated, 2 * g + x + 1)
                    if g:
                        act.wait_ge(filled, 2 * KD * (g - 1) + 2 * KD)
                    nc.scalar.activation(oh[:, x], o[:, x], ACT.Copy).then_inc(hi_done, 1)

        @block.gpsimd
        def _(pool):
            for g in range(NG):
                for x in range(2):
                    pool.wait_ge(hi_done, 2 * g + x + 1)
                    nc.gpsimd.tensor_tensor(ol[:, x], o[:, x], oh[:, x].bitcast(F32),
                                            ALU.subtract).then_inc(lo_done, 1)

        @block.vector
        def _(dve):
            def gated_group(g):
                for x in range(2):
                    dve.wait_ge(o_in[x], 32 * (g + 1))
                    nc.vector.tensor_tensor(o[:, x], o[:, x], gate[:, x], ALU.mult).then_inc(gated, 1)

            gated_group(0)
            for x in range(2):
                dve.wait_ge(w_hi, x + 1)
                nc.vector.tensor_tensor(w[x][1][:], raw[:, x], w[x][0][:].bitcast(F32),
                                        ALU.subtract).then_inc(w_lo, 1)
            for n in range(NG * KD):
                g = n // KD
                if n % KD == 2 and g + 1 < NG:
                    gated_group(g + 1)
                dve.wait_ge(m_in[n % 2], 32 * (n // 2 + 1))
                if n:
                    dve.wait_ge(added, n)
                for x in range(2):
                    dve.wait_ge(filled, 2 * n + x + 1)
                    nc.vector.tensor_tensor(part[:, x], ps[:, n % 4, x], m[:, n % 2, x],
                                            ALU.mult).then_inc(weighed, 1)
                dve.wait_ge(weighed, 2 * n + 2)
                if n >= 2:
                    dve.wait_ge(stored[n % 2], 16 * (n // 2))
                nc.vector.tensor_tensor(total[:, n % 2], part[:, 0], part[:, 1], ALU.add).then_inc(added, 1)

        @block.tensor
        def _(pe):
            pe.wait_ge(w_lo, 2)
            for n in range(NG * KD):
                g, f = n // KD, n % KD
                if n >= 4:
                    pe.wait_ge(weighed, 2 * (n - 3))
                for x in range(2):
                    if f == 0:
                        pe.wait_ge(lo_done, 2 * g + x + 1)
                    for k in range(KO):
                        cols = slice(f * P, (f + 1) * P)
                        last = mm3(nc.tensor, ps[:, n % 4, x], [y[:, k, cols] for y in w[x]],
                                   (oh[:, x, k], ol[:, x, k]), start=k == 0, stop=k == KO - 1)
                    last.then_inc(filled, 1)


def stage_out(nc, sem, tag, actT, gateT, weight, residual, out, final_gain=None):
    GO = 2 * P
    with ExitStack() as c:
        sb = lambda n, s, d=F32: c.enter_context(nc.sbuf_tensor(f"{tag}_{n}", s, d))
        raw = sb("raw", [P, 2, D])
        w = [sb(f"w_{n}", [P, KD, D], F32R) for n in ("hi", "lo")]
        a = sb("a", [P, 2, KD, GO])
        gate = sb("gate", [P, KD, GO]) if gateT is not None else None
        ah = sb("ah", [P, 2, KD, GO], F32R)
        al = sb("al", [P, 2, KD, GO], F32R)
        x = sb("x", [P, 2, D])
        y = sb("y", [P, 2, D])
        if final_gain is not None:
            gain = sb("gain", [P, D])
            junk = sb("junk", [P, D])
            ss, ms, sd, rs = (sb(n, [P, NT]) for n in ("ss", "ms", "sd", "rs"))
        ps = c.enter_context(nc.psum_tensor(f"{tag}_ps", [P, 4, 2, GT], F32))
        w_in, a_in, x_in, stored = (sem(f"{tag}_{n}", 2) for n in ("w_in", "a_in", "x_in", "stored"))
        gate_in, gain_in, w_hi, w_lo, gated, hi_done, lo_done, filled, added, squared, meaned, rooted, done = (
            sem(f"{tag}_{n}") for n in ("gate_in", "gain_in", "w_hi", "w_lo", "gated", "hi_done", "lo_done",
                                        "filled", "added", "squared", "meaned", "rooted", "done"))
        block = c.enter_context(nc.Block())
        view = lambda z: z.rearrange("(k p) t -> p k t", p=P)
        n_groups = T // GO

        @block.sync
        def _(sp):
            def load(g):
                s = slice(g * GO, (g + 1) * GO)
                if g >= 2:
                    sp.wait_ge(lo_done, g - 1)
                sp.dma_start(a[:, g % 2], view(actT)[:, :, s]).then_inc(a_in[g % 2], 16)
                if gate is not None:
                    if g >= 1:
                        sp.wait_ge(gated, g)
                    sp.dma_start(gate[:], view(gateT)[:, :, s]).then_inc(gate_in, 16)

            def load_x(t):
                if t >= 2:
                    sp.wait_ge(added, t - 1)
                sp.dma_start(x[:, t % 2], residual[t * P:(t + 1) * P, :]).then_inc(x_in[t % 2], 16)

            load(0)
            for k in range(KD):
                if k >= 2:
                    sp.wait_ge(w_lo, k - 1)
                sp.dma_start(raw[:, k % 2], weight[k * P:(k + 1) * P, :]).then_inc(w_in[k % 2], 16)
            if final_gain is not None:
                sp.dma_start(gain[:], final_gain.partition_broadcast(P)).then_inc(gain_in, 16)
            load_x(0)
            load_x(1)
            load(1)
            for t in range(NT):
                if t % 2 == 0 and t // 2 + 2 < n_groups:
                    load(t // 2 + 2)
                sp.wait_ge(done, t + 1)
                sp.dma_start(out[t * P:(t + 1) * P, :], y[:, t % 2]).then_inc(stored[t % 2], 16)
                if t + 2 < NT:
                    load_x(t + 2)
            for p in range(2):
                sp.wait_ge(stored[p], 16 * (NT // 2))

        @block.gpsimd
        def _(pool):
            for g in range(n_groups):
                pool.wait_ge(hi_done, g + 1)
                if g >= 2:
                    pool.wait_ge(filled, 4 * (g - 1))
                nc.gpsimd.tensor_tensor(al[:, g % 2], a[:, g % 2], ah[:, g % 2].bitcast(F32),
                                        ALU.subtract).then_inc(lo_done, 1)

        @block.scalar
        def _(act):
            for k in range(KD):
                act.wait_ge(w_in[k % 2], 16 * (k // 2 + 1))
                nc.scalar.activation(w[0][:, k], raw[:, k % 2], ACT.Copy).then_inc(w_hi, 1)

            def hi(g):
                if gate is not None:
                    act.wait_ge(gated, g + 1)
                else:
                    act.wait_ge(a_in[g % 2], 16 * (g // 2 + 1))
                if g >= 2:
                    act.wait_ge(filled, 4 * (g - 1))
                nc.scalar.activation(ah[:, g % 2], a[:, g % 2], ACT.Copy).then_inc(hi_done, 1)

            hi(0)
            for t in range(NT):
                if t % 2 == 0 and t // 2 + 1 < n_groups:
                    hi(t // 2 + 1)
                if final_gain is not None:
                    act.wait_ge(added, t + 1)
                    nc.scalar.activation(junk[:], y[:, t % 2], ACT.Square,
                                         accum_out=ss[:, t:t + 1]).then_inc(squared, 1)
                    act.wait_ge(meaned, t + 1)
                    nc.scalar.activation(sd[:, t:t + 1], ms[:, t:t + 1], ACT.Sqrt).then_inc(rooted, 1)

        @block.vector
        def _(dve):
            def multiply_gate(g):
                if gate is not None:
                    dve.wait_ge(a_in[g % 2], 16 * (g // 2 + 1))
                    dve.wait_ge(gate_in, 16 * (g + 1))
                    nc.vector.tensor_tensor(a[:, g % 2], a[:, g % 2], gate[:], ALU.mult).then_inc(gated, 1)

            def finish(t):
                dve.wait_ge(squared, t + 1)
                nc.vector.tensor_scalar(ms[:, t:t + 1], ss[:, t:t + 1], 1.0 / D, EPS, ALU.mult,
                                        ALU.add).then_inc(meaned, 1)
                dve.wait_ge(rooted, t + 1)
                nc.vector.reciprocal(rs[:, t:t + 1], sd[:, t:t + 1])
                dve.drain()
                nc.vector.scalar_tensor_tensor(out=y[:, t % 2], in0=y[:, t % 2], scalar=rs[:, t:t + 1],
                                               in1=gain[:], op0=ALU.mult, op1=ALU.mult).then_inc(done, 1)

            multiply_gate(0)
            for k in range(KD):
                dve.wait_ge(w_hi, k + 1)
                nc.vector.tensor_tensor(w[1][:, k], raw[:, k % 2], w[0][:, k].bitcast(F32),
                                        ALU.subtract).then_inc(w_lo, 1)
            if final_gain is not None:
                dve.wait_ge(gain_in, 16)
            for t in range(NT):
                if t % 2 == 0 and t // 2 + 1 < n_groups:
                    multiply_gate(t // 2 + 1)
                dve.wait_ge(x_in[t % 2], 16 * (t // 2 + 1))
                if t >= 2:
                    dve.wait_ge(stored[t % 2], 16 * (t // 2))
                dve.wait_ge(filled, 2 * t + 2)
                last = nc.vector.tensor_tensor(y[:, t % 2], ps[:, t % 4].rearrange("p a b -> p (a b)"),
                                               x[:, t % 2], ALU.add)
                last.then_inc(added, 1)
                if final_gain is None:
                    dve.wait_ge(added, t + 1)
                    dve.sem_inc(done, 1)
                elif t >= 1:
                    finish(t - 1)
            if final_gain is not None:
                finish(NT - 1)

        @block.tensor
        def _(pe):
            pe.wait_ge(w_lo, KD)
            for t in range(NT):
                g, s = t // 2 % 2, slice(t % 2 * P, (t % 2 + 1) * P)
                pe.wait_ge(lo_done, t // 2 + 1)
                if t >= 4:
                    pe.wait_ge(added, t - 3)
                for b in range(2):
                    cols = slice(b * GT, (b + 1) * GT)
                    for k in range(KD):
                        last = mm3(nc.tensor, ps[:, t % 4, b], (ah[:, g, k, s], al[:, g, k, s]),
                                   [z[:, k, cols] for z in w], start=k == 0, stop=k == KD - 1)
                    last.then_inc(filled, 1)


def fm_run(count, column, dst, row, func=ACT.Copy, bias=False):
    return Run("fm", count, lambda j: [(0, column + P * j, P)],
               lambda j, g: dst[bass.ds(row + P * j, P), g * GT:(g + 1) * GT], func, bias)


def first_layer_runs(cqT, tm, gates):
    tm_parts = [[(0, C_PE, 32), (32, C_QB, 242)], [(0, C_QB + 242, 274)],
                [(0, C_QB + 516, 252), (252, C_QI, 22)], [(0, C_QI + 22, 274)]]
    return [Run("tm", 4, lambda j: tm_parts[j],
                lambda j, t: tm[t * P:(t + 1) * P, j * TM_CHUNK:(j + 1) * TM_CHUNK]),
            fm_run(3, C_Q, cqT, 0),
            fm_run(4, C_GA, gates, 0, ACT.Silu),
            fm_run(4, C_GB, gates, 512, ACT.Silu),
            fm_run(16, C_MA, gates, 1024, ACT.Sigmoid, True)]


def second_layer_runs(qT, kT, v, zT):
    nq, nkv = WH * HD, WKV * HD
    return [Run("tm", 1, lambda j: [(0, nq + nkv, nkv)], lambda j, t: v[t * P:(t + 1) * P, :]),
            fm_run(2, 0, qT, 0),
            fm_run(6, 2 * P, qT, 2 * P),
            fm_run(2, nq, kT, 0),
            fm_run(8, nq + 2 * nkv, zT, 0, ACT.Silu)]


def make_ident(nc, sem, ident):
    made = sem("ident_made")
    with nc.Block() as block:
        @block.gpsimd
        def _(pool):
            nc.gpsimd.memset(ident[:], 0.0).then_inc(made, 1)
            pool.wait_ge(made, 1)
            nc.gpsimd.affine_select(out=ident[:], in_=ident[:], compare_op=ALU.not_equal, fill=1.0,
                                    base=0, pattern=[[-1, P]], channel_multiplier=1).then_inc(made, 1)


def program(nc, a, out):
    with ExitStack() as c:
        sem = Sems(nc)
        dram = lambda n, *s, d=F32: nc.dram_tensor(f"scratch_{n}", s, d).ap()
        cqT, tm, gates = dram("cqT", 384, T), dram("tm", T, TM_W), dram("gates", 3072, T)
        qkT, va = dram("qkT", 2, 2 * H, QK, T), dram("va", 2, T, H * HD)
        qbT, kbT, vb = dram("qbT", 2, 4, P, T), dram("kbT", 2, P, T), dram("vb", 2, T, P)
        qiT, kiT, wi = dram("qiT", 2, 2, P, T), dram("kiT", 2, IDX, T), dram("wi", T, H)
        mask = dram("mask", T, T, d=BF16)
        oaT, obT, mergedT = dram("oaT", H * HD, T), dram("obT", H * HD, T), dram("mergedT", D, T)
        x1 = dram("x1", T, D)
        q2T, k2T, v2 = dram("q2T", WH * HD, T), dram("k2T", WKV * HD, T), dram("v2", T, WKV * HD)
        z2T, o2T = dram("z2T", WH * HD, T), dram("o2T", WH * HD, T)
        spread = dram("spread", WH, P, 3 * P)
        ident = c.enter_context(nc.sbuf_tensor("ident", [P, P], F32))
        make_ident(nc, sem, ident)
        sem.end_stage()

        with ExitStack() as c1:
            hT = [c1.enter_context(nc.sbuf_tensor(f"h1T_{n}", [P, KD, T], F32R)) for n in ("hi", "lo")]
            stage_norm(nc, sem, "n1", a["x"][0], a["norm_gain"][0], ident, hT)
            sem.end_stage()
            stage_project(nc, sem, "p1", hT, a["w_in"][0], TM_CHUNK, first_layer_runs(cqT, tm, gates),
                          a["b_merge"][0].rearrange("a n -> (a n)"))
            sem.end_stage()
        stage_qkv(nc, sem, ident, a, cqT, tm, qkT, qbT, kbT, qiT, kiT, va, vb, wi)
        sem.end_stage()
        stage_attention(nc, sem, "mla", ident, Mla(qkT, va, oaT))
        sem.end_stage()
        stage_index(nc, sem, ident, qiT, kiT, wi, mask)
        sem.end_stage()
        stage_attention(nc, sem, "dsa", ident, Dsa(qbT, kbT, vb, mask, obT))
        sem.end_stage()
        stage_branch(nc, sem, oaT, obT, gates, a["w_branch_mla"][0], a["w_branch_dsa"][0], mergedT)
        sem.end_stage()
        stage_out(nc, sem, "o1", mergedT, None, a["w_out"][0], a["x"][0], x1)
        sem.end_stage()

        with ExitStack() as c1:
            hT = [c1.enter_context(nc.sbuf_tensor(f"h2T_{n}", [P, KD, T], F32R)) for n in ("hi", "lo")]
            stage_norm(nc, sem, "n2", x1, a["norm_g_2"][0], ident, hT)
            sem.end_stage()
            stage_project(nc, sem, "p2", hT, a["a_w_in_2"][0], WKV * HD,
                          second_layer_runs(q2T, k2T, v2, z2T))
            sem.end_stage()
        stage_bias(nc, sem, a["one_hot"], a["t5_table_2"], spread)
        sem.end_stage()
        stage_attention(nc, sem, "win", ident, Window(q2T, k2T, v2, spread, a["a_sinks_2"][0], o2T))
        sem.end_stage()
        stage_out(nc, sem, "o2", o2T, z2T, a["a_w_out_2"][0], x1, out[0], a["final_g_2"])
        sem.end_stage()


_INS = ["x", "positions", "norm_gain", "w_in", "b_merge", "mla_q_norm", "mla_w_uq", "mla_kv_norm",
        "mla_w_ukv", "mla_q_gain", "mla_k_gain", "dsa_q_gain", "dsa_k_gain", "w_branch_mla",
        "w_branch_dsa", "w_out", "t5_table_2", "norm_g_2", "final_g_2", "a_w_in_2", "a_sinks_2",
        "a_w_out_2"]


def kernel(**inputs):
    import concourse.bacc as bacc
    from concourse.bass_utils import run_bass_kernel_spmd

    nc = bacc.Bacc("TRN2", target_bir_lowering=False, num_devices=1)
    given = {name: np.ascontiguousarray(inputs[name]) for name in _INS}
    given["one_hot"] = t5_one_hot()
    arrays, aps = {}, {}
    for name, x in given.items():
        arrays[f"in_{name}"] = x
        aps[name] = nc.dram_tensor(f"in_{name}", x.shape, mybir.dt.from_np(x.dtype), kind="ExternalInput").ap()
    out = nc.dram_tensor("out_x", (1, T, D), F32, kind="ExternalOutput").ap()
    program(nc, aps, out)
    r = run_bass_kernel_spmd(nc, [arrays], core_ids=[0])
    return r.results[0]["out_x"]
```

```python
import math
from contextlib import ExitStack

import numpy as np
import concourse.bass as bass
from concourse import mybir
from concourse.alu_op_type import AluOpType as ALU

F32 = mybir.dt.float32
F32R = mybir.dt.float32r
BF16 = mybir.dt.bfloat16
I32 = mybir.dt.int32
ACT = mybir.ActivationFunctionType
AX = mybir.AxisListType

P = 128
T = 2048
NT = T // P
D = 1024
KD = D // P
GT = 512
NG = T // GT
EPS = 1e-6

H = 8
QK, NOPE, ROPE_M = 96, 64, 32
HD = 64
KV = 2
IDX = 32
TOPK = min(256, T // 4)
ROT_D, ROT_I = 16, 8
THETA = 500000.0

SPLITS = [256, 128, 32, 512, 512, 128, 128, 512, 256, 32, 8, 1024, 1024]
(C_Q, C_KV, C_PE, C_GA, C_QB, C_KB, C_VB, C_GB, C_QI, C_KI, C_WI, C_MA, C_MB) = (
    sum(SPLITS[:i]) for i in range(len(SPLITS)))
C_END = sum(SPLITS)

TM_PE, TM_QB, TM_KB, TM_VB, TM_QI, TM_KI, TM_WI = 0, 32, 544, 672, 800, 1056, 1088
TM_W = 1096
TM_CHUNK = TM_W // 4

WH, WKV, WG = 16, 4, 4
WINDOW = 128
NEG = -1e30
ND = 257


class Sems:

    def __init__(self, nc):
        self.nc, self.live = nc, []

    def __call__(self, name, count=None):
        if count is None:
            self.live.append(self.nc.alloc_semaphore(name=name))
            return self.live[-1]
        return [self(f"{name}{i}") for i in range(count)]

    def end_stage(self):
        self.nc.clear_and_free_semaphores(self.live)
        self.nc.all_engine_barrier()
        self.live = []


def mm3(pe, out, l, r, start, stop):
    pe.matmul(out, l[0], r[1], start=start, stop=False)
    pe.matmul(out, l[1], r[0], start=False, stop=False)
    return pe.matmul(out, l[0], r[0], start=False, stop=stop)


def stage_norm(nc, sem, tag, x_dram, gain_dram, ident, hT):
    hi, lo = hT
    with ExitStack() as c:
        sb = lambda n, s, d=F32: c.enter_context(nc.sbuf_tensor(f"{tag}_{n}", s, d))
        xt = sb("xt", [P, 3, D])
        h = sb("h", [P, 2, D])
        junk = sb("junk", [P, D])
        g = sb("g", [P, 2, KD, P])
        gain = sb("gain", [P, KD])
        ss = sb("ss", [P, NT])
        ms = sb("ms", [P, NT])
        sd = sb("sd", [P, NT])
        rs = sb("rs", [P, NT])
        tp = c.enter_context(nc.psum_tensor(f"{tag}_tp", [P, 2, KD, P], F32))
        x_in = sem(f"{tag}_x_in", 3)
        gain_in, squared, meaned, rooted, normed, turned, gained, hi_done, lo_done = (
            sem(f"{tag}_{n}") for n in ("gain_in", "squared", "meaned", "rooted", "normed", "turned",
                                        "gained", "hi_done", "lo_done"))
        block = c.enter_context(nc.Block())

        @block.sync
        def _(sp):
            sp.dma_start(gain[:], gain_dram.rearrange("(k p) -> p k", p=P),
                         allow_slow_non_contiguous=True).then_inc(gain_in, 16)
            for t in range(NT):
                if t >= 3:
                    sp.wait_ge(normed, t - 2)
                sp.dma_start(xt[:, t % 3], x_dram[t * P:(t + 1) * P, :]).then_inc(x_in[t % 3], 16)

        @block.scalar
        def _(act):
            def square(t):
                act.wait_ge(x_in[t % 3], 16 * (t // 3 + 1))
                if t >= 1:
                    act.wait_ge(squared, t)
                nc.scalar.activation(junk[:], xt[:, t % 3], ACT.Square,
                                     accum_out=ss[:, t:t + 1]).then_inc(squared, 1)

            square(0)
            for t in range(NT):
                if t + 1 < NT:
                    square(t + 1)
                act.wait_ge(meaned, t + 1)
                nc.scalar.activation(sd[:, t:t + 1], ms[:, t:t + 1], ACT.Sqrt).then_inc(rooted, 1)
                if t >= 1:
                    act.wait_ge(gained, t)
                    nc.scalar.activation(hi[:, :, (t - 1) * P:t * P], g[:, (t - 1) % 2],
                                         ACT.Copy).then_inc(hi_done, 1)
            act.wait_ge(gained, NT)
            nc.scalar.activation(hi[:, :, (NT - 1) * P:NT * P], g[:, (NT - 1) % 2],
                                 ACT.Copy).then_inc(hi_done, 1)

        @block.vector
        def _(dve):
            def mean(t):
                dve.wait_ge(squared, t + 1)
                nc.vector.tensor_scalar(ms[:, t:t + 1], ss[:, t:t + 1], 1.0 / D, EPS, ALU.mult,
                                        ALU.add).then_inc(meaned, 1)

            def norm(t):
                dve.wait_ge(rooted, t + 1)
                nc.vector.reciprocal(rs[:, t:t + 1], sd[:, t:t + 1])
                dve.drain()
                if t >= 2:
                    dve.wait_ge(turned, t - 1)
                nc.vector.tensor_scalar(h[:, t % 2], xt[:, t % 3], rs[:, t:t + 1], None,
                                        ALU.mult).then_inc(normed, 1)

            def gains(t):
                dve.wait_ge(turned, t + 1)
                if t >= 2:
                    dve.wait_ge(lo_done, t - 1)
                nc.vector.tensor_tensor(g[:, t % 2], tp[:, t % 2],
                                        gain[:].unsqueeze(2).broadcast_to([P, KD, P]),
                                        ALU.mult).then_inc(gained, 1)

            dve.wait_ge(gain_in, 16)
            mean(0)
            for t in range(NT):
                norm(t)
                if t + 1 < NT:
                    mean(t + 1)
                if t >= 1:
                    gains(t - 1)
            gains(NT - 1)

        @block.gpsimd
        def _(pool):
            for t in range(NT):
                pool.wait_ge(hi_done, t + 1)
                s = slice(t * P, (t + 1) * P)
                nc.gpsimd.tensor_tensor(lo[:, :, s], g[:, t % 2], hi[:, :, s].bitcast(F32),
                                        ALU.subtract).then_inc(lo_done, 1)

        @block.tensor
        def _(pe):
            for t in range(NT):
                pe.wait_ge(normed, t + 1)
                if t >= 2:
                    pe.wait_ge(gained, t - 1)
                for k in range(KD):
                    last = nc.tensor.transpose(tp[:, t % 2, k], h[:, t % 2, k * P:(k + 1) * P], ident[:])
                last.then_inc(turned, 1)


class Run:

    def __init__(self, kind, count, columns, store, func=ACT.Copy):
        self.kind, self.count, self.columns, self.store = kind, count, columns, store
        self.func = func


def each_chunk(eng, runs, body):
    n = 0
    for run in runs:
        if run.kind == "fm" and run.count >= 4:
            with eng.Fori(0, run.count // 2) as i:
                for p in (0, 1):
                    body(n + p + 2 * i, (n + p) % 2, (n + p) // 2 + i, p + 2 * i, run)
        else:
            for j in range(run.count):
                body(n + j, (n + j) % 2, (n + j) // 2, j, run)
        n += run.count


def stage_project(nc, sem, tag, hT, weight, width, runs, h_dram=None):
    n_tm = sum(r.count for r in runs if r.kind == "tm")
    total = sum(r.count for r in runs)
    w_view = weight.rearrange("(k p) n -> p k n", p=P)
    parts = [len(r.columns(j if r.kind == "tm" else 0)) for r in runs for j in range(r.count)]
    assert all(x == 1 for x in parts[n_tm:])

    def first_step(n):
        if isinstance(n, int) and n <= n_tm:
            return NT * n
        return NG * n + (NT - NG) * n_tm

    def loaded(n, par, use):
        if isinstance(n, int):
            return 16 * sum(parts[m] for m in range(par, n + 1, 2))
        return 16 * (use + 1 + sum(parts[m] - 1 for m in range(par, n_tm, 2)))

    def steps(n, par, run):
        if run.kind == "tm":
            return [(first_step(n) + t, t % 8, t % 4, t, width) for t in range(NT)]
        return [(first_step(n) + g, g + NG * ((par + n_tm) % 2), g, g, GT) for g in range(NG)]

    def stores_before(n, g):
        if isinstance(n, int) and n < n_tm:
            return 4 * n + g // 4
        return n + 3 * n_tm

    with ExitStack() as c:
        sb = lambda n, s, d=F32: c.enter_context(nc.sbuf_tensor(f"{tag}_{n}", s, d))
        ws = sb("ws", [P, 2, KD, width])
        wh = sb("wh", [P, 2, KD, width], F32R)
        wl = sb("wl", [P, 2, KD, width], F32R)
        ob = sb("ob", [P, 4, GT])
        ps = c.enter_context(nc.psum_tensor(f"{tag}_ps", [P, 8, GT], F32))
        w_in = sem(f"{tag}_w_in", 2)
        stored = sem(f"{tag}_stored", 4)
        w_split, filled, evacuated, h_stored = (
            sem(f"{tag}_{n}") for n in ("w_split", "filled", "evacuated", "h_stored"))
        block = c.enter_context(nc.Block())

        @block.sync
        def _(sp):
            def load(n, par, use, j, run):
                if not isinstance(n, int) or n >= 2:
                    sp.wait_ge(w_split, n - 1)
                for at, c0, w in run.columns(j):
                    sp.dma_start(ws[:, par, :, at:at + w],
                                 w_view[:, :, bass.ds(c0, w)]).then_inc(w_in[par], 16)

            each_chunk(sp, runs, load)

        @block.gpsimd
        def _(pool):
            if h_dram is not None:
                for g in range(NG):
                    for half in range(2):
                        s = slice(g * GT, (g + 1) * GT)
                        pool.dma_start(h_dram[half, :, :, s], hT[half][:, :, s].bitcast(F32)).then_inc(h_stored, 16)
                pool.wait_ge(h_stored, 32 * NG)

        @block.vector
        def _(dve):
            def split(n, par, use, j, run):
                w = width if run.kind == "tm" else P
                dve.wait_ge(w_in[par], loaded(n, par, use))
                if not isinstance(n, int) or n >= 2:
                    dve.wait_ge(filled, first_step(n - 1))
                nc.vector.tensor_copy(wh[:, par, :, 0:w], ws[:, par, :, 0:w])
                dve.drain()
                nc.vector.tensor_tensor(wl[:, par, :, 0:w], ws[:, par, :, 0:w],
                                        wh[:, par, :, 0:w].bitcast(F32), ALU.subtract).then_inc(w_split, 1)

            each_chunk(dve, runs, split)

        @block.tensor
        def _(pe):
            hi, lo = hT

            def multiply(n, par, use, j, run):
                pe.wait_ge(w_split, n + 1)
                for u, bank, _, g, w in steps(n, par, run):
                    if not isinstance(u, int) or u >= 8:
                        pe.wait_ge(evacuated, u - 7)
                    for k in range(KD):
                        if run.kind == "tm":
                            s = slice(g * P, (g + 1) * P)
                            l, r = (hi[:, k, s], lo[:, k, s]), (wh[:, par, k, 0:w], wl[:, par, k, 0:w])
                        else:
                            s = slice(g * GT, (g + 1) * GT)
                            l, r = (wh[:, par, k, 0:P], wl[:, par, k, 0:P]), (hi[:, k, s], lo[:, k, s])
                        last = mm3(nc.tensor, ps[:, bank, 0:w], l, r, start=k == 0, stop=k == KD - 1)
                    last.then_inc(filled, 1)

            each_chunk(pe, runs, multiply)

        @block.scalar
        def _(act):
            def evacuate(n, par, use, j, run):
                for u, bank, slot, g, w in steps(n, par, run):
                    target = ob[:, slot, 0:w]
                    if not isinstance(n, int) or stores_before(n, g) >= 1:
                        act.wait_ge(stored[slot], 16 * stores_before(n, g))
                    act.wait_ge(filled, u + 1)
                    nc.scalar.activation(target, ps[:, bank, 0:w], run.func).then_inc(evacuated, 1)
                    act.wait_ge(evacuated, u + 1)
                    act.dma_start(run.store(j, g), target).then_inc(stored[slot], 16)

            each_chunk(act, runs, evacuate)
            for g in range(4):
                act.wait_ge(stored[g], 16 * (total + 3 * n_tm))


FREQS = [(ROPE_M, 0), (ROT_D, ROPE_M // 2), (ROT_I, ROPE_M // 2 + ROT_D // 2)]
NF = (ROPE_M + ROT_D + ROT_I) // 2
TWO_PI = 2 * math.pi
PI_A = 6.28125
PI_B = float(np.float32(np.round((TWO_PI - PI_A) * 2.0 ** 19) / 2.0 ** 19))
PI_C = float(TWO_PI - PI_A - PI_B)
ROUNDER = 1.5 * 2.0 ** 23


def stage_qkv(nc, sem, ident, a, cqT, tm, qkT, qbT, kbT, qiT, kiT, va, vb, wi):
    RING = 7
    AHEAD = 2
    NB = 6
    with ExitStack() as c:
        sb = lambda n, s, d=F32: c.enter_context(nc.sbuf_tensor(f"b_{n}", s, d))
        pos_i = sb("pos_i", [P, NT], I32)
        pos = sb("pos", [P, NT])
        freq = sb("freq", [P, NF])
        ang = sb("ang", [P, NT, NF])
        turns = sb("turns", [P, NT, NF])
        red = sb("red", [P, 2, NT, NF])
        cos2 = sb("cos2", [P, NT, 2 * NF])
        sin2 = sb("sin2", [P, NT, 2 * NF])
        c_gain = sb("c_gain", [P, 3])
        qk_gain = sb("qk_gain", [P, 2, QK])
        b_gain = sb("b_gain", [P, 2, HD])
        ones = sb("ones", [P, 2])
        uqs = [sb(f"uq_{n}", [P, 2, H * QK], F32R) for n in ("hi", "lo")]
        ukv = sb("ukv", [P, D])
        ukvs = [sb(f"ukv_{n}", [P, D], F32R) for n in ("hi", "lo")]
        tmb = sb("tmb", [P, RING, TM_W])
        cq = sb("cq", [P, 4, 3, P])
        csq = sb("csq", [P, 2, 3, P])
        cg = sb("cg", [P, 2, 3, P])
        ch = sb("ch", [P, 2, 3, P], F32R)
        cl = sb("cl", [P, 2, 3, P], F32R)
        st1 = sb("st1", [P, NT, 2])
        sd1 = sb("sd1", [P, NT, 2])
        rs1 = sb("rs1", [P, NT, 2])
        qk = sb("qk", [P, RING, 2 * H, QK])
        qb = sb("qb", [P, 4, H + KV, HD])
        sq = sb("sq", [P, 2 * H * QK + (H + KV) * HD])
        uq = sq[:, 0:2 * H * QK].rearrange("p (k n) -> p k n", k=2)
        st2 = sb("st2", [P, 26])
        ms2 = sb("ms2", [P, 26])
        sd2 = sb("sd2", [P, 26])
        rs2 = sb("rs2", [P, 26])
        rot = sb("rot", [P, 2, 2 * H, ROPE_M])
        rot_p = sb("rot_p", [P, 2, H + KV, ROT_D])
        v = sb("v", [P, 4, 640])
        vh = sb("vh", [P, 3, 640], F32R)
        vl = sb("vl", [P, 3, 640], F32R)
        wi_all = sb("wi_all", [P, NT, H])
        th = sb("th", [P, NB, GT], F32R)
        tl = sb("tl", [P, NB, GT], F32R)
        p_ss = c.enter_context(nc.psum_tensor("b_ps_ss", [P, 4], F32))
        p_up = c.enter_context(nc.psum_tensor("b_ps_up", [P, 4, GT], F32))
        p_t = c.enter_context(nc.psum_tensor("b_ps_t", [P, 3, GT], F32))
        const_in, w_ready, trig_r, trig, filled_c = (
            sem(f"b_{n}") for n in ("const_in", "w_ready", "trig_r", "trig", "ones_made"))
        tm_in, cq_in = sem("b_tm_in", RING), sem("b_cq_in", 4)
        (c_squared, c_gained, c_hi, c_lo, summed, meaned1, rooted1, scaled1, up, up_read, pe_spread,
         squared2, meaned2, rooted2, normed, gained, roped, roped_p, v_hi, v_lo, turned, t_hi, t_lo) = (
            sem(f"b_{n}") for n in
            ("c_squared", "c_gained", "c_hi", "c_lo", "summed", "meaned1", "rooted1", "scaled1", "up",
             "up_read", "pe_spread", "squared2", "meaned2", "rooted2", "normed", "gained", "roped",
             "roped_p", "v_hi", "v_lo", "turned", "t_hi", "t_lo"))
        t_stored = sem("b_t_stored", NB)
        v_stored = sem("b_v_stored", 3)
        wi_made, wi_stored = sem("b_wi_made"), sem("b_wi_stored")
        block = c.enter_context(nc.Block())
        def staged(parts):
            for i in range(NT + max(k for k, _ in parts)):
                for k, f in parts:
                    if 0 <= i - k < NT:
                        f(i - k)

        def stored_of(tiles, b):
            return (96 if b == NB - 1 else 32) * tiles

        def rotate(ops, eng, x, table, t, tmp, done):
            rd, f0 = FREQS[table]
            n, h = x.shape[1], rd // 2
            spread = lambda tab, a0, a1: tab[:, t, 2 * f0 + a0:2 * f0 + a1].unsqueeze(1)\
                .broadcast_to([P, n, a1 - a0])
            ops.tensor_tensor(tmp[:, 1, 0:n, 0:h], x[:, :, h:rd], spread(sin2, 0, h), ALU.mult)
            ops.tensor_tensor(tmp[:, 1, 0:n, h:rd], x[:, :, 0:h], spread(sin2, h, rd), ALU.mult)
            ops.tensor_tensor(tmp[:, 0, 0:n, 0:rd], x, spread(cos2, 0, rd), ALU.mult)
            eng.drain()
            last = ops.tensor_tensor(x, tmp[:, 0, 0:n, 0:rd], tmp[:, 1, 0:n, 0:rd], ALU.add)
            if done is not None:
                last.then_inc(done, 1)
            return last

        @block.sync
        def _(sp):
            sp.dma_start(pos_i[:], a["positions"][0].rearrange("(t p) -> p t", p=P),
                         allow_slow_non_contiguous=True).then_inc(const_in, 16)
            sp.dma_start(c_gain[:, 0:2], a["mla_q_norm"][0].rearrange("(k p) -> p k", p=P),
                         allow_slow_non_contiguous=True).then_inc(const_in, 16)
            sp.dma_start(c_gain[:, 2:3], a["mla_kv_norm"].rearrange("a p -> p a"),
                         allow_slow_non_contiguous=True).then_inc(const_in, 16)
            for dst, name in ((qk_gain[:, 0], "mla_q_gain"), (qk_gain[:, 1], "mla_k_gain"),
                              (b_gain[:, 0], "dsa_q_gain"), (b_gain[:, 1], "dsa_k_gain")):
                sp.dma_start(dst, a[name][0].partition_broadcast(P)).then_inc(const_in, 16)
            sp.dma_start(uq, a["mla_w_uq"][0].rearrange("(k p) n -> p k n", p=P)).then_inc(const_in, 16)
            sp.dma_start(ukv[:], a["mla_w_ukv"][0]).then_inc(const_in, 16)

            def load(t):
                s = slice(t * P, (t + 1) * P)
                if t >= RING:
                    sp.wait_ge(turned, NB * (t - RING + 1))
                    sp.wait_ge(v_lo, t - RING + 1)
                sp.dma_start(tmb[:, t % RING], tm[s, :]).then_inc(tm_in[t % RING], 16)
                if t >= 4:
                    sp.wait_ge(c_gained, t - 3)
                    sp.wait_ge(c_squared, t - 3)
                sp.dma_start(cq[:, t % 4], cqT.rearrange("(k p) t -> p k t", p=P)[:, :, s])\
                    .then_inc(cq_in[t % 4], 16)

            def store_values(t):
                s = slice(t * P, (t + 1) * P)
                sp.wait_ge(v_lo, t + 1)
                for half, src in ((0, vh), (1, vl)):
                    sp.dma_start(va[half, s, :], src[:, t % 3, 0:512].bitcast(F32)).then_inc(v_stored[t % 3], 16)
                    sp.dma_start(vb[half, s, :], src[:, t % 3, 512:640].bitcast(F32)).then_inc(v_stored[t % 3], 16)

            def store_turned(t):
                s = slice(t * P, (t + 1) * P)
                for b in range(NB):
                    sp.wait_ge(t_lo, NB * t + b + 1)
                    for half, src in ((0, th), (1, tl)):
                        x = src[:, b].bitcast(F32).rearrange("p (j t) -> p j t", t=P)
                        done = t_stored[b]
                        if b < 4:
                            sp.dma_start(qkT[half, 4 * b:4 * b + 4, :, s].rearrange("h d t -> d h t"),
                                         x[0:QK]).then_inc(done, 16)
                        elif b == 4:
                            sp.dma_start(qbT[half, :, :, s].rearrange("j p t -> p j t"), x).then_inc(done, 16)
                        else:
                            sp.dma_start(kbT[half, :, s], x[:, 0]).then_inc(done, 16)
                            sp.dma_start(qiT[half, :, :, s].rearrange("j p t -> p j t"),
                                         x[:, 1:3]).then_inc(done, 16)
                            sp.dma_start(kiT[half, :, s], x[0:IDX, 3]).then_inc(done, 16)

            staged([(AHEAD + 6, store_turned), (AHEAD + 3, store_values), (0, load)])
            sp.wait_ge(wi_made, NT)
            sp.dma_start(wi.rearrange("(t p) h -> p t h", p=P), wi_all[:]).then_inc(wi_stored, 16)
            sp.wait_ge(wi_stored, 16)
            for b in range(NB):
                sp.wait_ge(t_stored[b], stored_of(NT, b))
            for n in range(3):
                sp.wait_ge(v_stored[n], 64 * len(range(n, NT, 3)))

        @block.scalar
        def _(act):
            act.wait_ge(trig_r, 1)
            nc.scalar.activation(red[:], red[:], ACT.Sin).then_inc(trig_r, 1)

            def squares_c(t):
                act.wait_ge(cq_in[t % 4], 16 * (t // 4 + 1))
                if t >= 2:
                    act.wait_ge(summed, t - 1)
                nc.scalar.activation(csq[:, t % 2], cq[:, t % 4], ACT.Square).then_inc(c_squared, 1)

            def split_c(t):
                act.wait_ge(c_gained, t + 1)
                if t >= 2:
                    act.wait_ge(up, 2 * (t - 1))
                nc.scalar.activation(ch[:, t % 2], cg[:, t % 2], ACT.Copy).then_inc(c_hi, 1)

            def roots_c(t):
                act.wait_ge(meaned1, t + 1)
                nc.scalar.activation(sd1[:, t], st1[:, t], ACT.Sqrt).then_inc(rooted1, 1)

            def heads(t):
                act.wait_ge(scaled1, t + 1)
                if t >= RING:
                    act.wait_ge(turned, NB * (t - RING + 1))
                if t >= 4:
                    act.wait_ge(v_lo, t - 3)
                act.wait_ge(up, 2 * t + 1)
                for b in range(2):
                    nc.scalar.activation(qk[:, t % RING, 4 * b:4 * b + 4],
                                         p_up[:, b, 0:4 * QK].rearrange("p (h d) -> p h d", d=QK),
                                         ACT.Copy, scale=rs1[:, t, 0:1])
                act.wait_ge(up, 2 * t + 2)
                for b in range(2):
                    kv = p_up[:, 2 + b].rearrange("p (h d) -> p h d", d=NOPE + HD)
                    nc.scalar.activation(qk[:, t % RING, H + 4 * b:H + 4 * b + 4, 0:NOPE], kv[:, :, 0:NOPE],
                                         ACT.Copy, scale=rs1[:, t, 1:2])
                    last = nc.scalar.activation(
                        v[:, t % 4, 256 * b:256 * b + 256].rearrange("p (h d) -> p h d", d=HD),
                        kv[:, :, NOPE:], ACT.Copy, scale=rs1[:, t, 1:2])
                last.then_inc(up_read, 1)

            def squares(t):
                act.wait_ge(up_read, t + 1)
                act.wait_ge(pe_spread, t + 1)
                if t >= 1:
                    act.wait_ge(meaned2, t)
                n = 2 * H * QK
                nc.scalar.activation(sq[:, 0:n], qk[:, t % RING].rearrange("p h d -> p (h d)"), ACT.Square)
                nc.scalar.activation(sq[:, n:], tmb[:, t % RING, TM_QB:TM_VB], ACT.Square).then_inc(squared2, 1)
                if t >= 3:
                    act.wait_ge(v_stored[t % 3], 64 * (t // 3))
                    act.wait_ge(v_lo, t - 2)
                nc.scalar.activation(vh[:, t % 3], v[:, t % 4], ACT.Copy).then_inc(v_hi, 1)

            def roots(t):
                act.wait_ge(meaned2, t + 1)
                if t >= 1:
                    act.wait_ge(normed, t)
                nc.scalar.activation(sd2[:], ms2[:], ACT.Sqrt).then_inc(rooted2, 1)

            def split_turned(t):
                for b in range(NB):
                    u = NB * t + b
                    act.wait_ge(turned, u + 1)
                    if t >= 1:
                        act.wait_ge(t_stored[b], stored_of(t, b))
                        act.wait_ge(t_lo, u - NB + 1)
                    rows = QK if b < 4 else P
                    parts = [(rows, 0, GT)] if b < 5 else [(P, 0, 3 * P), (IDX, 3 * P, GT)]
                    for r, x0, x1 in parts:
                        last = nc.scalar.activation(th[0:r, b, x0:x1], p_t[0:r, u % 3, x0:x1], ACT.Copy)
                    last.then_inc(t_hi, 1)

            staged([(1, roots_c), (6, split_turned), (2, squares), (0, squares_c), (0, split_c), (1, heads),
                    (2, roots)])

        @block.vector
        def _(dve):
            for n, (rd, f0) in enumerate(FREQS):
                for f in range(rd // 2):
                    value = float(np.float32(THETA) ** (-np.float32(2 * f) / np.float32(rd)))
                    nc.vector.memset(freq[:, f0 + f:f0 + f + 1], value)
            nc.vector.memset(ones[:], 1.0).then_inc(filled_c, 1)
            dve.wait_ge(const_in, 16 * 9)
            nc.vector.tensor_copy(pos[:], pos_i[:])
            nc.vector.tensor_copy(uqs[0][:], uq)
            nc.vector.tensor_copy(ukvs[0][:], ukv[:])
            dve.drain()
            nc.vector.tensor_tensor(uqs[1][:], uq, uqs[0][:].bitcast(F32), ALU.subtract)
            nc.vector.tensor_tensor(ukvs[1][:], ukv[:], ukvs[0][:].bitcast(F32), ALU.subtract)\
                .then_inc(w_ready, 1)
            nc.vector.tensor_tensor(ang[:], pos[:].unsqueeze(2).broadcast_to([P, NT, NF]),
                                    freq[:].unsqueeze(1).broadcast_to([P, NT, NF]), ALU.mult)
            dve.drain()
            for which, quarter in ((0, 0.25), (1, 0.0)):
                nc.vector.tensor_scalar(turns[:], ang[:], 1 / TWO_PI, quarter, ALU.mult, ALU.add)
                dve.drain()
                nc.vector.tensor_scalar(turns[:], turns[:], ROUNDER, None, ALU.add)
                dve.drain()
                nc.vector.tensor_scalar(turns[:], turns[:], ROUNDER, None, ALU.subtract)
                dve.drain()
                src = ang[:]
                for part in (PI_A, PI_B, PI_C):
                    nc.vector.scalar_tensor_tensor(out=red[:, which], in0=turns[:], scalar=-part, in1=src,
                                                   op0=ALU.mult, op1=ALU.add)
                    dve.drain()
                    src = red[:, which]
                if quarter:
                    nc.vector.tensor_scalar(red[:, which], red[:, which], math.pi / 2, None, ALU.add)
                    dve.drain()
            last = nc.vector.tensor_scalar(red[:], red[:], 3.1415925, -3.1415925, ALU.min, ALU.max)
            last.then_inc(trig_r, 1)
            dve.wait_ge(trig_r, 2)
            for rd, f0 in FREQS:
                h = rd // 2
                for half in range(2):
                    at = slice(2 * f0 + half * h, 2 * f0 + half * h + h)
                    nc.vector.tensor_copy(cos2[:, :, at], red[:, 0, :, f0:f0 + h])
                    last = nc.vector.tensor_scalar(sin2[:, :, at], red[:, 1, :, f0:f0 + h],
                                                   1.0 if half else -1.0, None, ALU.mult)
            last.then_inc(trig, 1)

            def gains_c(t):
                dve.wait_ge(cq_in[t % 4], 16 * (t // 4 + 1))
                if t >= 2:
                    dve.wait_ge(c_lo, t - 1)
                    dve.wait_ge(c_hi, t - 1)
                nc.vector.tensor_tensor(cg[:, t % 2], cq[:, t % 4],
                                        c_gain[:].unsqueeze(2).broadcast_to([P, 3, P]),
                                        ALU.mult).then_inc(c_gained, 1)

            def split_c(t):
                dve.wait_ge(c_hi, t + 1)
                nc.vector.tensor_tensor(cl[:, t % 2], cg[:, t % 2], ch[:, t % 2].bitcast(F32),
                                        ALU.subtract).then_inc(c_lo, 1)
                dve.wait_ge(summed, t + 1)
                nc.vector.tensor_scalar(st1[:, t, 0:1], p_ss[:, 0:1], 1.0 / 256, EPS, ALU.mult, ALU.add)
                nc.vector.tensor_scalar(st1[:, t, 1:2], p_ss[:, 2:3], 1.0 / 128, EPS, ALU.mult,
                                        ALU.add).then_inc(meaned1, 1)

            def scales_c(t):
                dve.wait_ge(rooted1, t + 1)
                nc.vector.reciprocal(rs1[:, t], sd1[:, t]).then_inc(scaled1, 1)

            def means(t):
                dve.wait_ge(squared2, t + 1)
                n = 2 * H * QK
                nc.vector.tensor_reduce(st2[:, 0:16], sq[:, 0:n].rearrange("p (h d) -> p h d", d=QK),
                                        AX.X, ALU.add)
                nc.vector.tensor_reduce(st2[:, 16:26], sq[:, n:].rearrange("p (h d) -> p h d", d=HD),
                                        AX.X, ALU.add)
                dve.drain()
                if t >= 1:
                    dve.wait_ge(rooted2, t)
                nc.vector.tensor_scalar(ms2[:, 0:16], st2[:, 0:16], 1.0 / QK, EPS, ALU.mult, ALU.add)
                nc.vector.tensor_scalar(ms2[:, 16:26], st2[:, 16:26], 1.0 / HD, EPS, ALU.mult,
                                        ALU.add).then_inc(meaned2, 1)

            def norms(t):
                dve.wait_ge(rooted2, t + 1)
                nc.vector.reciprocal(rs2[:], sd2[:])
                dve.drain()
                if t >= 4:
                    dve.wait_ge(turned, NB * (t - 3))
                nc.vector.tensor_tensor(qk[:, t % RING], qk[:, t % RING],
                                        rs2[:, 0:16].unsqueeze(2).broadcast_to([P, 16, QK]), ALU.mult)
                nc.vector.tensor_tensor(qb[:, t % 4],
                                        tmb[:, t % RING, TM_QB:TM_VB].rearrange("p (h d) -> p h d", d=HD),
                                        rs2[:, 16:26].unsqueeze(2).broadcast_to([P, 10, HD]),
                                        ALU.mult).then_inc(normed, 1)

            def rotate_heads(t):
                dve.wait_ge(gained, t + 1)
                rotate(nc.vector, dve, qk[:, t % RING, :, NOPE:QK], 0, t, rot, roped)

            def split_turned(t):
                for b in range(NB):
                    u = NB * t + b
                    dve.wait_ge(t_hi, u + 1)
                    parts = [(QK if b < 4 else P, 0, GT)] if b < 5 else [(P, 0, 3 * P), (IDX, 3 * P, GT)]
                    for r, x0, x1 in parts:
                        last = nc.vector.tensor_tensor(tl[0:r, b, x0:x1], p_t[0:r, u % 3, x0:x1],
                                                       th[0:r, b, x0:x1].bitcast(F32), ALU.subtract)
                    last.then_inc(t_lo, 1)

            staged([(0, gains_c), (6, split_turned), (1, scales_c), (3, norms), (2, means),
                    (5, rotate_heads), (0, split_c)])

        @block.gpsimd
        def _(pool):
            pool.wait_ge(const_in, 16 * 9)
            pool.wait_ge(trig, 1)

            def spread_k(t):
                pool.wait_ge(tm_in[t % RING], 16 * (t // RING + 1))
                if t >= RING:
                    pool.wait_ge(turned, NB * (t - RING + 1))
                nc.gpsimd.tensor_copy(qk[:, t % RING, H:2 * H, NOPE:QK],
                                      tmb[:, t % RING, 0:ROPE_M].unsqueeze(1).broadcast_to([P, H, ROPE_M]))
                nc.gpsimd.tensor_copy(v[:, t % 4, 512:640], tmb[:, t % RING, TM_VB:TM_QI]).then_inc(pe_spread, 1)

            def split_values(t):
                pool.wait_ge(v_hi, t + 1)
                if t >= 3:
                    pool.wait_ge(v_stored[t % 3], 64 * (t // 3))
                nc.gpsimd.tensor_tensor(vl[:, t % 3], v[:, t % 4], vh[:, t % 3].bitcast(F32),
                                        ALU.subtract).then_inc(v_lo, 1)
                ix = tmb[:, t % RING, TM_QI:TM_WI].rearrange("p (h d) -> p h d", d=IDX)
                rotate(nc.gpsimd, pool, ix[:, :, 0:ROT_I], 2, t, rot_p, None)
                nc.gpsimd.tensor_scalar(wi_all[:, t], tmb[:, t % RING, TM_WI:TM_W],
                                        H ** -0.5 * IDX ** -0.5, None, ALU.mult).then_inc(wi_made, 1)
                pool.drain()

            def gains(t):
                pool.wait_ge(normed, t + 1)
                for n in range(2):
                    x = qk[:, t % RING, H * n:H * n + H]
                    last = nc.gpsimd.tensor_tensor(x, x, qk_gain[:, n].unsqueeze(1)
                                                   .broadcast_to([P, H, QK]), ALU.mult)
                last.then_inc(gained, 1)
                for n, (h0, h1) in enumerate(((0, H), (H, H + KV))):
                    x = qb[:, t % 4, h0:h1]
                    nc.gpsimd.tensor_tensor(x, x, b_gain[:, n].unsqueeze(1)
                                            .broadcast_to([P, h1 - h0, HD]), ALU.mult)
                pool.drain()
                rotate(nc.gpsimd, pool, qb[:, t % 4, :, 0:ROT_D], 1, t, rot_p, roped_p)
                pool.drain()

            staged([(4, gains), (1, spread_k), (3, split_values)])

        @block.tensor
        def _(pe):
            pe.wait_ge(filled_c, 1)
            pe.wait_ge(w_ready, 1)

            def sums_c(t):
                pe.wait_ge(c_squared, t + 1)
                if t >= 1:
                    pe.wait_ge(meaned1, t)
                for k in range(2):
                    nc.tensor.matmul(p_ss[:, 0:2], csq[:, t % 2, k], ones[:], start=k == 0, stop=k == 1)
                nc.tensor.matmul(p_ss[:, 2:4], csq[:, t % 2, 2], ones[:], start=True, stop=True)\
                    .then_inc(summed, 1)

            def up_project(t):
                pe.wait_ge(c_lo, t + 1)
                if t >= 1:
                    pe.wait_ge(up_read, t)
                for b in range(2):
                    for k in range(2):
                        s = slice(4 * QK * b, 4 * QK * (b + 1))
                        last = mm3(nc.tensor, p_up[:, b, 0:4 * QK], (ch[:, t % 2, k], cl[:, t % 2, k]),
                                   (uqs[0][:, k, s], uqs[1][:, k, s]), start=k == 0, stop=k == 1)
                last.then_inc(up, 1)
                for b in range(2):
                    s = slice(GT * b, GT * (b + 1))
                    last = mm3(nc.tensor, p_up[:, 2 + b], (ch[:, t % 2, 2], cl[:, t % 2, 2]),
                               (ukvs[0][:, s], ukvs[1][:, s]), start=True, stop=True)
                last.then_inc(up, 1)

            def turn(t):
                pe.wait_ge(roped, t + 1)
                pe.wait_ge(roped_p, t + 1)
                for b in range(NB):
                    u = NB * t + b
                    if u >= 3:
                        pe.wait_ge(t_lo, u - 2)
                    if b < 4:
                        blocks = [(QK, qk[:, t % RING, 4 * b + j]) for j in range(4)]
                    elif b == 4:
                        blocks = [(P, qb[:, t % 4, 2 * j:2 * j + 2]) for j in range(4)]
                    else:
                        x = tmb[:, t % RING]
                        blocks = [(P, qb[:, t % 4, H:H + KV]), (P, x[:, TM_QI:TM_QI + P]),
                                  (P, x[:, TM_QI + P:TM_KI]), (IDX, x[:, TM_KI:TM_WI])]
                    for j, (rows, src) in enumerate(blocks):
                        last = nc.tensor.transpose(p_t[0:rows, u % 3, j * P:(j + 1) * P], src, ident[:])
                    last.then_inc(turned, 1)

            staged([(6, turn), (1, up_project), (0, sums_c)])


class Attention:
    width = T
    ahead = 4
    lead = 8
    output_late = 2
    depth = 2

    def pe_start(self, pe): ...
    def dve_start(self, dve): ...
    def act_start(self, act): ...
    def pool_start(self, pool): ...
    def pool_unit(self, pool, n): ...
    def wait_bias(self, dve, n, s): ...
    def act_sub(self, act, n, s, shift): ...
    def add_sinks(self, dve, n, sums): ...

    def least_max(self, n, s):
        return -3e38


def schedule(units, behind, lead, output_late):
    steps, late = [], []
    blocks = 0
    for n in range(len(units) + behind):
        m = n - behind
        s_steps = []
        if n < len(units):
            for s in range(4):
                keys = units[n]["keys"][s]
                for c, k0 in enumerate(range(0, keys, GT)):
                    s_steps.append(("S", n, s, c, k0, min(GT, keys - k0), k0 + GT >= keys))
        b_steps = [("B", m, i, j, s0) for i, (j, s0) in enumerate(units[m]["blocks"])] + [("V", m)] if m >= 0 else []
        pending = []

        def take_scores():
            nonlocal pending
            step = s_steps.pop(0)
            steps.append(step)
            steps.extend(pending)
            pending = [("E", n, step[2])] if step[6] else []

        for _ in range(min(lead, len(s_steps))):
            take_scores()
        total, rest = len(b_steps), len(s_steps)
        for x in range(total):
            steps.append(b_steps[x])
            blocks += steps[-1][0] == "B"
            while late and late[0][1] <= blocks:
                steps.append(("O", late.pop(0)[0]))
            while s_steps and (rest - len(s_steps)) * total < (x + 1) * rest:
                take_scores()
        while s_steps:
            take_scores()
        steps += pending
        if m >= 0:
            late.append((m, blocks + output_late))
    return steps + [("O", n) for n, _ in late]


def stage_attention(nc, sem, tag, ident, layer):
    units = layer.units
    R = layer.depth
    steps = schedule(units, R - 1, layer.lead, layer.output_late)
    n_b = [sum(len(u["blocks"]) for u in units[:n]) for n in range(len(units) + 1)]
    ring = lambda n, place: (n_b[n] + n + place) % 3
    n_sub = lambda n, s: 4 * n + s
    with ExitStack() as c:
        sb = lambda n, s, d=F32: c.enter_context(nc.sbuf_tensor(f"{tag}_{n}", s, d))
        probs = sb("probs", [P, R, 4, layer.width])
        maxes = sb("maxes", [P, R, 4, 4])
        top = sb("top", [P, R, 4])
        shift = sb("shift", [P, R, 4])
        th = sb("th", [P, 3, GT], F32R)
        tl = sb("tl", [P, 3, GT], F32R)
        sums = sb("sums", [P, R, 4])
        inv = sb("inv", [P, 2, 4])
        spread = sb("spread", [P, 2, GT])
        halves = sb("halves", [P, 2, GT])
        ot = sb("ot", [HD, 2, GT])
        p_s = c.enter_context(nc.psum_tensor(f"{tag}_p_s", [P, 3, GT], F32))
        p_t = c.enter_context(nc.psum_tensor(f"{tag}_p_t", [P, 3, GT], F32))
        p_o = c.enter_context(nc.psum_tensor(f"{tag}_p_o", [P, 2, GT], F32))
        scored, moved, shifted, exped, turned, hi_done, lo_done, multiplied, inverted, inv_turned, spread_done, weighed, out_done = (
            sem(f"{tag}_{n}") for n in ("scored", "moved", "shifted", "exped", "turned", "hi_done",
                                        "lo_done", "multiplied", "inverted", "inv_turned", "spread_done",
                                        "weighed", "out_done"))
        stored = sem(f"{tag}_stored", 2)
        n_s = [sum(-(-k // GT) for u in units[:n] for k in u["keys"]) for n in range(len(units) + 1)]
        layer.setup(nc, sem, ident, c, dict(exped=exped, inverted=inverted, multiplied=multiplied, moved=moved,
                                            lo_done=lo_done, n_b=n_b, n_s=n_s))
        block = c.enter_context(nc.Block())

        @block.sync
        def _(sp):
            ahead = layer.ahead
            for n in range(ahead):
                layer.load(sp, n)
            for n in range(len(units)):
                if n + ahead < len(units):
                    layer.load(sp, n + ahead)
                if n >= 1:
                    sp.wait_ge(out_done, n)
                    sp.dma_start(layer.store(n - 1), ot[:, (n - 1) % 2]).then_inc(stored[(n - 1) % 2], 16)
            n = len(units) - 1
            sp.wait_ge(out_done, n + 1)
            sp.dma_start(layer.store(n), ot[:, n % 2]).then_inc(stored[n % 2], 16)
            for p in range(2):
                sp.wait_ge(stored[p], 16 * len(range(p, len(units), 2)))

        @block.tensor
        def _(pe):
            layer.pe_start(pe)
            i = 0
            behind = []

            def multiply():
                n, place, j, s0 = behind.pop(0)
                b = n_b[n] + place
                if place == 0:
                    layer.wait_values(pe, n)
                    if n >= 2:
                        pe.wait_ge(weighed, n - 1)
                pe.wait_ge(hi_done, b + 1)
                out = p_o[:, n % 2, s0 * P:GT]
                v = layer.values(n, j)
                nc.tensor.matmul(out, v, th[:, b % 3, s0 * P:GT], start=place == 0, stop=False)
                pe.wait_ge(lo_done, b + 1)
                nc.tensor.matmul(out, v, tl[:, b % 3, s0 * P:GT], start=False,
                                 stop=place == len(units[n]["blocks"]) - 1).then_inc(multiplied, 1)

            def wait_bank(n, place):
                r = n_b[n] + n + place - 3
                if r < 0:
                    return
                m = max(x for x in range(n + 1) if n_b[x] + x <= r)
                if r - n_b[m] - m == len(units[m]["blocks"]):
                    pe.wait_ge(spread_done, m + 1)
                else:
                    pe.wait_ge(lo_done, r - m + 1)

            for step in steps:
                if step[0] == "S":
                    _, n, s, ch, k0, w, last = step
                    if s == 0 and ch == 0:
                        layer.wait_scores(pe, n)
                    if i >= 3:
                        pe.wait_ge(moved, i - 2)
                    layer.scores(p_s[:, i % 3, 0:w], n, s, k0, w).then_inc(scored, 1)
                    i += 1
                elif step[0] == "B":
                    _, n, place, j, s0 = step
                    if place == 0:
                        pe.wait_ge(exped, n_sub(n, 3) + 1)
                    wait_bank(n, place)
                    for s in range(s0, 4):
                        last = nc.tensor.transpose(p_t[:, ring(n, place), s * P:(s + 1) * P],
                                                   probs[:, n % R, s, j * P:(j + 1) * P], ident[:])
                    last.then_inc(turned, 1)
                    behind.append((n, place, j, s0))
                    if len(behind) > 2:
                        multiply()
                elif step[0] == "V":
                    n = step[1]
                    place = len(units[n]["blocks"])
                    wait_bank(n, place)
                    pe.wait_ge(inverted, n + 1)
                    for s in range(4):
                        last = nc.tensor.transpose(p_t[:, ring(n, place), s * P:(s + 1) * P],
                                                   inv[:, n % 2, s:s + 1].broadcast_to([P, P]), ident[:])
                    last.then_inc(inv_turned, 1)
            while behind:
                multiply()

        @block.vector
        def _(dve):
            layer.dve_start(dve)
            i = 0
            for step in steps:
                if step[0] == "S":
                    _, n, s, ch, k0, w, last = step
                    if ch == 0:
                        layer.wait_bias(dve, n, s)
                        if n >= R and s == 0:
                            dve.wait_ge(turned, n_b[n - R + 1])
                    dve.wait_ge(scored, i + 1)
                    nc.vector.tensor_tensor_reduce(
                        out=probs[:, n % R, s, k0:k0 + w], in0=p_s[:, i % 3, 0:w],
                        in1=layer.bias(n, s, k0, w), scale=1.0, scalar=layer.least_max(n, s),
                        op0=ALU.add, op1=ALU.max, accum_out=maxes[:, n % R, s, ch:ch + 1]).then_inc(moved, 1)
                    i += 1
                    if last:
                        m = maxes[:, n % R, s, 0:1]
                        dve.wait_ge(moved, i)
                        if ch > 0:
                            m = top[:, n % R, s:s + 1]
                            nc.vector.tensor_reduce(m, maxes[:, n % R, s, 0:ch + 1], AX.X, ALU.max)
                            dve.drain()
                        if n >= R:
                            dve.wait_ge(exped, n_sub(n - R, s) + 1)
                        nc.vector.tensor_scalar(shift[:, n % R, s:s + 1], m, -layer.scale, None,
                                                ALU.mult).then_inc(shifted, 1)
                elif step[0] == "B":
                    _, n, place, j, s0 = step
                    b = n_b[n] + place
                    if b >= 3:
                        dve.wait_ge(multiplied, b - 2)
                    dve.wait_ge(hi_done, b + 1)
                    nc.vector.tensor_tensor(tl[:, b % 3, s0 * P:GT], p_t[:, ring(n, place), s0 * P:GT],
                                            th[:, b % 3, s0 * P:GT].bitcast(F32),
                                            ALU.subtract).then_inc(lo_done, 1)
                    if place == 0:
                        dve.wait_ge(exped, n_sub(n, 3) + 1)
                        layer.add_sinks(dve, n, sums[:, n % R])
                        if n >= 2:
                            dve.wait_ge(inv_turned, n - 1)
                        nc.vector.reciprocal(inv[:, n % 2], sums[:, n % R]).then_inc(inverted, 1)
                elif step[0] == "O":
                    n = step[1]
                    dve.wait_ge(multiplied, n_b[n + 1])
                    dve.wait_ge(spread_done, n + 1)
                    if n >= 2:
                        dve.wait_ge(out_done, n - 1)
                    nc.vector.tensor_tensor(halves[:, n % 2], p_o[:, n % 2], spread[:, n % 2],
                                            ALU.mult).then_inc(weighed, 1)
                    dve.wait_ge(weighed, n + 1)
                    if n >= 2:
                        dve.wait_ge(stored[n % 2], 16 * (n // 2))
                    nc.vector.tensor_tensor(ot[:, n % 2], halves[0:HD, n % 2], halves[HD:P, n % 2],
                                            ALU.add).then_inc(out_done, 1)
                    dve.drain()

        @block.scalar
        def _(act):
            layer.act_start(act)
            for step in steps:
                if step[0] == "E":
                    _, n, s = step
                    act.wait_ge(shifted, n_sub(n, s) + 1)
                    x = probs[:, n % R, s, 0:units[n]["keys"][s]]
                    layer.act_sub(act, n, s, shift[:, n % R, s:s + 1])
                    if n >= R and s == 0:
                        act.wait_ge(inverted, n - R + 1)
                    nc.scalar.activation(x, x, ACT.Exp, bias=shift[:, n % R, s:s + 1], scale=layer.scale,
                                         accum_out=sums[:, n % R, s:s + 1]).then_inc(exped, 1)
                elif step[0] == "B":
                    _, n, place, j, s0 = step
                    b = n_b[n] + place
                    act.wait_ge(turned, b + 1)
                    if b >= 3:
                        act.wait_ge(multiplied, b - 2)
                    nc.scalar.activation(th[:, b % 3, s0 * P:GT], p_t[:, ring(n, place), s0 * P:GT],
                                         ACT.Copy).then_inc(hi_done, 1)
                elif step[0] == "V":
                    n = step[1]
                    act.wait_ge(inv_turned, n + 1)
                    if n >= 2:
                        act.wait_ge(weighed, n - 1)
                    nc.scalar.activation(spread[:, n % 2], p_t[:, ring(n, len(units[n]["blocks"]))],
                                         ACT.Copy).then_inc(spread_done, 1)

        @block.gpsimd
        def _(pool):
            layer.pool_start(pool)
            for n in range(len(units)):
                layer.pool_unit(pool, n)


class Mla(Attention):
    scale = QK ** -0.5

    def __init__(self, qkT, va, oT):
        self.qkT, self.va, self.oT = qkT, va, oT
        self.of = [(h, NG - 1 - g if h % 2 else g) for h in range(H) for g in range(NG)]
        self.units = [dict(keys=[P * (NG * g + s + 1) for s in range(4)],
                           blocks=[(j, max(0, j - 4 * g)) for j in range(4 * g + 4)])
                      for _, g in self.of]

    def setup(self, nc, sem, ident, ctx, sems):
        sb = lambda n, s, d=F32: ctx.enter_context(nc.sbuf_tensor(f"mla_{n}", s, d))
        self.nc, self.sems = nc, sems
        self.q = [sb(f"q_{n}", [QK, 2, T], F32R) for n in ("hi", "lo")]
        self.k = [sb(f"k_{n}", [QK, 2, T], F32R) for n in ("hi", "lo")]
        self.v = sb("v", [P, 2, NT, P], F32R)
        self.none = sb("none", [P, GT])
        self.causal = sb("causal", [P, GT])
        self.qk_in, self.v_in = sem("mla_qk_in", 2), sem("mla_v_in", 2)
        self.bias_made = sem("mla_bias_made")

    def pool_start(self, pool):
        g = self.nc.gpsimd
        g.memset(self.none[:], 0.0)
        g.memset(self.causal[:], 0.0)
        pool.drain()
        g.affine_select(out=self.causal[:, GT - P:GT], in_=self.causal[:, GT - P:GT],
                        compare_op=ALU.is_ge, fill=NEG, base=0, pattern=[[-1, P]],
                        channel_multiplier=1).then_inc(self.bias_made, 1)

    def dve_start(self, dve):
        dve.wait_ge(self.bias_made, 1)

    def load(self, sp, n):
        h = n // NG
        if n % NG:
            return
        p = h % 2
        if h >= 2:
            sp.wait_ge(self.sems["multiplied"], self.sems["n_b"][NG * (h - 1)])
        for half in range(2):
            sp.dma_start(self.q[half][:, p].bitcast(F32), self.qkT[half, h]).then_inc(self.qk_in[p], 16)
            sp.dma_start(self.k[half][:, p].bitcast(F32), self.qkT[half, H + h]).then_inc(self.qk_in[p], 16)
        for half in range(2):
            sp.dma_start(self.v[:, p, :, half * HD:(half + 1) * HD].bitcast(F32),
                         self.va[half, :, h * HD:(h + 1) * HD].rearrange("(j p) d -> p j d", p=P))\
                .then_inc(self.v_in[p], 16)

    def wait_scores(self, pe, n):
        pe.wait_ge(self.qk_in[n // NG % 2], 64 * (n // NG // 2 + 1))

    def wait_values(self, pe, n):
        pe.wait_ge(self.v_in[n // NG % 2], 32 * (n // NG // 2 + 1))

    def scores(self, out, n, s, k0, w):
        p, t = n // NG % 2, self.of[n][1] * 4 + s
        q = [x[:, p, t * P:(t + 1) * P] for x in self.q]
        k = [x[:, p, k0:k0 + w] for x in self.k]
        return mm3(self.nc.tensor, out, q, k, start=True, stop=True)

    def bias(self, n, s, k0, w):
        if k0 + w == self.units[n]["keys"][s]:
            return self.causal[:, GT - w:GT]
        return self.none[:, 0:w]

    def values(self, n, j):
        return self.v[:, n // NG % 2, j]

    def store(self, n):
        h, g = self.of[n]
        return self.oT[h * HD:(h + 1) * HD, g * GT:(g + 1) * GT]

SENTINEL = -3.2e38
FUTURE = -3e38
HALVINGS = 10
WIDE = 2 * GT




def gate_chunks():
    return [(c0 + P * j, row + P * j, func, j if biased else None)
            for c0, row, func, count, biased in ((C_GA, 0, ACT.Silu, 4, False), (C_GB, 512, ACT.Silu, 4, False),
                                                 (C_MA, 1024, ACT.Sigmoid, 16, True))
            for j in range(count)]


def index_steps(tiles, chunks):
    total = NG * len(gate_chunks()) * KD
    keys = lambda t: P * (t + 1)
    late = tiles[2:]
    paired = sum(H * len(chunks(t)) for t in late)
    cost = {t: 11 * keys(t) / 960 + 14 for t in late}
    steps, given, u = [("W", 0), ("W", 1)], 0, 0

    def give(count):
        nonlocal given
        for _ in range(min(count, total - given)):
            step, k = divmod(given, KD)
            steps.append(("G", step, k))
            given += 1
            if k == KD - 1 and step % NG == 0:
                n = step // NG + 1
                if 2 <= n < len(gate_chunks()):
                    steps.append(("W", n))

    whole, passed = sum(cost.values()), 0
    for t in tiles:
        for h in range(H):
            for k0, width in chunks(t):
                steps.append(("I", t, h, k0, width))
                if t in cost:
                    give(1)
        steps.append(("M", t))
        for i in range(HALVINGS):
            if t in cost:
                passed += cost[t] / HALVINGS
                seen = sum(H * len(chunks(x)) for x in late if x <= t)
                give(seen + int((total - paired) * passed / whole + 0.5) - given)
            steps.append(("H", t, i))
        steps.append(("T", t))
    give(total)
    return steps


def stage_index(nc, sem, ident, qiT, kiT, wi, mask, h_dram, w_in, b_merge, gates):
    with ExitStack() as c:
        sb = lambda n, s, d=F32: c.enter_context(nc.sbuf_tensor(f"i_{n}", s, d))
        hT = [sb(f"hT_{n}", [P, KD, T], F32R) for n in ("hi", "lo")]
        ws = sb("ws", [P, KD, P])
        wh = sb("wh", [P, 2, KD, P], F32R)
        wl = sb("wl", [P, 2, KD, P], F32R)
        ob = sb("ob", [P, 2, GT])
        bias_m = sb("bias_m", [P, 16])
        q = sb("q", [P, 2, H, P], F32R)
        k = sb("k", [P, T], F32R)
        w = sb("w", [P, NT, H])
        relu = sb("relu", [P, 3, WIDE])
        score = sb("score", [P, 2, T + 8])
        above = sb("above", [P, T], BF16)
        bias = sb("bias", [P, T], BF16)
        halves = sb("halves", [P, HALVINGS + 1])
        steps8 = sb("steps8", [P, 8])
        lim = sb("lim", [P, 2])
        rng = sb("rng", [P, 1])
        mid = sb("mid", [P, 1])
        widths = sb("widths", [P, HALVINGS + 1])
        count = sb("count", [P, 1])
        side = sb("side", [P, 1])
        few = sb("few", [P, 1])
        off = sb("off", [P, 1])
        left = sb("left", [P, 1])
        rounds = sb("rounds", [1, 1])
        rounds_i = sb("rounds_i", [1, 1], I32)
        best = sb("best", [P, 8])
        taken = sb("taken", [P, 8])
        gone = sb("gone", [P, 8])
        p_s = c.enter_context(nc.psum_tensor("i_p_s", [P, 2, WIDE], F32))
        p_l = c.enter_context(nc.psum_tensor("i_p_l", [P, GT], F32))
        p_g = c.enter_context(nc.psum_tensor("i_p_g", [P, 3, GT], F32))
        k_in, stored, bias_in, w_loaded, w_hi, w_split, filled, evacuated = (
            sem(f"i_{n}") for n in ("k_in", "stored", "bias_in", "w_loaded", "w_hi", "w_split", "filled",
                                    "evacuated"))
        q_in, h_in, g_stored = sem("i_q_in", 2), sem("i_h_in", NG), sem("i_g_stored", 2)
        consts, scored, relued, summed, masked, counted, turned, made, fixed = (
            sem(f"i_{n}") for n in ("consts", "scored", "relued", "summed", "masked", "counted", "turned",
                                    "made", "fixed"))
        block = c.enter_context(nc.Block())

        def chunks(t):
            keys = P * (t + 1)
            return [(k0, min(WIDE, keys - k0)) for k0 in range(0, keys, WIDE)]

        tiles = range(TOPK // P, NT)
        steps = index_steps(tiles, chunks)
        wanted = gate_chunks()
        n_at, n = {}, 0
        for t in tiles:
            n_at[t] = n
            n += H * len(chunks(t))
        n_at[NT] = n

        @block.sync
        def _(sp):
            def load(n):
                if n >= 1:
                    sp.wait_ge(w_split, n)
                c0 = wanted[n][0]
                sp.dma_start(ws[:], w_in[:, c0:c0 + P].rearrange("(k p) n -> p k n", p=P)).then_inc(w_loaded, 16)

            load(0)
            sp.dma_start(bias_m[:], b_merge.rearrange("(j p) -> p j", p=P),
                         allow_slow_non_contiguous=True).then_inc(bias_in, 16)
            for g in range(NG):
                s = slice(g * GT, (g + 1) * GT)
                for half in range(2):
                    sp.dma_start(hT[half][:, :, s].bitcast(F32), h_dram[half, :, :, s]).then_inc(h_in[g], 16)
                if g == 0:
                    load(1)
            for u in range(NG * len(wanted)):
                n, g = divmod(u, NG)
                if g == 0 and 1 <= n < len(wanted) - 1:
                    load(n + 1)
                row = wanted[n][1]
                sp.wait_ge(evacuated, u + 1)
                sp.dma_start(gates[row:row + P, g * GT:(g + 1) * GT], ob[:, u % 2]).then_inc(g_stored[u % 2], 16)
            for p in range(2):
                sp.wait_ge(g_stored[p], 16 * (NG * len(wanted) // 2))

        @block.tensor
        def _(pe):
            pe.wait_ge(k_in, 80)
            n = 0
            for step in steps:
                if step[0] == "I":
                    _, t, h, k0, width = step
                    if h == 0 and k0 == 0:
                        pe.wait_ge(q_in[t % 2], 64 * ((t - tiles[0]) // 2 + 1))
                    if n >= 2:
                        pe.wait_ge(relued, n - 1)
                    for x in range(0, width, GT):
                        y = min(GT, width - x)
                        last = nc.tensor.matmul(p_s[:, n % 2, x:x + y], q[:, t % 2, h],
                                                k[:, k0 + x:k0 + x + y], start=True, stop=True)
                    last.then_inc(scored, 1)
                    n += 1
                elif step[0] == "T":
                    pe.wait_ge(counted, step[1] - tiles[0] + 1)
                    nc.tensor.transpose(p_l[0:1, 0:P], left[:], ident[:]).then_inc(turned, 1)
                elif step[0] == "G":
                    _, u, b = step
                    chunk, g = divmod(u, NG)
                    if b == 0:
                        pe.wait_ge(w_split, chunk + 1)
                        pe.wait_ge(h_in[g], 32)
                        if u >= 3:
                            pe.wait_ge(evacuated, u - 2)
                    s = slice(g * GT, (g + 1) * GT)
                    last = mm3(nc.tensor, p_g[:, u % 3], (wh[:, chunk % 2, b], wl[:, chunk % 2, b]),
                               [x[:, b, s] for x in hT], start=b == 0, stop=b == KD - 1)
                    if b == KD - 1:
                        last.then_inc(filled, 1)

        @block.scalar
        def _(act):
            act.wait_ge(bias_in, 16)
            n = 0
            for step in steps:
                if step[0] == "I":
                    width = step[4]
                    act.wait_ge(scored, n + 1)
                    if n >= 3:
                        act.wait_ge(summed, n - 2)
                    nc.scalar.activation(relu[:, n % 3, 0:width], p_s[:, n % 2, 0:width],
                                         ACT.Relu).then_inc(relued, 1)
                    n += 1
                elif step[0] == "W":
                    chunk = step[1]
                    act.wait_ge(w_loaded, 16 * (chunk + 1))
                    if chunk >= 2:
                        act.wait_ge(filled, NG * (chunk - 1))
                    nc.scalar.activation(wh[:, chunk % 2], ws[:], ACT.Copy).then_inc(w_hi, 1)
                elif step[0] == "G" and step[2] == KD - 1:
                    u = step[1]
                    _, _, func, bias_col = wanted[u // NG]
                    act.wait_ge(filled, u + 1)
                    if u >= 2:
                        act.wait_ge(g_stored[u % 2], 16 * (u // 2))
                    if bias_col is None:
                        nc.scalar.activation(ob[:, u % 2], p_g[:, u % 3], func).then_inc(evacuated, 1)
                    else:
                        nc.scalar.activation(ob[:, u % 2], p_g[:, u % 3], func,
                                             bias=bias_m[:, bias_col:bias_col + 1]).then_inc(evacuated, 1)

        @block.gpsimd
        def _(pool):
            def load(t):
                for r in range(4):
                    src = qiT[r // 2].rearrange("j (r d) t -> d (j r) t", d=IDX)
                    pool.dma_start(q[IDX * r:IDX * (r + 1), t % 2].bitcast(F32),
                                   src[:, :, t * P:(t + 1) * P]).then_inc(q_in[t % 2], 16)

            load(tiles[0])
            pool.dma_start(w[:], wi.rearrange("(t p) h -> p t h", p=P)).then_inc(k_in, 16)
            for r in range(4):
                pool.dma_start(k[IDX * r:IDX * (r + 1)].bitcast(F32), kiT[r % 2]).then_inc(k_in, 16)
            load(tiles[1])
            nc.gpsimd.iota(steps8[:], pattern=[[1, 8]], base=0, channel_multiplier=0,
                           allow_small_or_imprecise_dtypes=True).then_inc(consts, 1)
            for t in range(NT):
                keys = P * (t + 1)
                if t in n_at:
                    pool.wait_ge(summed, n_at[t + 1])
                    d = score[:, t % 2, keys - P:keys]
                    nc.gpsimd.affine_select(out=d, in_=d, compare_op=ALU.is_ge, fill=FUTURE, base=0,
                                            pattern=[[-1, P]], channel_multiplier=1).then_inc(masked, 1)
                    if t + 2 < NT:
                        load(t + 2)
                    pool.wait_ge(made, t - tiles[0] + 1)
                else:
                    if t >= 1:
                        pool.wait_ge(stored, 16 * t)
                    nc.gpsimd.memset(bias[:, 0:keys], 0.0)
                    pool.drain()
                d = bias[:, keys - P:keys]
                nc.gpsimd.affine_select(out=d, in_=d, compare_op=ALU.is_ge, fill=NEG, base=0,
                                        pattern=[[-1, P]], channel_multiplier=1).then_inc(fixed, 1)
                pool.wait_ge(fixed, t + 1)
                pool.dma_start(mask[t * P:(t + 1) * P, 0:keys], bias[:, 0:keys]).then_inc(stored, 16)
            pool.wait_ge(stored, 16 * NT)

        @block.vector
        def _(dve):
            for i in range(HALVINGS + 1):
                nc.vector.memset(halves[:, i:i + 1], 2.0 ** -(i + 1))
            dve.wait_ge(k_in, 80)
            dve.wait_ge(consts, 1)
            n = 0
            for step in steps:
                if step[0] == "W":
                    chunk = step[1]
                    dve.wait_ge(w_hi, chunk + 1)
                    nc.vector.tensor_tensor(wl[:, chunk % 2], ws[:], wh[:, chunk % 2].bitcast(F32),
                                            ALU.subtract).then_inc(w_split, 1)
                    continue
                if step[0] == "G":
                    continue
                t = step[1]
                keys = P * (t + 1)
                s = score[:, t % 2, 0:keys]
                if step[0] == "I":
                    _, _, h, k0, width = step
                    dve.wait_ge(relued, n + 1)
                    r, acc = relu[:, n % 3, 0:width], score[:, t % 2, k0:k0 + width]
                    if h == 0:
                        nc.vector.tensor_scalar(acc, r, w[:, t, 0:1], None, ALU.mult).then_inc(summed, 1)
                    else:
                        dve.wait_ge(summed, n + 1 - len(chunks(t)))
                        nc.vector.scalar_tensor_tensor(out=acc, in0=r, scalar=w[:, t, h:h + 1], in1=acc,
                                                       op0=ALU.mult, op1=ALU.add).then_inc(summed, 1)
                    n += 1
                elif step[0] == "M":
                    dve.wait_ge(masked, t - tiles[0] + 1)
                    sample = score[:, t % 2, 0:keys - P:(keys - P) // 256]
                    nc.vector.tensor_reduce(lim[:, 0:1], sample, AX.X, ALU.max)
                    nc.vector.tensor_reduce(lim[:, 1:2], sample, AX.X, ALU.min)
                    dve.drain()
                    nc.vector.tensor_tensor(rng[:], lim[:, 0:1], lim[:, 1:2], ALU.subtract)
                    dve.drain()
                    nc.vector.tensor_scalar(widths[:], halves[:], rng[:], 1.25, ALU.mult, ALU.mult)
                    dve.drain()
                    nc.vector.tensor_tensor(mid[:], lim[:, 0:1], widths[:, 0:1], ALU.subtract)
                    dve.drain()
                elif step[0] == "H":
                    i = step[2]
                    nc.vector.tensor_scalar(above[:, 0:keys], s, mid[:], None, ALU.is_ge, ALU.add,
                                            accum_out=count[:])
                    dve.drain()
                    nc.vector.tensor_scalar(side[:], count[:], TOPK - 0.5, 0.5, ALU.is_ge, ALU.subtract)
                    dve.drain()
                    nc.vector.scalar_tensor_tensor(out=mid[:], in0=side[:], scalar=widths[:, i:i + 1],
                                                   in1=mid[:], op0=ALU.mult, op1=ALU.add)
                    dve.drain()
                elif step[0] == "T":
                    nc.vector.tensor_tensor(mid[:], mid[:], widths[:, HALVINGS - 1:HALVINGS], ALU.add)
                    dve.drain()
                    nc.vector.tensor_scalar(above[:, 0:keys], s, mid[:], None, ALU.is_ge, ALU.add,
                                            accum_out=count[:])
                    dve.drain()
                    nc.vector.tensor_scalar(few[:], count[:], TOPK - 0.5, None, ALU.is_lt)
                    dve.drain()
                    nc.vector.tensor_scalar(off[:], few[:], NEG, None, ALU.mult)
                    nc.vector.tensor_tensor(left[:], few[:], count[:], ALU.mult)
                    dve.drain()
                    nc.vector.tensor_scalar(left[:], left[:], -1.0, float(TOPK), ALU.mult, ALU.add)\
                        .then_inc(counted, 1)
                    nc.vector.scalar_tensor_tensor(out=s, in0=above[:, 0:keys], scalar=off[:], in1=s,
                                                   op0=ALU.mult, op1=ALU.add)
                    dve.wait_ge(turned, t - tiles[0] + 1)
                    nc.vector.tensor_reduce(rounds[:], p_l[0:1, 0:P], AX.X, ALU.max)
                    dve.drain()
                    nc.vector.tensor_scalar(rounds[:], rounds[:], 3.5, 0.125, ALU.add, ALU.mult)
                    dve.drain()
                    nc.vector.tensor_scalar(rounds[:], rounds[:], ROUNDER, None, ALU.add)
                    dve.drain()
                    nc.vector.tensor_scalar(rounds[:], rounds[:], ROUNDER, None, ALU.subtract)
                    dve.drain()
                    nc.vector.tensor_copy(rounds_i[:], rounds[:])
                    dve.drain()
                    n_rounds = dve.value_load(rounds_i[0:1, 0:1], min_val=1, max_val=TOPK // 8)
                    whole = score[:, t % 2, 0:keys + 8]
                    with dve.Fori(0, n_rounds) as _i:
                        nc.vector.memset(score[:, t % 2, keys:keys + 8], SENTINEL)
                        nc.vector.max(out=best[:], in_=s)
                        nc.vector.tensor_scalar(taken[:], steps8[:], left[:], None, ALU.is_lt)
                        dve.drain()
                        nc.vector.tensor_scalar(left[:], left[:], 8.0, None, ALU.subtract)
                        nc.vector.tensor_tensor(best[:], best[:], taken[:], ALU.mult)
                        nc.vector.tensor_scalar(gone[:], taken[:], 1.0, -SENTINEL, ALU.subtract, ALU.mult)
                        dve.drain()
                        nc.vector.tensor_tensor(best[:], best[:], gone[:], ALU.add)
                        dve.drain()
                        nc.vector.match_replace(out=whole, in_to_replace=best[:], in_values=whole, imm_value=NEG)
                        dve.drain()
                    dve.wait_ge(stored, 16 * t)
                    nc.vector.tensor_scalar(bias[:, 0:keys], s, NEG / 2, NEG, ALU.is_ge,
                                            ALU.mult).then_inc(made, 1)


class Dsa(Attention):
    scale = HD ** -0.5

    def __init__(self, qbT, kbT, vb, mask, oT):
        self.qbT, self.kbT, self.vb, self.mask, self.oT = qbT, kbT, vb, mask, oT
        self.units = [dict(keys=[P * (t + 1)] * 4, blocks=[(j, 0) for j in range(t + 1)])
                      for t in range(NT) for g in range(KV)]

    def setup(self, nc, sem, ident, ctx, sems):
        sb = lambda n, s, d=F32: ctx.enter_context(nc.sbuf_tensor(f"dsa_{n}", s, d))
        self.nc, self.sems = nc, sems
        self.q = sb("q", [P, 2, H, P], F32R)
        self.k_hi = sb("k_hi", [P, KV, T], F32R)
        self.k_lo = sb("k_lo", [HD, KV, T], F32R)
        self.v = sb("v", [P, NT, KV, P], F32R)
        self.m = sb("mask", [P, 2, T], BF16)
        self.q_in, self.m_in = sem("dsa_q_in", 2), sem("dsa_m_in", 2)
        self.kv_in = sem("dsa_kv_in")

    def pe_start(self, pe):
        pe.wait_ge(self.kv_in, 16 * 7)

    def load(self, sp, n):
        t, g = n // KV, n % KV
        if g:
            return
        if t >= 2:
            sp.wait_ge(self.sems["moved"], self.sems["n_s"][KV * (t - 1)])
        at = slice(t * P, (t + 1) * P)
        for half in range(2):
            sp.dma_start(self.q[half * HD:(half + 1) * HD, t % 2].bitcast(F32),
                         self.qbT[half].rearrange("j (r d) t -> d (j r) t", d=HD)[:, :, at])\
                .then_inc(self.q_in[t % 2], 16)
        keys = P * (t + 1)
        sp.dma_start(self.m[:, t % 2, 0:keys], self.mask[at, 0:keys]).then_inc(self.m_in[t % 2], 16)
        if n == 0:
            k = [self.kbT[half].rearrange("(g d) t -> d g t", d=HD) for half in range(2)]
            for dst, src in ((self.k_hi[0:HD], k[0]), (self.k_hi[HD:P], k[0]), (self.k_lo[:], k[1])):
                sp.dma_start(dst.bitcast(F32), src).then_inc(self.kv_in, 16)
            for half in range(2):
                for g in range(KV):
                    sp.dma_start(self.v[:, :, g, half * HD:(half + 1) * HD].bitcast(F32),
                                 self.vb[half, :, g * HD:(g + 1) * HD].rearrange("(j p) d -> p j d", p=P))\
                        .then_inc(self.kv_in, 16)

    def wait_scores(self, pe, n):
        pe.wait_ge(self.q_in[n // KV % 2], 32 * (n // KV // 2 + 1))

    def wait_values(self, pe, n): ...

    def wait_bias(self, dve, n, s):
        dve.wait_ge(self.m_in[n // KV % 2], 16 * (n // KV // 2 + 1))

    def scores(self, out, n, s, k0, w):
        t, g = n // KV, n % KV
        q = self.q[:, t % 2, 4 * g + s]
        self.nc.tensor.matmul(out, q, self.k_hi[:, g, k0:k0 + w], start=True, stop=False)
        return self.nc.tensor.matmul(out, q[0:HD], self.k_lo[:, g, k0:k0 + w], start=False, stop=True)

    def bias(self, n, s, k0, w):
        return self.m[:, n // KV % 2, k0:k0 + w]

    def values(self, n, j):
        return self.v[:, j, n % KV]

    def store(self, n):
        t, g = n // KV, n % KV
        rows = self.oT[g * 4 * HD:(g + 1) * 4 * HD, t * P:(t + 1) * P]
        return rows.rearrange("(h d) t -> d h t", d=HD)


def t5_one_hot():
    out = np.zeros((32, 3 * P), np.float32)
    for dist in range(WINDOW):
        if dist < 16:
            bucket = dist
        else:
            ratio = np.log(np.float32(dist) / np.float32(16)) / np.float32(math.log(8.0))
            bucket = min(31, 16 + int(np.float32(ratio) * np.float32(16)))
        out[bucket, 2 * P - 1 - dist] = 1.0
    return out


def stage_bias(nc, sem, one_hot, table, spread):
    with ExitStack() as c:
        sb = lambda n, s: c.enter_context(nc.sbuf_tensor(f"t_{n}", s, F32))
        hot = sb("hot", [32, 3 * P])
        tab = sb("tab", [32, WH])
        row = sb("row", [WH, 3 * P])
        ps = c.enter_context(nc.psum_tensor("t_ps", [WH, 3 * P], F32))
        loaded, product, filled, stored = (sem(f"t_{n}") for n in ("loaded", "product", "filled", "stored"))
        block = c.enter_context(nc.Block())

        @block.sync
        def _(sp):
            sp.dma_start(hot[:], one_hot).then_inc(loaded, 16)
            sp.dma_start(tab[:], table).then_inc(loaded, 16)
            sp.wait_ge(filled, 2)
            sp.dma_start(spread, row[:].unsqueeze(1).broadcast_to([WH, P, 3 * P])).then_inc(stored, 16)
            sp.wait_ge(stored, 16)

        @block.tensor
        def _(pe):
            pe.wait_ge(loaded, 32)
            nc.tensor.matmul(ps[:], tab[:], hot[:], start=True, stop=True).then_inc(product, 1)

        @block.vector
        def _(dve):
            nc.vector.memset(row[:], NEG).then_inc(filled, 1)
            dve.wait_ge(filled, 1)
            dve.wait_ge(product, 1)
            nc.vector.tensor_scalar(row[:, P:2 * P], ps[:, P:2 * P], 1 / Window.scale, None,
                                    ALU.mult).then_inc(filled, 1)


class Window(Attention):
    scale = HD ** -0.5
    width = 2 * P
    depth = 3
    ahead = 6
    lead = 1

    def __init__(self, qT, kT, v, spread, sinks, oT):
        self.qT, self.kT, self.v_dram, self.spread, self.sinks, self.oT = qT, kT, v, spread, sinks, oT
        self.units = [dict(keys=[P * min(2, t + 1)] * 4, blocks=[(j, 0) for j in range(min(2, t + 1))])
                      for t in range(NT) for g in range(WKV)]

    def setup(self, nc, sem, ident, ctx, sems):
        sb = lambda n, s, d=F32: ctx.enter_context(nc.sbuf_tensor(f"win_{n}", s, d))
        self.nc, self.sems = nc, sems
        self.q_raw = sb("q_raw", [P, 2, WH, P])
        self.k_raw = sb("k_raw", [P, 2, WKV, P])
        self.v_raw = sb("v_raw", [P, 2, WKV * HD])
        self.q = sb("q", [P, 2, WH, P], F32R)
        self.k_hi = sb("k_hi", [P, WKV, 4, P], F32R)
        self.k_lo = sb("k_lo", [HD, WKV, 4, P], F32R)
        self.v = sb("v", [P, 4, WKV, P], F32R)
        self.b = sb("bias", [P, WH, 2 * P])
        self.sink8 = sb("sink8", [P, WH])
        self.e_sink = sb("e_sink", [P, self.depth, 4])
        self.tile_in = sem("win_tile_in", 2)
        self.const_in, self.sink_made, self.kv_split, self.q_hi = (
            sem(f"win_{n}") for n in ("const_in", "sink_made", "kv_split", "q_hi"))

    def load(self, sp, n):
        t, g = n // WKV, n % WKV
        if n == 0:
            sp.dma_start(self.sink8[:], self.sinks.partition_broadcast(P)).then_inc(self.const_in, 16)
            flat = self.spread.rearrange("h r u -> h (r u)")[:, P - 1:P - 1 + P * (3 * P - 1)]
            toeplitz = flat.rearrange("h (q u) -> q h u", u=3 * P - 1)[:, :, 0:2 * P]
            sp.dma_start(self.b[:], toeplitz).then_inc(self.const_in, 16)
        if g:
            return
        at = slice(t * P, (t + 1) * P)
        if t >= 2:
            sp.wait_ge(self.kv_split, t - 1)
        done = self.tile_in[t % 2]
        for rows in (slice(0, HD), slice(HD, P)):
            sp.dma_start(self.q_raw[rows, t % 2],
                         self.qT.rearrange("(h d) t -> d h t", d=HD)[:, :, at]).then_inc(done, 16)
            sp.dma_start(self.k_raw[rows, t % 2],
                         self.kT.rearrange("(h d) t -> d h t", d=HD)[:, :, at]).then_inc(done, 16)
        sp.dma_start(self.v_raw[:, t % 2], self.v_dram[at, :]).then_inc(done, 16)

    def pool_start(self, pool):
        self.split_tile(pool, 0)

    def pool_unit(self, pool, n):
        if n % WKV == 0 and n // WKV + 1 < NT:
            self.split_tile(pool, n // WKV + 1)

    def split_tile(self, pool, t):
        p, r = t % 2, t % 4
        pool.wait_ge(self.tile_in[p], 80 * (t // 2 + 1))
        if t >= 4:
            pool.wait_ge(self.sems["multiplied"], self.sems["n_b"][WKV * (t - 2)])
        v_raw = self.v_raw[:, p].rearrange("p (g d) -> p g d", d=HD)
        g = self.nc.gpsimd
        g.tensor_copy(self.k_hi[:, :, r], self.k_raw[:, p])
        g.tensor_copy(self.v[:, r, :, 0:HD], v_raw)
        pool.drain()
        g.tensor_tensor(self.k_lo[:, :, r], self.k_raw[0:HD, p], self.k_hi[0:HD, :, r].bitcast(F32),
                        ALU.subtract)
        pool.drain()
        g.tensor_tensor(self.v[:, r, :, HD:P], v_raw, self.v[:, r, :, 0:HD].bitcast(F32), ALU.subtract)
        pool.drain()
        pool.wait_ge(self.q_hi, t + 1)
        g.tensor_tensor(self.q[HD:P, p], self.q_raw[HD:P, p], self.q[HD:P, p].bitcast(F32),
                        ALU.subtract).then_inc(self.kv_split, 1)
        pool.drain()

    def dve_start(self, dve):
        dve.wait_ge(self.const_in, 32)
        self.nc.vector.tensor_scalar(self.sink8[:], self.sink8[:], 1 / self.scale, None,
                                     ALU.mult).then_inc(self.sink_made, 1)
        dve.drain()

    def act_start(self, act):
        self.round_queries(act, 0)
        act.wait_ge(self.sink_made, 1)

    def round_queries(self, act, t):
        p = t % 2
        act.wait_ge(self.tile_in[p], 80 * (t // 2 + 1))
        if t >= 2:
            act.wait_ge(self.sems["moved"], self.sems["n_s"][WKV * (t - 1)])
        self.nc.scalar.activation(self.q[:, p], self.q_raw[:, p], ACT.Copy).then_inc(self.q_hi, 1)

    def act_sub(self, act, n, s, shift):
        if n % WKV == 2 and s == 0 and n // WKV + 1 < NT:
            self.round_queries(act, n // WKV + 1)
        if n >= self.depth and s == 0:
            act.wait_ge(self.sems["inverted"], n - self.depth + 1)
        h = 4 * (n % WKV) + s
        self.nc.scalar.activation(self.e_sink[:, n % self.depth, s:s + 1], self.sink8[:, h:h + 1], ACT.Exp,
                                  bias=shift, scale=self.scale)

    def least_max(self, n, s):
        h = 4 * (n % WKV) + s
        return self.sink8[:, h:h + 1]

    def add_sinks(self, dve, n, sums):
        self.nc.vector.tensor_tensor(sums, sums, self.e_sink[:, n % self.depth], ALU.add)
        dve.drain()

    def wait_scores(self, pe, n):
        pe.wait_ge(self.kv_split, n // WKV + 1)

    def wait_values(self, pe, n): ...

    def scores(self, out, n, s, k0, w):
        t, g = n // WKV, n % WKV
        q = self.q[:, t % 2, 4 * g + s]
        first = (t - w // P + 1) % 4
        runs = [(first, w // P)] if first + w // P <= 4 else [(3, 1), (0, 1)]
        at = 0
        for r, tiles in runs:
            o = out[:, at:at + tiles * P]
            hi = self.k_hi[:, g, r:r + tiles].rearrange("p r t -> p (r t)")
            lo = self.k_lo[:, g, r:r + tiles].rearrange("p r t -> p (r t)")
            self.nc.tensor.matmul(o, q, hi, start=True, stop=False)
            last = self.nc.tensor.matmul(o, q[0:HD], lo, start=False, stop=True)
            at += tiles * P
        return last

    def bias(self, n, s, k0, w):
        return self.b[:, 4 * (n % WKV) + s, 2 * P - w:2 * P]

    def values(self, n, j):
        t, g = n // WKV, n % WKV
        return self.v[:, (t - len(self.units[n]["blocks"]) + 1 + j) % 4, g]

    def store(self, n):
        t, g = n // WKV, n % WKV
        rows = self.oT[g * 4 * HD:(g + 1) * 4 * HD, t * P:(t + 1) * P]
        return rows.rearrange("(h d) t -> d h t", d=HD)


def stage_branch(nc, sem, oaT, obT, gates, w_mla, w_dsa, mergedT):
    KO = 4
    with ExitStack() as c:
        sb = lambda n, s, d=F32: c.enter_context(nc.sbuf_tensor(f"m_{n}", s, d))
        raw = sb("raw", [P, 2, KO, D])
        w = [[sb(f"w{x}_{n}", [P, KO, D], F32R) for n in ("hi", "lo")] for x in "ab"]
        o = sb("o", [P, 2, KO, GT])
        gate = sb("gate", [P, 2, KO, GT])
        oh = sb("oh", [P, 2, KO, GT], F32R)
        ol = sb("ol", [P, 2, KO, GT], F32R)
        m = sb("m", [P, 2, 2, GT])
        part = sb("part", [P, 2, GT])
        total = sb("total", [P, 2, GT])
        ps = c.enter_context(nc.psum_tensor("m_ps", [P, 4, 2, GT], F32))
        w_in = sem("m_w_in")
        o_in, m_in, stored = sem("m_o_in", 2), sem("m_m_in", 2), sem("m_stored", 2)
        w_hi, w_lo, gated, hi_done, lo_done, filled, weighed, added = (
            sem(f"m_{n}") for n in ("w_hi", "w_lo", "gated", "hi_done", "lo_done", "filled", "weighed",
                                    "added"))
        block = c.enter_context(nc.Block())
        view = lambda x: x.rearrange("(k p) t -> p k t", p=P)
        tok = lambda g: slice(g * GT, (g + 1) * GT)

        @block.sync
        def _(sp):
            for x, src in enumerate((w_mla, w_dsa)):
                sp.dma_start(raw[:, x], view(src)).then_inc(w_in, 16)

            def load(g):
                for x, src in enumerate((oaT, obT)):
                    if g:
                        sp.wait_ge(lo_done, 2 * g - 1 + x)
                    sp.dma_start(o[:, x], view(src)[:, :, tok(g)]).then_inc(o_in[x], 16)
                    sp.dma_start(gate[:, x], view(gates[x * 512:(x + 1) * 512])[:, :, tok(g)])\
                        .then_inc(o_in[x], 16)

            def load_m(n):
                g, f = n // KD, n % KD
                if n >= 2:
                    sp.wait_ge(weighed, 2 * (n - 1))
                for x in range(2):
                    r = 1024 * (x + 1) + f * P
                    sp.dma_start(m[:, n % 2, x], gates[r:r + P, tok(g)]).then_inc(m_in[n % 2], 16)

            def store(n):
                g, f = n // KD, n % KD
                sp.wait_ge(added, n + 1)
                sp.dma_start(mergedT[f * P:(f + 1) * P, tok(g)], total[:, n % 2]).then_inc(stored[n % 2], 16)

            load(0)
            load_m(0)
            for n in range(NG * KD):
                if n % KD == 0 and n // KD + 1 < NG:
                    load(n // KD + 1)
                if n + 1 < NG * KD:
                    load_m(n + 1)
                store(n)
            for p in range(2):
                sp.wait_ge(stored[p], 16 * (NG * KD // 2))

        @block.scalar
        def _(act):
            act.wait_ge(w_in, 32)
            for x in range(2):
                nc.scalar.activation(w[x][0][:], raw[:, x], ACT.Copy).then_inc(w_hi, 1)
            for g in range(NG):
                for x in range(2):
                    act.wait_ge(gated, 2 * g + x + 1)
                    if g:
                        act.wait_ge(filled, 2 * KD * (g - 1) + 2 * KD)
                    nc.scalar.activation(oh[:, x], o[:, x], ACT.Copy).then_inc(hi_done, 1)

        @block.gpsimd
        def _(pool):
            for g in range(NG):
                for x in range(2):
                    pool.wait_ge(hi_done, 2 * g + x + 1)
                    nc.gpsimd.tensor_tensor(ol[:, x], o[:, x], oh[:, x].bitcast(F32),
                                            ALU.subtract).then_inc(lo_done, 1)

        @block.vector
        def _(dve):
            def gated_group(g):
                for x in range(2):
                    dve.wait_ge(o_in[x], 32 * (g + 1))
                    nc.vector.tensor_tensor(o[:, x], o[:, x], gate[:, x], ALU.mult).then_inc(gated, 1)

            gated_group(0)
            for x in range(2):
                dve.wait_ge(w_hi, x + 1)
                nc.vector.tensor_tensor(w[x][1][:], raw[:, x], w[x][0][:].bitcast(F32),
                                        ALU.subtract).then_inc(w_lo, 1)
            for n in range(NG * KD):
                g = n // KD
                if n % KD == 2 and g + 1 < NG:
                    gated_group(g + 1)
                dve.wait_ge(m_in[n % 2], 32 * (n // 2 + 1))
                if n:
                    dve.wait_ge(added, n)
                for x in range(2):
                    dve.wait_ge(filled, 2 * n + x + 1)
                    nc.vector.tensor_tensor(part[:, x], ps[:, n % 4, x], m[:, n % 2, x],
                                            ALU.mult).then_inc(weighed, 1)
                dve.wait_ge(weighed, 2 * n + 2)
                if n >= 2:
                    dve.wait_ge(stored[n % 2], 16 * (n // 2))
                nc.vector.tensor_tensor(total[:, n % 2], part[:, 0], part[:, 1], ALU.add).then_inc(added, 1)

        @block.tensor
        def _(pe):
            pe.wait_ge(w_lo, 2)
            for n in range(NG * KD):
                g, f = n // KD, n % KD
                if n >= 4:
                    pe.wait_ge(weighed, 2 * (n - 3))
                for x in range(2):
                    if f == 0:
                        pe.wait_ge(lo_done, 2 * g + x + 1)
                    for k in range(KO):
                        cols = slice(f * P, (f + 1) * P)
                        last = mm3(nc.tensor, ps[:, n % 4, x], [y[:, k, cols] for y in w[x]],
                                   (oh[:, x, k], ol[:, x, k]), start=k == 0, stop=k == KO - 1)
                    last.then_inc(filled, 1)


def stage_out(nc, sem, tag, actT, gateT, weight, residual, out, final_gain=None):
    GO = 2 * P
    with ExitStack() as c:
        sb = lambda n, s, d=F32: c.enter_context(nc.sbuf_tensor(f"{tag}_{n}", s, d))
        raw = sb("raw", [P, 2, D])
        w = [sb(f"w_{n}", [P, KD, D], F32R) for n in ("hi", "lo")]
        a = sb("a", [P, 2, KD, GO])
        gate = sb("gate", [P, KD, GO]) if gateT is not None else None
        ah = sb("ah", [P, 2, KD, GO], F32R)
        al = sb("al", [P, 2, KD, GO], F32R)
        x = sb("x", [P, 2, D])
        y = sb("y", [P, 2, D])
        if final_gain is not None:
            gain = sb("gain", [P, D])
            junk = sb("junk", [P, D])
            ss, ms, sd, rs = (sb(n, [P, NT]) for n in ("ss", "ms", "sd", "rs"))
        ps = c.enter_context(nc.psum_tensor(f"{tag}_ps", [P, 4, 2, GT], F32))
        w_in, a_in, x_in, stored = (sem(f"{tag}_{n}", 2) for n in ("w_in", "a_in", "x_in", "stored"))
        gate_in, gain_in, w_hi, w_lo, gated, hi_done, lo_done, filled, added, squared, meaned, rooted, done = (
            sem(f"{tag}_{n}") for n in ("gate_in", "gain_in", "w_hi", "w_lo", "gated", "hi_done", "lo_done",
                                        "filled", "added", "squared", "meaned", "rooted", "done"))
        block = c.enter_context(nc.Block())
        view = lambda z: z.rearrange("(k p) t -> p k t", p=P)
        n_groups = T // GO

        @block.sync
        def _(sp):
            def load(g):
                s = slice(g * GO, (g + 1) * GO)
                if g >= 2:
                    sp.wait_ge(lo_done, g - 1)
                sp.dma_start(a[:, g % 2], view(actT)[:, :, s]).then_inc(a_in[g % 2], 16)
                if gate is not None:
                    if g >= 1:
                        sp.wait_ge(gated, g)
                    sp.dma_start(gate[:], view(gateT)[:, :, s]).then_inc(gate_in, 16)

            def load_x(t):
                if t >= 2:
                    sp.wait_ge(added, t - 1)
                sp.dma_start(x[:, t % 2], residual[t * P:(t + 1) * P, :]).then_inc(x_in[t % 2], 16)

            load(0)
            for k in range(KD):
                if k >= 2:
                    sp.wait_ge(w_lo, k - 1)
                sp.dma_start(raw[:, k % 2], weight[k * P:(k + 1) * P, :]).then_inc(w_in[k % 2], 16)
            if final_gain is not None:
                sp.dma_start(gain[:], final_gain.partition_broadcast(P)).then_inc(gain_in, 16)
            load_x(0)
            load_x(1)
            load(1)
            for t in range(NT):
                if t % 2 == 0 and t // 2 + 2 < n_groups:
                    load(t // 2 + 2)
                sp.wait_ge(done, t + 1)
                sp.dma_start(out[t * P:(t + 1) * P, :], y[:, t % 2]).then_inc(stored[t % 2], 16)
                if t + 2 < NT:
                    load_x(t + 2)
            for p in range(2):
                sp.wait_ge(stored[p], 16 * (NT // 2))

        @block.gpsimd
        def _(pool):
            for g in range(n_groups):
                pool.wait_ge(hi_done, g + 1)
                if g >= 2:
                    pool.wait_ge(filled, 4 * (g - 1))
                nc.gpsimd.tensor_tensor(al[:, g % 2], a[:, g % 2], ah[:, g % 2].bitcast(F32),
                                        ALU.subtract).then_inc(lo_done, 1)

        @block.scalar
        def _(act):
            for k in range(KD):
                act.wait_ge(w_in[k % 2], 16 * (k // 2 + 1))
                nc.scalar.activation(w[0][:, k], raw[:, k % 2], ACT.Copy).then_inc(w_hi, 1)

            def hi(g):
                if gate is not None:
                    act.wait_ge(gated, g + 1)
                else:
                    act.wait_ge(a_in[g % 2], 16 * (g // 2 + 1))
                if g >= 2:
                    act.wait_ge(filled, 4 * (g - 1))
                nc.scalar.activation(ah[:, g % 2], a[:, g % 2], ACT.Copy).then_inc(hi_done, 1)

            hi(0)
            for t in range(NT):
                if t % 2 == 0 and t // 2 + 1 < n_groups:
                    hi(t // 2 + 1)
                if final_gain is not None:
                    act.wait_ge(added, t + 1)
                    nc.scalar.activation(junk[:], y[:, t % 2], ACT.Square,
                                         accum_out=ss[:, t:t + 1]).then_inc(squared, 1)
                    act.wait_ge(meaned, t + 1)
                    nc.scalar.activation(sd[:, t:t + 1], ms[:, t:t + 1], ACT.Sqrt).then_inc(rooted, 1)

        @block.vector
        def _(dve):
            def multiply_gate(g):
                if gate is not None:
                    dve.wait_ge(a_in[g % 2], 16 * (g // 2 + 1))
                    dve.wait_ge(gate_in, 16 * (g + 1))
                    nc.vector.tensor_tensor(a[:, g % 2], a[:, g % 2], gate[:], ALU.mult).then_inc(gated, 1)

            def finish(t):
                dve.wait_ge(squared, t + 1)
                nc.vector.tensor_scalar(ms[:, t:t + 1], ss[:, t:t + 1], 1.0 / D, EPS, ALU.mult,
                                        ALU.add).then_inc(meaned, 1)
                dve.wait_ge(rooted, t + 1)
                nc.vector.reciprocal(rs[:, t:t + 1], sd[:, t:t + 1])
                dve.drain()
                nc.vector.scalar_tensor_tensor(out=y[:, t % 2], in0=y[:, t % 2], scalar=rs[:, t:t + 1],
                                               in1=gain[:], op0=ALU.mult, op1=ALU.mult).then_inc(done, 1)

            multiply_gate(0)
            for k in range(KD):
                dve.wait_ge(w_hi, k + 1)
                nc.vector.tensor_tensor(w[1][:, k], raw[:, k % 2], w[0][:, k].bitcast(F32),
                                        ALU.subtract).then_inc(w_lo, 1)
            if final_gain is not None:
                dve.wait_ge(gain_in, 16)
            for t in range(NT):
                if t % 2 == 0 and t // 2 + 1 < n_groups:
                    multiply_gate(t // 2 + 1)
                dve.wait_ge(x_in[t % 2], 16 * (t // 2 + 1))
                if t >= 2:
                    dve.wait_ge(stored[t % 2], 16 * (t // 2))
                dve.wait_ge(filled, 2 * t + 2)
                last = nc.vector.tensor_tensor(y[:, t % 2], ps[:, t % 4].rearrange("p a b -> p (a b)"),
                                               x[:, t % 2], ALU.add)
                last.then_inc(added, 1)
                if final_gain is None:
                    dve.wait_ge(added, t + 1)
                    dve.sem_inc(done, 1)
                elif t >= 1:
                    finish(t - 1)
            if final_gain is not None:
                finish(NT - 1)

        @block.tensor
        def _(pe):
            pe.wait_ge(w_lo, KD)
            for t in range(NT):
                g, s = t // 2 % 2, slice(t % 2 * P, (t % 2 + 1) * P)
                pe.wait_ge(lo_done, t // 2 + 1)
                if t >= 4:
                    pe.wait_ge(added, t - 3)
                for b in range(2):
                    cols = slice(b * GT, (b + 1) * GT)
                    for k in range(KD):
                        last = mm3(nc.tensor, ps[:, t % 4, b], (ah[:, g, k, s], al[:, g, k, s]),
                                   [z[:, k, cols] for z in w], start=k == 0, stop=k == KD - 1)
                    last.then_inc(filled, 1)


def fm_run(count, column, dst, row, func=ACT.Copy):
    return Run("fm", count, lambda j: [(0, column + P * j, P)],
               lambda j, g: dst[bass.ds(row + P * j, P), g * GT:(g + 1) * GT], func)


def first_layer_runs(cqT, tm):
    tm_parts = [[(0, C_PE, 32), (32, C_QB, 242)], [(0, C_QB + 242, 274)],
                [(0, C_QB + 516, 252), (252, C_QI, 22)], [(0, C_QI + 22, 274)]]
    return [Run("tm", 4, lambda j: tm_parts[j],
                lambda j, t: tm[t * P:(t + 1) * P, j * TM_CHUNK:(j + 1) * TM_CHUNK]),
            fm_run(3, C_Q, cqT, 0)]


def second_layer_runs(qT, kT, v, zT):
    nq, nkv = WH * HD, WKV * HD
    return [Run("tm", 1, lambda j: [(0, nq + nkv, nkv)], lambda j, t: v[t * P:(t + 1) * P, :]),
            fm_run(2, 0, qT, 0),
            fm_run(6, 2 * P, qT, 2 * P),
            fm_run(2, nq, kT, 0),
            fm_run(8, nq + 2 * nkv, zT, 0, ACT.Silu)]


def make_ident(nc, sem, ident):
    made = sem("ident_made")
    with nc.Block() as block:
        @block.gpsimd
        def _(pool):
            nc.gpsimd.memset(ident[:], 0.0).then_inc(made, 1)
            pool.wait_ge(made, 1)
            nc.gpsimd.affine_select(out=ident[:], in_=ident[:], compare_op=ALU.not_equal, fill=1.0,
                                    base=0, pattern=[[-1, P]], channel_multiplier=1).then_inc(made, 1)


def program(nc, a, out):
    with ExitStack() as c:
        sem = Sems(nc)
        dram = lambda n, *s, d=F32: nc.dram_tensor(f"scratch_{n}", s, d).ap()
        cqT, tm, gates = dram("cqT", 384, T), dram("tm", T, TM_W), dram("gates", 3072, T)
        qkT, va = dram("qkT", 2, 2 * H, QK, T), dram("va", 2, T, H * HD)
        qbT, kbT, vb = dram("qbT", 2, 4, P, T), dram("kbT", 2, P, T), dram("vb", 2, T, P)
        qiT, kiT, wi = dram("qiT", 2, 2, P, T), dram("kiT", 2, IDX, T), dram("wi", T, H)
        h_dram = dram("h", 2, P, KD, T)
        mask = dram("mask", T, T, d=BF16)
        oaT, obT, mergedT = dram("oaT", H * HD, T), dram("obT", H * HD, T), dram("mergedT", D, T)
        x1 = dram("x1", T, D)
        q2T, k2T, v2 = dram("q2T", WH * HD, T), dram("k2T", WKV * HD, T), dram("v2", T, WKV * HD)
        z2T, o2T = dram("z2T", WH * HD, T), dram("o2T", WH * HD, T)
        spread = dram("spread", WH, P, 3 * P)
        ident = c.enter_context(nc.sbuf_tensor("ident", [P, P], F32))
        make_ident(nc, sem, ident)
        sem.end_stage()

        with ExitStack() as c1:
            hT = [c1.enter_context(nc.sbuf_tensor(f"h1T_{n}", [P, KD, T], F32R)) for n in ("hi", "lo")]
            stage_norm(nc, sem, "n1", a["x"][0], a["norm_gain"][0], ident, hT)
            sem.end_stage()
            stage_project(nc, sem, "p1", hT, a["w_in"][0], TM_CHUNK, first_layer_runs(cqT, tm), h_dram)
            sem.end_stage()
        stage_qkv(nc, sem, ident, a, cqT, tm, qkT, qbT, kbT, qiT, kiT, va, vb, wi)
        sem.end_stage()
        stage_attention(nc, sem, "mla", ident, Mla(qkT, va, oaT))
        sem.end_stage()
        stage_index(nc, sem, ident, qiT, kiT, wi, mask, h_dram, a["w_in"][0],
                    a["b_merge"][0].rearrange("a n -> (a n)"), gates)
        sem.end_stage()
        stage_attention(nc, sem, "dsa", ident, Dsa(qbT, kbT, vb, mask, obT))
        sem.end_stage()
        stage_branch(nc, sem, oaT, obT, gates, a["w_branch_mla"][0], a["w_branch_dsa"][0], mergedT)
        sem.end_stage()
        stage_out(nc, sem, "o1", mergedT, None, a["w_out"][0], a["x"][0], x1)
        sem.end_stage()

        with ExitStack() as c1:
            hT = [c1.enter_context(nc.sbuf_tensor(f"h2T_{n}", [P, KD, T], F32R)) for n in ("hi", "lo")]
            stage_norm(nc, sem, "n2", x1, a["norm_g_2"][0], ident, hT)
            sem.end_stage()
            stage_project(nc, sem, "p2", hT, a["a_w_in_2"][0], WKV * HD,
                          second_layer_runs(q2T, k2T, v2, z2T))
            sem.end_stage()
        stage_bias(nc, sem, a["one_hot"], a["t5_table_2"], spread)
        sem.end_stage()
        stage_attention(nc, sem, "win", ident, Window(q2T, k2T, v2, spread, a["a_sinks_2"][0], o2T))
        sem.end_stage()
        stage_out(nc, sem, "o2", o2T, z2T, a["a_w_out_2"][0], x1, out[0], a["final_g_2"])
        sem.end_stage()


_INS = ["x", "positions", "norm_gain", "w_in", "b_merge", "mla_q_norm", "mla_w_uq", "mla_kv_norm",
        "mla_w_ukv", "mla_q_gain", "mla_k_gain", "dsa_q_gain", "dsa_k_gain", "w_branch_mla",
        "w_branch_dsa", "w_out", "t5_table_2", "norm_g_2", "final_g_2", "a_w_in_2", "a_sinks_2",
        "a_w_out_2"]


def kernel(**inputs):
    import concourse.bacc as bacc
    from concourse.bass_utils import run_bass_kernel_spmd

    nc = bacc.Bacc("TRN2", target_bir_lowering=False, num_devices=1)
    given = {name: np.ascontiguousarray(inputs[name]) for name in _INS}
    given["one_hot"] = t5_one_hot()
    arrays, aps = {}, {}
    for name, x in given.items():
        arrays[f"in_{name}"] = x
        aps[name] = nc.dram_tensor(f"in_{name}", x.shape, mybir.dt.from_np(x.dtype), kind="ExternalInput").ap()
    out = nc.dram_tensor("out_x", (1, T, D), F32, kind="ExternalOutput").ap()
    program(nc, aps, out)
    r = run_bass_kernel_spmd(nc, [arrays], core_ids=[0])
    return r.results[0]["out_x"]
```

```python
import math
from contextlib import ExitStack

import numpy as np
import concourse.bass as bass
from concourse import mybir
from concourse.alu_op_type import AluOpType as ALU

F32 = mybir.dt.float32
F32R = mybir.dt.float32r
BF16 = mybir.dt.bfloat16
I32 = mybir.dt.int32
ACT = mybir.ActivationFunctionType
AX = mybir.AxisListType

P = 128
T = 2048
NT = T // P
D = 1024
KD = D // P
GT = 512
NG = T // GT
EPS = 1e-6

H = 8
QK, NOPE, ROPE_M = 96, 64, 32
HD = 64
KV = 2
IDX = 32
TOPK = min(256, T // 4)
ROT_D, ROT_I = 16, 8
THETA = 500000.0

SPLITS = [256, 128, 32, 512, 512, 128, 128, 512, 256, 32, 8, 1024, 1024]
(C_Q, C_KV, C_PE, C_GA, C_QB, C_KB, C_VB, C_GB, C_QI, C_KI, C_WI, C_MA, C_MB) = (
    sum(SPLITS[:i]) for i in range(len(SPLITS)))
C_END = sum(SPLITS)

TM_PE, TM_QB, TM_KB, TM_VB, TM_QI, TM_KI, TM_WI = 0, 32, 544, 672, 800, 1056, 1088
TM_W = 1096
TM_CHUNK = TM_W // 4

WH, WKV, WG = 16, 4, 4
WINDOW = 128
NEG = -1e30
ND = 257


class Sems:

    def __init__(self, nc):
        self.nc, self.live = nc, []

    def __call__(self, name, count=None):
        if count is None:
            self.live.append(self.nc.alloc_semaphore(name=name))
            return self.live[-1]
        return [self(f"{name}{i}") for i in range(count)]

    def end_stage(self):
        self.nc.clear_and_free_semaphores(self.live)
        self.nc.all_engine_barrier()
        self.live = []


def mm3(pe, out, l, r, start, stop):
    pe.matmul(out, l[0], r[1], start=start, stop=False)
    pe.matmul(out, l[1], r[0], start=False, stop=False)
    return pe.matmul(out, l[0], r[0], start=False, stop=stop)


class Norm:

    def __init__(self, x_dram, gain_dram, ident):
        self.x_dram, self.gain_dram, self.ident = x_dram, gain_dram, ident

    def setup(self, nc, sem, tag, ctx, hT, room, tp):
        sb = lambda n, s, d=F32: ctx.enter_context(nc.sbuf_tensor(f"{tag}_{n}", s, d))
        self.nc, self.tp = nc, tp
        self.hi, self.lo = hT
        self.h = room[:, 0:D]
        blocks = lambda z: z.rearrange("p (k t) -> p k t", k=KD)
        self.g = [blocks(room[:, D:2 * D]), blocks(sb("g", [P, D])[:])]
        self.junk = sb("junk", [P, D], BF16)
        self.xt = sb("xt", [P, 3, D])
        self.gain = sb("gain", [P, KD])
        self.ss, self.ms, self.sd, self.rs = (sb(n, [P, NT]) for n in ("ss", "ms", "sd", "rs"))
        self.x_in = sem(f"{tag}_x_in", 3)
        (self.gain_in, self.squared, self.meaned, self.rooted, self.normed, self.turned, self.gained,
         self.hi_done, self.lo_done) = (
            sem(f"{tag}_{n}") for n in ("gain_in", "squared", "meaned", "rooted", "normed", "turned",
                                        "gained", "hi_done", "lo_done"))

    def load(self, sp, tiles):
        if tiles[0] == 0:
            sp.dma_start(self.gain[:], self.gain_dram.rearrange("(k p) -> p k", p=P),
                         allow_slow_non_contiguous=True).then_inc(self.gain_in, 16)
        for t in tiles:
            if t >= 3:
                sp.wait_ge(self.normed, t - 2)
            sp.dma_start(self.xt[:, t % 3], self.x_dram[t * P:(t + 1) * P, :]).then_inc(self.x_in[t % 3], 16)

    def square(self, act, t):
        act.wait_ge(self.x_in[t % 3], 16 * (t // 3 + 1))
        if t >= 1:
            act.wait_ge(self.squared, t)
        self.nc.scalar.activation(self.junk[:], self.xt[:, t % 3], ACT.Square,
                                  accum_out=self.ss[:, t:t + 1]).then_inc(self.squared, 1)

    def root(self, act, t):
        act.wait_ge(self.meaned, t + 1)
        self.nc.scalar.activation(self.sd[:, t:t + 1], self.ms[:, t:t + 1], ACT.Sqrt).then_inc(self.rooted, 1)

    def round_tile(self, act, t):
        act.wait_ge(self.gained, t + 1)
        self.nc.scalar.activation(self.hi[:, :, t * P:(t + 1) * P], self.g[t % 2],
                                  ACT.Copy).then_inc(self.hi_done, 1)

    def mean(self, dve, t):
        dve.wait_ge(self.squared, t + 1)
        self.nc.vector.tensor_scalar(self.ms[:, t:t + 1], self.ss[:, t:t + 1], 1.0 / D, EPS, ALU.mult,
                                     ALU.add).then_inc(self.meaned, 1)

    def norm(self, dve, t):
        dve.wait_ge(self.rooted, t + 1)
        self.nc.vector.reciprocal(self.rs[:, t:t + 1], self.sd[:, t:t + 1])
        dve.drain()
        if t >= 1:
            dve.wait_ge(self.turned, t)
        self.nc.vector.tensor_scalar(self.h, self.xt[:, t % 3], self.rs[:, t:t + 1], None,
                                     ALU.mult).then_inc(self.normed, 1)

    def gains(self, dve, t):
        dve.wait_ge(self.turned, t + 1)
        if t >= 2:
            dve.wait_ge(self.lo_done, t - 1)
        self.nc.vector.tensor_tensor(self.g[t % 2], self.tp[:, t % 2],
                                     self.gain[:].unsqueeze(2).broadcast_to([P, KD, P]),
                                     ALU.mult).then_inc(self.gained, 1)

    def split_tile(self, pool, t):
        pool.wait_ge(self.hi_done, t + 1)
        s = slice(t * P, (t + 1) * P)
        self.nc.gpsimd.tensor_tensor(self.lo[:, :, s], self.g[t % 2], self.hi[:, :, s].bitcast(F32),
                                     ALU.subtract).then_inc(self.lo_done, 1)

    def turn(self, pe, t):
        pe.wait_ge(self.normed, t + 1)
        if t >= 2:
            pe.wait_ge(self.gained, t - 1)
        for k in range(KD):
            last = self.nc.tensor.transpose(self.tp[:, t % 2, k], self.h[:, k * P:(k + 1) * P],
                                            self.ident[:])
        last.then_inc(self.turned, 1)


class Run:

    def __init__(self, kind, count, columns, store, func=ACT.Copy):
        self.kind, self.count, self.columns, self.store = kind, count, columns, store
        self.func = func


def each_chunk(eng, runs, body, first=0):
    n = 0
    for run in runs:
        if run.kind == "fm" and run.count >= 4:
            with eng.Fori(0, run.count // 2) as i:
                for p in (0, 1):
                    body(n + p + 2 * i, (n + p) % 2, (n + p) // 2 + i, p + 2 * i, run)
        else:
            for j in range(max(0, first - n), run.count):
                body(n + j, (n + j) % 2, (n + j) // 2, j, run)
        n += run.count


def stage_project(nc, sem, tag, norm, hT, weight, width, runs, h_dram=None, beside=None):
    n_tm = sum(r.count for r in runs if r.kind == "tm")
    total = sum(r.count for r in runs)
    w_view = weight.rearrange("(k p) n -> p k n", p=P)
    parts = [len(r.columns(j if r.kind == "tm" else 0)) for r in runs for j in range(r.count)]
    assert all(x == 1 for x in parts[n_tm:])

    def first_step(n):
        if isinstance(n, int) and n <= n_tm:
            return NT * n
        return NG * n + (NT - NG) * n_tm

    def loaded(n, par, use):
        if isinstance(n, int):
            return 16 * sum(parts[m] for m in range(par, n + 1, 2))
        return 16 * (use + 1 + sum(parts[m] - 1 for m in range(par, n_tm, 2)))

    def steps(n, par, run):
        if run.kind == "tm":
            banks = 4 if isinstance(n, int) and n == 0 else 8
            return [(first_step(n) + t, t % banks, t % 4, t, width) for t in range(NT)]
        return [(first_step(n) + g, g + NG * ((par + n_tm) % 2), g, g, GT) for g in range(NG)]

    def stores_before(n, g):
        if isinstance(n, int) and n < n_tm:
            return 4 * n + g // 4
        return n + 3 * n_tm

    with ExitStack() as c:
        sb = lambda n, s, d=F32: c.enter_context(nc.sbuf_tensor(f"{tag}_{n}", s, d))
        ws = sb("ws", [P, 2, KD, width])
        wh = sb("wh", [P, 2, KD, width], F32R)
        wl = sb("wl", [P, 2, KD, width], F32R)
        ob = sb("ob", [P, 4, GT])
        ps = c.enter_context(nc.psum_tensor(f"{tag}_ps", [P, 8, GT], F32))
        norm.setup(nc, sem, tag, c, hT, ws[:, 1].rearrange("p k n -> p (k n)")[:, 0:2 * D],
                   ps[:, 4:8].rearrange("p (s b) (k t) -> p s (b k) t", s=2, t=P))
        w_in = sem(f"{tag}_w_in", 2)
        stored = sem(f"{tag}_stored", 4)
        w_split, filled, evacuated, h_stored = (
            sem(f"{tag}_{n}") for n in ("w_split", "filled", "evacuated", "h_stored"))
        block = c.enter_context(nc.Block())

        @block.sync
        def _(sp):
            def load(n, par, use, j, run):
                if not isinstance(n, int) or n >= 2:
                    sp.wait_ge(w_split, n - 1)
                elif n == 1:
                    sp.wait_ge(norm.lo_done, NT)
                for at, c0, w in run.columns(j):
                    sp.dma_start(ws[:, par, :, at:at + w],
                                 w_view[:, :, bass.ds(c0, w)]).then_inc(w_in[par], 16)

            norm.load(sp, range(0, 2))
            load(0, 0, 0, 0, runs[0])
            norm.load(sp, range(2, NT))
            each_chunk(sp, runs, load, first=1)
            if beside is not None:
                beside.finish(sp)

        @block.gpsimd
        def _(pool):
            for g in range(NG):
                for t in range(4 * g, 4 * g + 4):
                    norm.split_tile(pool, t)
                if h_dram is not None:
                    pool.wait_ge(norm.lo_done, 4 * g + 4)
                    for half in range(2):
                        s = slice(g * GT, (g + 1) * GT)
                        pool.dma_start(h_dram[half, :, :, s], hT[half][:, :, s].bitcast(F32)).then_inc(h_stored, 16)
            if h_dram is not None:
                pool.wait_ge(h_stored, 32 * NG)

        @block.vector
        def _(dve):
            def split(n, par, use, j, run):
                w = width if run.kind == "tm" else P
                dve.wait_ge(w_in[par], loaded(n, par, use))
                if not isinstance(n, int) or n >= 2:
                    dve.wait_ge(filled, first_step(n - 1))
                nc.vector.tensor_copy(wh[:, par, :, 0:w], ws[:, par, :, 0:w])
                dve.drain()
                nc.vector.tensor_tensor(wl[:, par, :, 0:w], ws[:, par, :, 0:w],
                                        wh[:, par, :, 0:w].bitcast(F32), ALU.subtract).then_inc(w_split, 1)

            dve.wait_ge(norm.gain_in, 16)
            norm.mean(dve, 0)
            for t in range(NT):
                norm.norm(dve, t)
                if t + 1 < NT:
                    norm.mean(dve, t + 1)
                if t == 1:
                    split(0, 0, 0, 0, runs[0])
                if t >= 1:
                    norm.gains(dve, t - 1)
            norm.gains(dve, NT - 1)
            each_chunk(dve, runs, split, first=1)

        @block.tensor
        def _(pe):
            hi, lo = hT

            def multiply(n, par, use, j, run):
                pe.wait_ge(w_split, n + 1)
                for u, bank, _, g, w in steps(n, par, run):
                    first_pass = isinstance(u, int) and u < NT + 4
                    if first_pass and u >= 4:
                        pe.wait_ge(evacuated, u - 3)
                    elif not first_pass:
                        pe.wait_ge(evacuated, u - 7)
                    fill(bank, par, g, w, run.kind)

            def fill(bank, par, g, w, kind):
                for k in range(KD):
                    if kind == "tm":
                        s = slice(g * P, (g + 1) * P)
                        l, r = (hi[:, k, s], lo[:, k, s]), (wh[:, par, k, 0:w], wl[:, par, k, 0:w])
                    else:
                        s = slice(g * GT, (g + 1) * GT)
                        l, r = (wh[:, par, k, 0:P], wl[:, par, k, 0:P]), (hi[:, k, s], lo[:, k, s])
                    last = mm3(nc.tensor, ps[:, bank, 0:w], l, r, start=k == 0, stop=k == KD - 1)
                last.then_inc(filled, 1)

            for t in range(NT + 2):
                if t < NT:
                    norm.turn(pe, t)
                if t >= 2:
                    u = t - 2
                    if u == 0:
                        pe.wait_ge(w_split, 1)
                    if u >= 4:
                        pe.wait_ge(evacuated, u - 3)
                    pe.wait_ge(norm.lo_done, u + 1)
                    fill(u % 4, 0, u, width, "tm")
            each_chunk(pe, runs, multiply, first=1)

        @block.scalar
        def _(act):
            def evacuate(n, par, use, j, run):
                for step in steps(n, par, run):
                    evacuate_step(n, j, run, *step)

            def evacuate_step(n, j, run, u, bank, slot, g, w):
                target = ob[:, slot, 0:w]
                if not isinstance(n, int) or stores_before(n, g) >= 1:
                    act.wait_ge(stored[slot], 16 * stores_before(n, g))
                act.wait_ge(filled, u + 1)
                nc.scalar.activation(target, ps[:, bank, 0:w], run.func).then_inc(evacuated, 1)
                act.wait_ge(evacuated, u + 1)
                act.dma_start(run.store(j, g), target).then_inc(stored[slot], 16)

            first_chunk = steps(0, 0, runs[0])
            norm.square(act, 0)
            for t in range(NT):
                if t + 1 < NT:
                    norm.square(act, t + 1)
                norm.root(act, t)
                if t >= 1:
                    norm.round_tile(act, t - 1)
                if t >= 4:
                    evacuate_step(0, 0, runs[0], *first_chunk[t - 4])
            norm.round_tile(act, NT - 1)
            for t in range(NT - 4, NT):
                evacuate_step(0, 0, runs[0], *first_chunk[t])
            each_chunk(act, runs, evacuate, first=1)
            for g in range(4):
                act.wait_ge(stored[g], 16 * (total + 3 * n_tm))


FREQS = [(ROPE_M, 0), (ROT_D, ROPE_M // 2), (ROT_I, ROPE_M // 2 + ROT_D // 2)]
NF = (ROPE_M + ROT_D + ROT_I) // 2
TWO_PI = 2 * math.pi
PI_A = 6.28125
PI_B = float(np.float32(np.round((TWO_PI - PI_A) * 2.0 ** 19) / 2.0 ** 19))
PI_C = float(TWO_PI - PI_A - PI_B)
ROUNDER = 1.5 * 2.0 ** 23


def stage_qkv(nc, sem, ident, a, cqT, tm, qkT, qbT, kbT, qiT, kiT, va, vb, wi):
    RING = 7
    AHEAD = 2
    NB = 6
    with ExitStack() as c:
        sb = lambda n, s, d=F32: c.enter_context(nc.sbuf_tensor(f"b_{n}", s, d))
        pos_i = sb("pos_i", [P, NT], I32)
        pos = sb("pos", [P, NT])
        freq = sb("freq", [P, NF])
        ang = sb("ang", [P, NT, NF])
        turns = sb("turns", [P, NT, NF])
        red = sb("red", [P, 2, NT, NF])
        cos2 = sb("cos2", [P, NT, 2 * NF])
        sin2 = sb("sin2", [P, NT, 2 * NF])
        c_gain = sb("c_gain", [P, 3])
        qk_gain = sb("qk_gain", [P, 2, QK])
        b_gain = sb("b_gain", [P, 2, HD])
        ones = sb("ones", [P, 2])
        uqs = [sb(f"uq_{n}", [P, 2, H * QK], F32R) for n in ("hi", "lo")]
        ukv = sb("ukv", [P, D])
        ukvs = [sb(f"ukv_{n}", [P, D], F32R) for n in ("hi", "lo")]
        tmb = sb("tmb", [P, RING, TM_W])
        cq = sb("cq", [P, 4, 3, P])
        csq = sb("csq", [P, 2, 3, P])
        cg = sb("cg", [P, 2, 3, P])
        ch = sb("ch", [P, 2, 3, P], F32R)
        cl = sb("cl", [P, 2, 3, P], F32R)
        st1 = sb("st1", [P, NT, 2])
        sd1 = sb("sd1", [P, NT, 2])
        rs1 = sb("rs1", [P, NT, 2])
        qk = sb("qk", [P, RING, 2 * H, QK])
        qb = sb("qb", [P, 4, H + KV, HD])
        sq = sb("sq", [P, 2 * H * QK + (H + KV) * HD])
        uq = sq[:, 0:2 * H * QK].rearrange("p (k n) -> p k n", k=2)
        st2 = sb("st2", [P, 26])
        ms2 = sb("ms2", [P, 26])
        sd2 = sb("sd2", [P, 26])
        rs2 = sb("rs2", [P, 26])
        rot = sb("rot", [P, 2, 2 * H, ROPE_M])
        rot_p = sb("rot_p", [P, 2, H + KV, ROT_D])
        v = sb("v", [P, 4, 640])
        vh = sb("vh", [P, 3, 640], F32R)
        vl = sb("vl", [P, 3, 640], F32R)
        wi_all = sb("wi_all", [P, NT, H])
        th = sb("th", [P, NB, GT], F32R)
        tl = sb("tl", [P, NB, GT], F32R)
        p_ss = c.enter_context(nc.psum_tensor("b_ps_ss", [P, 4], F32))
        p_up = c.enter_context(nc.psum_tensor("b_ps_up", [P, 4, GT], F32))
        p_t = c.enter_context(nc.psum_tensor("b_ps_t", [P, 3, GT], F32))
        const_in, w_ready, trig_r, trig, filled_c = (
            sem(f"b_{n}") for n in ("const_in", "w_ready", "trig_r", "trig", "ones_made"))
        tm_in, cq_in = sem("b_tm_in", RING), sem("b_cq_in", 4)
        (c_squared, c_gained, c_hi, c_lo, summed, meaned1, rooted1, scaled1, up, up_read, pe_spread,
         squared2, meaned2, rooted2, normed, gained, roped, roped_p, v_hi, v_lo, turned, t_hi, t_lo) = (
            sem(f"b_{n}") for n in
            ("c_squared", "c_gained", "c_hi", "c_lo", "summed", "meaned1", "rooted1", "scaled1", "up",
             "up_read", "pe_spread", "squared2", "meaned2", "rooted2", "normed", "gained", "roped",
             "roped_p", "v_hi", "v_lo", "turned", "t_hi", "t_lo"))
        t_stored = sem("b_t_stored", NB)
        v_stored = sem("b_v_stored", 3)
        wi_made, wi_stored = sem("b_wi_made"), sem("b_wi_stored")
        block = c.enter_context(nc.Block())
        def staged(parts, once=None):
            for i in range(NT + max(k for k, _ in parts)):
                if i == 2 and once is not None:
                    once()
                for k, f in parts:
                    if 0 <= i - k < NT:
                        f(i - k)

        def stored_of(tiles, b):
            return (96 if b == NB - 1 else 32) * tiles

        def rotate(ops, eng, x, table, t, tmp, done):
            rd, f0 = FREQS[table]
            n, h = x.shape[1], rd // 2
            spread = lambda tab, a0, a1: tab[:, t, 2 * f0 + a0:2 * f0 + a1].unsqueeze(1)\
                .broadcast_to([P, n, a1 - a0])
            ops.tensor_tensor(tmp[:, 1, 0:n, 0:h], x[:, :, h:rd], spread(sin2, 0, h), ALU.mult)
            ops.tensor_tensor(tmp[:, 1, 0:n, h:rd], x[:, :, 0:h], spread(sin2, h, rd), ALU.mult)
            ops.tensor_tensor(tmp[:, 0, 0:n, 0:rd], x, spread(cos2, 0, rd), ALU.mult)
            eng.drain()
            last = ops.tensor_tensor(x, tmp[:, 0, 0:n, 0:rd], tmp[:, 1, 0:n, 0:rd], ALU.add)
            if done is not None:
                last.then_inc(done, 1)
            return last

        @block.sync
        def _(sp):
            sp.dma_start(pos_i[:], a["positions"][0].rearrange("(t p) -> p t", p=P),
                         allow_slow_non_contiguous=True).then_inc(const_in, 16)
            sp.dma_start(c_gain[:, 0:2], a["mla_q_norm"][0].rearrange("(k p) -> p k", p=P),
                         allow_slow_non_contiguous=True).then_inc(const_in, 16)
            sp.dma_start(c_gain[:, 2:3], a["mla_kv_norm"].rearrange("a p -> p a"),
                         allow_slow_non_contiguous=True).then_inc(const_in, 16)
            for dst, name in ((qk_gain[:, 0], "mla_q_gain"), (qk_gain[:, 1], "mla_k_gain"),
                              (b_gain[:, 0], "dsa_q_gain"), (b_gain[:, 1], "dsa_k_gain")):
                sp.dma_start(dst, a[name][0].partition_broadcast(P)).then_inc(const_in, 16)
            sp.dma_start(uq, a["mla_w_uq"][0].rearrange("(k p) n -> p k n", p=P)).then_inc(const_in, 16)
            sp.dma_start(ukv[:], a["mla_w_ukv"][0]).then_inc(const_in, 16)

            def load(t):
                s = slice(t * P, (t + 1) * P)
                if t >= RING:
                    sp.wait_ge(turned, NB * (t - RING + 1))
                    sp.wait_ge(v_lo, t - RING + 1)
                sp.dma_start(tmb[:, t % RING], tm[s, :]).then_inc(tm_in[t % RING], 16)
                if t >= 4:
                    sp.wait_ge(c_gained, t - 3)
                    sp.wait_ge(c_squared, t - 3)
                sp.dma_start(cq[:, t % 4], cqT.rearrange("(k p) t -> p k t", p=P)[:, :, s])\
                    .then_inc(cq_in[t % 4], 16)

            def store_values(t):
                s = slice(t * P, (t + 1) * P)
                sp.wait_ge(v_lo, t + 1)
                for half, src in ((0, vh), (1, vl)):
                    sp.dma_start(va[half, s, :], src[:, t % 3, 0:512].bitcast(F32)).then_inc(v_stored[t % 3], 16)
                    sp.dma_start(vb[half, s, :], src[:, t % 3, 512:640].bitcast(F32)).then_inc(v_stored[t % 3], 16)

            def store_turned(t):
                s = slice(t * P, (t + 1) * P)
                for b in range(NB):
                    sp.wait_ge(t_lo, NB * t + b + 1)
                    for half, src in ((0, th), (1, tl)):
                        x = src[:, b].bitcast(F32).rearrange("p (j t) -> p j t", t=P)
                        done = t_stored[b]
                        if b < 4:
                            sp.dma_start(qkT[half, 4 * b:4 * b + 4, :, s].rearrange("h d t -> d h t"),
                                         x[0:QK]).then_inc(done, 16)
                        elif b == 4:
                            sp.dma_start(qbT[half, :, :, s].rearrange("j p t -> p j t"), x).then_inc(done, 16)
                        else:
                            sp.dma_start(kbT[half, :, s], x[:, 0]).then_inc(done, 16)
                            sp.dma_start(qiT[half, :, :, s].rearrange("j p t -> p j t"),
                                         x[:, 1:3]).then_inc(done, 16)
                            sp.dma_start(kiT[half, :, s], x[0:IDX, 3]).then_inc(done, 16)

            staged([(AHEAD + 6, store_turned), (AHEAD + 3, store_values), (0, load)])
            sp.wait_ge(wi_made, NT)
            sp.dma_start(wi.rearrange("(t p) h -> p t h", p=P), wi_all[:]).then_inc(wi_stored, 16)
            sp.wait_ge(wi_stored, 16)
            for b in range(NB):
                sp.wait_ge(t_stored[b], stored_of(NT, b))
            for n in range(3):
                sp.wait_ge(v_stored[n], 64 * len(range(n, NT, 3)))

        @block.scalar
        def _(act):
            def sines():
                act.wait_ge(trig_r, 1)
                nc.scalar.activation(red[:], red[:], ACT.Sin).then_inc(trig_r, 1)

            def squares_c(t):
                act.wait_ge(cq_in[t % 4], 16 * (t // 4 + 1))
                if t >= 2:
                    act.wait_ge(summed, t - 1)
                nc.scalar.activation(csq[:, t % 2], cq[:, t % 4], ACT.Square).then_inc(c_squared, 1)

            def split_c(t):
                act.wait_ge(c_gained, t + 1)
                if t >= 2:
                    act.wait_ge(up, 2 * (t - 1))
                nc.scalar.activation(ch[:, t % 2], cg[:, t % 2], ACT.Copy).then_inc(c_hi, 1)

            def roots_c(t):
                act.wait_ge(meaned1, t + 1)
                nc.scalar.activation(sd1[:, t], st1[:, t], ACT.Sqrt).then_inc(rooted1, 1)

            def heads(t):
                act.wait_ge(scaled1, t + 1)
                if t >= RING:
                    act.wait_ge(turned, NB * (t - RING + 1))
                if t >= 4:
                    act.wait_ge(v_lo, t - 3)
                act.wait_ge(up, 2 * t + 1)
                for b in range(2):
                    nc.scalar.activation(qk[:, t % RING, 4 * b:4 * b + 4],
                                         p_up[:, b, 0:4 * QK].rearrange("p (h d) -> p h d", d=QK),
                                         ACT.Copy, scale=rs1[:, t, 0:1])
                act.wait_ge(up, 2 * t + 2)
                for b in range(2):
                    kv = p_up[:, 2 + b].rearrange("p (h d) -> p h d", d=NOPE + HD)
                    nc.scalar.activation(qk[:, t % RING, H + 4 * b:H + 4 * b + 4, 0:NOPE], kv[:, :, 0:NOPE],
                                         ACT.Copy, scale=rs1[:, t, 1:2])
                    last = nc.scalar.activation(
                        v[:, t % 4, 256 * b:256 * b + 256].rearrange("p (h d) -> p h d", d=HD),
                        kv[:, :, NOPE:], ACT.Copy, scale=rs1[:, t, 1:2])
                last.then_inc(up_read, 1)

            def squares(t):
                act.wait_ge(up_read, t + 1)
                act.wait_ge(pe_spread, t + 1)
                if t >= 1:
                    act.wait_ge(meaned2, t)
                n = 2 * H * QK
                nc.scalar.activation(sq[:, 0:n], qk[:, t % RING].rearrange("p h d -> p (h d)"), ACT.Square)
                nc.scalar.activation(sq[:, n:], tmb[:, t % RING, TM_QB:TM_VB], ACT.Square).then_inc(squared2, 1)
                if t >= 3:
                    act.wait_ge(v_stored[t % 3], 64 * (t // 3))
                    act.wait_ge(v_lo, t - 2)
                nc.scalar.activation(vh[:, t % 3], v[:, t % 4], ACT.Copy).then_inc(v_hi, 1)

            def roots(t):
                act.wait_ge(meaned2, t + 1)
                if t >= 1:
                    act.wait_ge(normed, t)
                nc.scalar.activation(sd2[:], ms2[:], ACT.Sqrt).then_inc(rooted2, 1)

            def split_turned(t):
                for b in range(NB):
                    u = NB * t + b
                    act.wait_ge(turned, u + 1)
                    if t >= 1:
                        act.wait_ge(t_stored[b], stored_of(t, b))
                        act.wait_ge(t_lo, u - NB + 1)
                    rows = QK if b < 4 else P
                    parts = [(rows, 0, GT)] if b < 5 else [(P, 0, 3 * P), (IDX, 3 * P, GT)]
                    for r, x0, x1 in parts:
                        last = nc.scalar.activation(th[0:r, b, x0:x1], p_t[0:r, u % 3, x0:x1], ACT.Copy)
                    last.then_inc(t_hi, 1)

            staged([(1, roots_c), (6, split_turned), (2, squares), (0, squares_c), (0, split_c), (1, heads),
                    (2, roots)], sines)

        @block.vector
        def _(dve):
            for n, (rd, f0) in enumerate(FREQS):
                for f in range(rd // 2):
                    value = float(np.float32(THETA) ** (-np.float32(2 * f) / np.float32(rd)))
                    nc.vector.memset(freq[:, f0 + f:f0 + f + 1], value)
            nc.vector.memset(ones[:], 1.0).then_inc(filled_c, 1)
            dve.wait_ge(const_in, 16 * 9)
            nc.vector.tensor_copy(pos[:], pos_i[:])
            nc.vector.tensor_copy(uqs[0][:], uq)
            nc.vector.tensor_copy(ukvs[0][:], ukv[:])
            dve.drain()
            nc.vector.tensor_tensor(uqs[1][:], uq, uqs[0][:].bitcast(F32), ALU.subtract)
            nc.vector.tensor_tensor(ukvs[1][:], ukv[:], ukvs[0][:].bitcast(F32), ALU.subtract)\
                .then_inc(w_ready, 1)
            def angles():
                nc.vector.tensor_tensor(ang[:], pos[:].unsqueeze(2).broadcast_to([P, NT, NF]),
                                        freq[:].unsqueeze(1).broadcast_to([P, NT, NF]), ALU.mult)
                dve.drain()
                for which, quarter in ((0, 0.25), (1, 0.0)):
                    nc.vector.tensor_scalar(turns[:], ang[:], 1 / TWO_PI, quarter, ALU.mult, ALU.add)
                    dve.drain()
                    nc.vector.tensor_scalar(turns[:], turns[:], ROUNDER, None, ALU.add)
                    dve.drain()
                    nc.vector.tensor_scalar(turns[:], turns[:], ROUNDER, None, ALU.subtract)
                    dve.drain()
                    src = ang[:]
                    for part in (PI_A, PI_B, PI_C):
                        nc.vector.scalar_tensor_tensor(out=red[:, which], in0=turns[:], scalar=-part, in1=src,
                                                       op0=ALU.mult, op1=ALU.add)
                        dve.drain()
                        src = red[:, which]
                    if quarter:
                        nc.vector.tensor_scalar(red[:, which], red[:, which], math.pi / 2, None, ALU.add)
                        dve.drain()
                last = nc.vector.tensor_scalar(red[:], red[:], 3.1415925, -3.1415925, ALU.min, ALU.max)
                last.then_inc(trig_r, 1)
                dve.wait_ge(trig_r, 2)
                for rd, f0 in FREQS:
                    h = rd // 2
                    for half in range(2):
                        at = slice(2 * f0 + half * h, 2 * f0 + half * h + h)
                        nc.vector.tensor_copy(cos2[:, :, at], red[:, 0, :, f0:f0 + h])
                        last = nc.vector.tensor_scalar(sin2[:, :, at], red[:, 1, :, f0:f0 + h],
                                                       1.0 if half else -1.0, None, ALU.mult)
                last.then_inc(trig, 1)

            def gains_c(t):
                dve.wait_ge(cq_in[t % 4], 16 * (t // 4 + 1))
                if t >= 2:
                    dve.wait_ge(c_lo, t - 1)
                    dve.wait_ge(c_hi, t - 1)
                nc.vector.tensor_tensor(cg[:, t % 2], cq[:, t % 4],
                                        c_gain[:].unsqueeze(2).broadcast_to([P, 3, P]),
                                        ALU.mult).then_inc(c_gained, 1)

            def split_c(t):
                dve.wait_ge(c_hi, t + 1)
                nc.vector.tensor_tensor(cl[:, t % 2], cg[:, t % 2], ch[:, t % 2].bitcast(F32),
                                        ALU.subtract).then_inc(c_lo, 1)
                dve.wait_ge(summed, t + 1)
                nc.vector.tensor_scalar(st1[:, t, 0:1], p_ss[:, 0:1], 1.0 / 256, EPS, ALU.mult, ALU.add)
                nc.vector.tensor_scalar(st1[:, t, 1:2], p_ss[:, 2:3], 1.0 / 128, EPS, ALU.mult,
                                        ALU.add).then_inc(meaned1, 1)

            def scales_c(t):
                dve.wait_ge(rooted1, t + 1)
                nc.vector.reciprocal(rs1[:, t], sd1[:, t]).then_inc(scaled1, 1)

            def means(t):
                dve.wait_ge(squared2, t + 1)
                n = 2 * H * QK
                nc.vector.tensor_reduce(st2[:, 0:16], sq[:, 0:n].rearrange("p (h d) -> p h d", d=QK),
                                        AX.X, ALU.add)
                nc.vector.tensor_reduce(st2[:, 16:26], sq[:, n:].rearrange("p (h d) -> p h d", d=HD),
                                        AX.X, ALU.add)
                dve.drain()
                if t >= 1:
                    dve.wait_ge(rooted2, t)
                nc.vector.tensor_scalar(ms2[:, 0:16], st2[:, 0:16], 1.0 / QK, EPS, ALU.mult, ALU.add)
                nc.vector.tensor_scalar(ms2[:, 16:26], st2[:, 16:26], 1.0 / HD, EPS, ALU.mult,
                                        ALU.add).then_inc(meaned2, 1)

            def norms(t):
                dve.wait_ge(rooted2, t + 1)
                nc.vector.reciprocal(rs2[:], sd2[:])
                dve.drain()
                if t >= 4:
                    dve.wait_ge(turned, NB * (t - 3))
                nc.vector.tensor_tensor(qk[:, t % RING], qk[:, t % RING],
                                        rs2[:, 0:16].unsqueeze(2).broadcast_to([P, 16, QK]), ALU.mult)
                nc.vector.tensor_tensor(qb[:, t % 4],
                                        tmb[:, t % RING, TM_QB:TM_VB].rearrange("p (h d) -> p h d", d=HD),
                                        rs2[:, 16:26].unsqueeze(2).broadcast_to([P, 10, HD]),
                                        ALU.mult).then_inc(normed, 1)

            def rotate_heads(t):
                dve.wait_ge(gained, t + 1)
                rotate(nc.vector, dve, qk[:, t % RING, :, NOPE:QK], 0, t, rot, roped)

            def split_turned(t):
                for b in range(NB):
                    u = NB * t + b
                    dve.wait_ge(t_hi, u + 1)
                    parts = [(QK if b < 4 else P, 0, GT)] if b < 5 else [(P, 0, 3 * P), (IDX, 3 * P, GT)]
                    for r, x0, x1 in parts:
                        last = nc.vector.tensor_tensor(tl[0:r, b, x0:x1], p_t[0:r, u % 3, x0:x1],
                                                       th[0:r, b, x0:x1].bitcast(F32), ALU.subtract)
                    last.then_inc(t_lo, 1)

            staged([(0, gains_c), (6, split_turned), (1, scales_c), (3, norms), (2, means),
                    (5, rotate_heads), (0, split_c)], angles)

        @block.gpsimd
        def _(pool):
            pool.wait_ge(const_in, 16 * 9)

            def spread_k(t):
                pool.wait_ge(tm_in[t % RING], 16 * (t // RING + 1))
                if t >= RING:
                    pool.wait_ge(turned, NB * (t - RING + 1))
                nc.gpsimd.tensor_copy(qk[:, t % RING, H:2 * H, NOPE:QK],
                                      tmb[:, t % RING, 0:ROPE_M].unsqueeze(1).broadcast_to([P, H, ROPE_M]))
                nc.gpsimd.tensor_copy(v[:, t % 4, 512:640], tmb[:, t % RING, TM_VB:TM_QI]).then_inc(pe_spread, 1)

            def split_values(t):
                pool.wait_ge(v_hi, t + 1)
                if t >= 3:
                    pool.wait_ge(v_stored[t % 3], 64 * (t // 3))
                nc.gpsimd.tensor_tensor(vl[:, t % 3], v[:, t % 4], vh[:, t % 3].bitcast(F32),
                                        ALU.subtract).then_inc(v_lo, 1)
                if t == 0:
                    pool.wait_ge(trig, 1)
                ix = tmb[:, t % RING, TM_QI:TM_WI].rearrange("p (h d) -> p h d", d=IDX)
                rotate(nc.gpsimd, pool, ix[:, :, 0:ROT_I], 2, t, rot_p, None)
                nc.gpsimd.tensor_scalar(wi_all[:, t], tmb[:, t % RING, TM_WI:TM_W],
                                        H ** -0.5 * IDX ** -0.5, None, ALU.mult).then_inc(wi_made, 1)
                pool.drain()

            def gains(t):
                pool.wait_ge(normed, t + 1)
                for n in range(2):
                    x = qk[:, t % RING, H * n:H * n + H]
                    last = nc.gpsimd.tensor_tensor(x, x, qk_gain[:, n].unsqueeze(1)
                                                   .broadcast_to([P, H, QK]), ALU.mult)
                last.then_inc(gained, 1)
                for n, (h0, h1) in enumerate(((0, H), (H, H + KV))):
                    x = qb[:, t % 4, h0:h1]
                    nc.gpsimd.tensor_tensor(x, x, b_gain[:, n].unsqueeze(1)
                                            .broadcast_to([P, h1 - h0, HD]), ALU.mult)
                pool.drain()
                rotate(nc.gpsimd, pool, qb[:, t % 4, :, 0:ROT_D], 1, t, rot_p, roped_p)
                pool.drain()

            staged([(4, gains), (1, spread_k), (3, split_values)])

        @block.tensor
        def _(pe):
            pe.wait_ge(filled_c, 1)
            pe.wait_ge(w_ready, 1)

            def sums_c(t):
                pe.wait_ge(c_squared, t + 1)
                if t >= 1:
                    pe.wait_ge(meaned1, t)
                for k in range(2):
                    nc.tensor.matmul(p_ss[:, 0:2], csq[:, t % 2, k], ones[:], start=k == 0, stop=k == 1)
                nc.tensor.matmul(p_ss[:, 2:4], csq[:, t % 2, 2], ones[:], start=True, stop=True)\
                    .then_inc(summed, 1)

            def up_project(t):
                pe.wait_ge(c_lo, t + 1)
                if t >= 1:
                    pe.wait_ge(up_read, t)
                for b in range(2):
                    for k in range(2):
                        s = slice(4 * QK * b, 4 * QK * (b + 1))
                        last = mm3(nc.tensor, p_up[:, b, 0:4 * QK], (ch[:, t % 2, k], cl[:, t % 2, k]),
                                   (uqs[0][:, k, s], uqs[1][:, k, s]), start=k == 0, stop=k == 1)
                last.then_inc(up, 1)
                for b in range(2):
                    s = slice(GT * b, GT * (b + 1))
                    last = mm3(nc.tensor, p_up[:, 2 + b], (ch[:, t % 2, 2], cl[:, t % 2, 2]),
                               (ukvs[0][:, s], ukvs[1][:, s]), start=True, stop=True)
                last.then_inc(up, 1)

            def turn(t):
                pe.wait_ge(roped, t + 1)
                pe.wait_ge(roped_p, t + 1)
                for b in range(NB):
                    u = NB * t + b
                    if u >= 3:
                        pe.wait_ge(t_lo, u - 2)
                    if b < 4:
                        blocks = [(QK, qk[:, t % RING, 4 * b + j]) for j in range(4)]
                    elif b == 4:
                        blocks = [(P, qb[:, t % 4, 2 * j:2 * j + 2]) for j in range(4)]
                    else:
                        x = tmb[:, t % RING]
                        blocks = [(P, qb[:, t % 4, H:H + KV]), (P, x[:, TM_QI:TM_QI + P]),
                                  (P, x[:, TM_QI + P:TM_KI]), (IDX, x[:, TM_KI:TM_WI])]
                    for j, (rows, src) in enumerate(blocks):
                        last = nc.tensor.transpose(p_t[0:rows, u % 3, j * P:(j + 1) * P], src, ident[:])
                    last.then_inc(turned, 1)

            staged([(6, turn), (1, up_project), (0, sums_c)])


class Attention:
    width = T
    ahead = 4
    lead = 8
    output_late = 3
    split_ring = 4
    lag = 3
    score_banks = 3
    packed = True
    batched = False
    depth = 2

    def pe_start(self, pe): ...
    def dve_start(self, dve): ...
    def act_start(self, act): ...
    def pool_start(self, pool): ...
    def pool_unit(self, pool, n): ...
    def wait_bias(self, dve, n, s): ...
    def act_sub(self, act, n, s, shift): ...
    def shift_made(self, dve, n, shift): ...
    def add_sinks(self, dve, n, sums): ...

    def least_max(self, n, s):
        return -3e38


def schedule(units, behind, lead, output_late, batched):
    steps, late = [], []
    blocks = 0
    for n in range(len(units) + behind):
        m = n - behind
        s_steps = []
        if n < len(units):
            for s in range(4):
                keys = units[n]["keys"][s]
                for c, k0 in enumerate(range(0, keys, GT)):
                    s_steps.append(("S", n, s, c, k0, min(GT, keys - k0), k0 + GT >= keys))
        b_steps = [("B", m, i, j, s0) for i, (j, s0) in enumerate(units[m]["blocks"])] + [("V", m)] if m >= 0 else []
        pending = []

        def take_scores():
            nonlocal pending
            step = s_steps.pop(0)
            steps.append(step)
            steps.extend(pending)
            pending = []
            if step[6] and not batched:
                pending = [("E", n, step[2])]
            elif step[6] and step[2] == 3:
                pending = [("E", n, s) for s in range(4)]

        for _ in range(min(lead, len(s_steps))):
            take_scores()
        total, rest = len(b_steps), len(s_steps)
        for x in range(total):
            steps.append(b_steps[x])
            blocks += steps[-1][0] == "B"
            while late and late[0][1] <= blocks:
                steps.append(("O", late.pop(0)[0]))
            while s_steps and (rest - len(s_steps)) * total < (x + 1) * rest:
                take_scores()
        while s_steps:
            take_scores()
        steps += pending
        if m >= 0:
            late.append((m, blocks + output_late))
    return steps + [("O", n) for n, _ in late]


def stage_attention(nc, sem, tag, ident, layer):
    units = layer.units
    R, S = layer.depth, layer.split_ring
    steps = schedule(units, R - 1, layer.lead, layer.output_late,
                     layer.batched)
    n_b = [sum(len(u["blocks"]) for u in units[:n]) for n in range(len(units) + 1)]
    A = layer.score_banks
    B = 6 - A
    ring = lambda n, place: (n_b[n] + n + place) % B
    n_sub = lambda n, s: 4 * n + s
    with ExitStack() as c:
        sb = lambda n, s, d=F32: c.enter_context(nc.sbuf_tensor(f"{tag}_{n}", s, d))
        probs = sb("probs", [P, R, 4, layer.width])
        maxes = sb("maxes", [P, R, 4, 4])
        top = sb("top", [P, R, 4])
        shift = sb("shift", [P, R, 4])
        th = sb("th", [P, S, GT], F32R)
        tl = sb("tl", [P, S, GT], F32R)
        sums = sb("sums", [P, R, 4])
        inv = sb("inv", [P, 2, 4])
        spread = sb("spread", [P, 2, GT])
        halves = sb("halves", [P, 2, GT])
        lower = sb("lower", [HD, GT])
        ot = sb("ot", [HD, 2, GT])
        p_s = c.enter_context(nc.psum_tensor(f"{tag}_p_s", [P, A, GT], F32))
        p_t = c.enter_context(nc.psum_tensor(f"{tag}_p_t", [P, B, GT], F32))
        p_o = c.enter_context(nc.psum_tensor(f"{tag}_p_o", [P, 2, GT], F32))
        scored, moved, shifted, exped, turned, hi_done, lo_done, multiplied, inverted, inv_turned, spread_done, weighed, out_done = (
            sem(f"{tag}_{n}") for n in ("scored", "moved", "shifted", "exped", "turned", "hi_done",
                                        "lo_done", "multiplied", "inverted", "inv_turned", "spread_done",
                                        "weighed", "out_done"))
        stored, lowered = sem(f"{tag}_stored", 2), sem(f"{tag}_lowered")
        n_s = [sum(-(-k // GT) for u in units[:n] for k in u["keys"]) for n in range(len(units) + 1)]
        output_read = weighed if layer.packed else out_done
        layer.setup(nc, sem, ident, c, dict(exped=exped, inverted=inverted, multiplied=multiplied, moved=moved,
                                            lo_done=lo_done, n_b=n_b, n_s=n_s))
        block = c.enter_context(nc.Block())

        @block.sync
        def _(sp):
            ahead = layer.ahead
            for n in range(ahead):
                layer.load(sp, n)
            for n in range(len(units)):
                if n + ahead < len(units):
                    layer.load(sp, n + ahead)
                if n >= 1:
                    sp.wait_ge(out_done, n)
                    sp.dma_start(layer.store(n - 1), ot[:, (n - 1) % 2]).then_inc(stored[(n - 1) % 2], 16)
            n = len(units) - 1
            sp.wait_ge(out_done, n + 1)
            sp.dma_start(layer.store(n), ot[:, n % 2]).then_inc(stored[n % 2], 16)
            for p in range(2):
                sp.wait_ge(stored[p], 16 * len(range(p, len(units), 2)))

        @block.tensor
        def _(pe):
            layer.pe_start(pe)
            i = 0
            behind = []

            def multiply():
                n, place, j, s0 = behind.pop(0)
                b = n_b[n] + place
                if place == 0:
                    layer.wait_values(pe, n)
                    if n >= 2:
                        pe.wait_ge(output_read, n - 1)
                pe.wait_ge(hi_done, b + 1)
                out = p_o[:, n % 2, s0 * P:GT]
                v, last = layer.values(n, j), place == len(units[n]["blocks"]) - 1
                hi, lo = th[:, b % S, s0 * P:GT], tl[:, b % S, s0 * P:GT]
                if layer.packed:
                    nc.tensor.matmul(out, v, hi, start=place == 0, stop=False)
                    pe.wait_ge(lo_done, b + 1)
                    nc.tensor.matmul(out, v, lo, start=False, stop=last).then_inc(multiplied, 1)
                else:
                    nc.tensor.matmul(out[0:HD], v[:, 0:HD], hi, start=place == 0, stop=False)
                    nc.tensor.matmul(out[0:HD], v[:, HD:P], hi, start=False, stop=False)
                    pe.wait_ge(lo_done, b + 1)
                    nc.tensor.matmul(out[0:HD], v[:, 0:HD], lo, start=False, stop=last)\
                        .then_inc(multiplied, 1)

            def wait_bank(n, place):
                r = n_b[n] + n + place - B
                if r < 0:
                    return
                m = max(x for x in range(n + 1) if n_b[x] + x <= r)
                if r - n_b[m] - m == len(units[m]["blocks"]):
                    pe.wait_ge(spread_done, m + 1)
                else:
                    pe.wait_ge(lo_done, r - m + 1)

            for step in steps:
                if step[0] == "S":
                    _, n, s, ch, k0, w, last = step
                    if s == 0 and ch == 0:
                        layer.wait_scores(pe, n)
                    if i >= A:
                        pe.wait_ge(moved, i - A + 1)
                    layer.scores(p_s[:, i % A, 0:w], n, s, k0, w).then_inc(scored, 1)
                    i += 1
                elif step[0] == "B":
                    _, n, place, j, s0 = step
                    if place == 0:
                        pe.wait_ge(exped, n_sub(n, 3) + 1)
                    wait_bank(n, place)
                    for s in range(s0, 4):
                        last = nc.tensor.transpose(p_t[:, ring(n, place), s * P:(s + 1) * P],
                                                   probs[:, n % R, s, j * P:(j + 1) * P], ident[:])
                    last.then_inc(turned, 1)
                    behind.append((n, place, j, s0))
                    if len(behind) > layer.lag:
                        multiply()
                elif step[0] == "V":
                    n = step[1]
                    place = len(units[n]["blocks"])
                    wait_bank(n, place)
                    pe.wait_ge(inverted, n + 1)
                    for s in range(4):
                        last = nc.tensor.transpose(p_t[:, ring(n, place), s * P:(s + 1) * P],
                                                   inv[:, n % 2, s:s + 1].broadcast_to([P, P]), ident[:])
                    last.then_inc(inv_turned, 1)
            while behind:
                multiply()

        @block.vector
        def _(dve):
            layer.dve_start(dve)
            i = 0
            for step in steps:
                if step[0] == "S":
                    _, n, s, ch, k0, w, last = step
                    if ch == 0:
                        layer.wait_bias(dve, n, s)
                        if n >= R and s == 0:
                            dve.wait_ge(turned, n_b[n - R + 1])
                    dve.wait_ge(scored, i + 1)
                    nc.vector.tensor_tensor_reduce(
                        out=probs[:, n % R, s, k0:k0 + w], in0=p_s[:, i % A, 0:w],
                        in1=layer.bias(n, s, k0, w), scale=1.0, scalar=layer.least_max(n, s),
                        op0=ALU.add, op1=ALU.max, accum_out=maxes[:, n % R, s, ch:ch + 1]).then_inc(moved, 1)
                    i += 1
                    if layer.batched:
                        if s == 3:
                            if n >= R:
                                dve.wait_ge(exped, n_sub(n - R, 3) + 1)
                            dve.wait_ge(moved, i)
                            nc.vector.tensor_scalar(shift[:, n % R], maxes[:, n % R, :, 0], -layer.scale, None,
                                                    ALU.mult).then_inc(shifted, 1)
                            layer.shift_made(dve, n, shift[:, n % R])
                    elif last:
                        m = maxes[:, n % R, s, 0:1]
                        dve.wait_ge(moved, i)
                        if ch > 0:
                            m = top[:, n % R, s:s + 1]
                            nc.vector.tensor_reduce(m, maxes[:, n % R, s, 0:ch + 1], AX.X, ALU.max)
                            dve.drain()
                        if n >= R:
                            dve.wait_ge(exped, n_sub(n - R, s) + 1)
                        nc.vector.tensor_scalar(shift[:, n % R, s:s + 1], m, -layer.scale, None,
                                                ALU.mult).then_inc(shifted, 1)
                elif step[0] == "B":
                    _, n, place, j, s0 = step
                    b = n_b[n] + place
                    if b >= S:
                        dve.wait_ge(multiplied, b - S + 1)
                    dve.wait_ge(hi_done, b + 1)
                    nc.vector.tensor_tensor(tl[:, b % S, s0 * P:GT], p_t[:, ring(n, place), s0 * P:GT],
                                            th[:, b % S, s0 * P:GT].bitcast(F32),
                                            ALU.subtract).then_inc(lo_done, 1)
                    if place == 0:
                        dve.wait_ge(exped, n_sub(n, 3) + 1)
                        layer.add_sinks(dve, n, sums[:, n % R])
                        if n >= 2:
                            dve.wait_ge(inv_turned, n - 1)
                        nc.vector.reciprocal(inv[:, n % 2], sums[:, n % R]).then_inc(inverted, 1)
                elif step[0] == "O":
                    n = step[1]
                    dve.wait_ge(multiplied, n_b[n + 1])
                    dve.wait_ge(spread_done, n + 1)
                    if not layer.packed:
                        if n >= 2:
                            dve.wait_ge(stored[n % 2], 16 * (n // 2))
                        nc.vector.tensor_tensor(ot[:, n % 2], p_o[0:HD, n % 2], spread[0:HD, n % 2],
                                                ALU.mult).then_inc(out_done, 1)
                        continue
                    if n >= 2:
                        dve.wait_ge(out_done, n - 1)
                    nc.vector.tensor_tensor(halves[:, n % 2], p_o[:, n % 2], spread[:, n % 2],
                                            ALU.mult).then_inc(weighed, 1)

        @block.scalar
        def _(act):
            layer.act_start(act)
            for step in steps:
                if step[0] == "E":
                    _, n, s = step
                    act.wait_ge(shifted, n + 1 if layer.batched else n_sub(n, s) + 1)
                    x = probs[:, n % R, s, 0:units[n]["keys"][s]]
                    layer.act_sub(act, n, s, shift[:, n % R, s:s + 1])
                    if n >= R and s == 0:
                        act.wait_ge(inverted, n - R + 1)
                    nc.scalar.activation(x, x, ACT.Exp, bias=shift[:, n % R, s:s + 1], scale=layer.scale,
                                         accum_out=sums[:, n % R, s:s + 1]).then_inc(exped, 1)
                elif step[0] == "B":
                    _, n, place, j, s0 = step
                    b = n_b[n] + place
                    act.wait_ge(turned, b + 1)
                    if b >= S:
                        act.wait_ge(multiplied, b - S + 1)
                    nc.scalar.activation(th[:, b % S, s0 * P:GT], p_t[:, ring(n, place), s0 * P:GT],
                                         ACT.Copy).then_inc(hi_done, 1)
                elif step[0] == "V":
                    n = step[1]
                    act.wait_ge(inv_turned, n + 1)
                    if n >= 2:
                        act.wait_ge(output_read, n - 1)
                    nc.scalar.activation(spread[:, n % 2], p_t[:, ring(n, len(units[n]["blocks"]))],
                                         ACT.Copy).then_inc(spread_done, 1)

        @block.gpsimd
        def _(pool):
            layer.pool_start(pool)
            for n in range(len(units)):
                layer.pool_unit(pool, n)
                if layer.packed:
                    pool.wait_ge(weighed, n + 1)
                    if n >= 1:
                        pool.wait_ge(out_done, n)
                    nc.gpsimd.tensor_copy(lower[:], halves[HD:P, n % 2]).then_inc(lowered, 1)
                    pool.wait_ge(lowered, n + 1)
                    if n >= 2:
                        pool.wait_ge(stored[n % 2], 16 * (n // 2))
                    nc.gpsimd.tensor_tensor(ot[:, n % 2], halves[0:HD, n % 2], lower[:],
                                            ALU.add).then_inc(out_done, 1)


class Mla(Attention):
    scale = QK ** -0.5

    def __init__(self, qkT, va, oT):
        self.qkT, self.va, self.oT = qkT, va, oT
        self.of = [(h, NG - 1 - g if h % 2 else g) for h in range(H) for g in range(NG)]
        self.units = [dict(keys=[P * (NG * g + s + 1) for s in range(4)],
                           blocks=[(j, max(0, j - 4 * g)) for j in range(4 * g + 4)])
                      for _, g in self.of]

    def setup(self, nc, sem, ident, ctx, sems):
        sb = lambda n, s, d=F32: ctx.enter_context(nc.sbuf_tensor(f"mla_{n}", s, d))
        self.nc, self.sems = nc, sems
        self.q = [sb(f"q_{n}", [QK, 2, T], F32R) for n in ("hi", "lo")]
        self.k = [sb(f"k_{n}", [QK, 2, T], F32R) for n in ("hi", "lo")]
        self.v = sb("v", [P, 2, NT, P], F32R)
        self.none = sb("none", [P, GT])
        self.causal = sb("causal", [P, GT])
        self.qk_in, self.v_in = sem("mla_qk_in", 2), sem("mla_v_in", 2)
        self.bias_made = sem("mla_bias_made")

    def pool_start(self, pool):
        g = self.nc.gpsimd
        g.memset(self.none[:], 0.0)
        g.memset(self.causal[:], 0.0)
        pool.drain()
        g.affine_select(out=self.causal[:, GT - P:GT], in_=self.causal[:, GT - P:GT],
                        compare_op=ALU.is_ge, fill=NEG, base=0, pattern=[[-1, P]],
                        channel_multiplier=1).then_inc(self.bias_made, 1)

    def dve_start(self, dve):
        dve.wait_ge(self.bias_made, 1)

    def load(self, sp, n):
        h = n // NG
        if n % NG:
            return
        p = h % 2
        if h >= 2:
            sp.wait_ge(self.sems["multiplied"], self.sems["n_b"][NG * (h - 1)])
        for half in range(2):
            sp.dma_start(self.q[half][:, p].bitcast(F32), self.qkT[half, h]).then_inc(self.qk_in[p], 16)
            sp.dma_start(self.k[half][:, p].bitcast(F32), self.qkT[half, H + h]).then_inc(self.qk_in[p], 16)
        for half in range(2):
            sp.dma_start(self.v[:, p, :, half * HD:(half + 1) * HD].bitcast(F32),
                         self.va[half, :, h * HD:(h + 1) * HD].rearrange("(j p) d -> p j d", p=P))\
                .then_inc(self.v_in[p], 16)

    def wait_scores(self, pe, n):
        pe.wait_ge(self.qk_in[n // NG % 2], 64 * (n // NG // 2 + 1))

    def wait_values(self, pe, n):
        pe.wait_ge(self.v_in[n // NG % 2], 32 * (n // NG // 2 + 1))

    def scores(self, out, n, s, k0, w):
        p, t = n // NG % 2, self.of[n][1] * 4 + s
        q = [x[:, p, t * P:(t + 1) * P] for x in self.q]
        k = [x[:, p, k0:k0 + w] for x in self.k]
        return mm3(self.nc.tensor, out, q, k, start=True, stop=True)

    def bias(self, n, s, k0, w):
        if k0 + w == self.units[n]["keys"][s]:
            return self.causal[:, GT - w:GT]
        return self.none[:, 0:w]

    def values(self, n, j):
        return self.v[:, n // NG % 2, j]

    def store(self, n):
        h, g = self.of[n]
        return self.oT[h * HD:(h + 1) * HD, g * GT:(g + 1) * GT]

SENTINEL = -3.2e38
FUTURE = -3e38
HALVINGS = 10
WIDE = 2 * GT




def gate_chunks():
    return [(c0 + P * j, row + P * j, func, j if biased else None)
            for c0, row, func, count, biased in ((C_GA, 0, ACT.Silu, 4, False), (C_GB, 512, ACT.Silu, 4, False),
                                                 (C_MA, 1024, ACT.Sigmoid, 16, True))
            for j in range(count)]


LOADING = 1
PAIR = 1
AFTER_TOP = 12


def index_steps(tiles, chunks):
    total = NG * len(gate_chunks()) * KD
    keys = lambda t: P * (t + 1)
    late = tiles[LOADING:]
    paired = lambda t: int(PAIR * H * keys(t) / WIDE) + AFTER_TOP
    cost = {t: 11 * keys(t) / 960 + 14 for t in late}
    steps, given = [("W", 0), ("W", 1)], 0

    def give(count):
        nonlocal given
        for _ in range(min(count, total - given)):
            step, k = divmod(given, KD)
            steps.append(("G", step, k))
            given += 1
            if k == KD - 1 and step % NG == 0:
                n = step // NG + 1
                if 2 <= n < len(gate_chunks()):
                    steps.append(("W", n))

    whole, passed = sum(cost.values()), 0
    rest = total - sum(paired(t) for t in late)
    for t in tiles:
        for h in range(H):
            for k0, width in chunks(t):
                steps.append(("I", t, h, k0, width))
                if t in cost:
                    done = h * keys(t) + k0
                    give(int(PAIR * (done + width) / WIDE) - int(PAIR * done / WIDE))
                    if h * len(chunks(t)) + k0 // WIDE == 1:
                        give(AFTER_TOP)
        steps.append(("M", t))
        for i in range(HALVINGS):
            if t in cost:
                passed += cost[t] / HALVINGS
                seen = sum(paired(x) for x in late if x <= t)
                give(seen + int(rest * passed / whole + 0.5) - given)
            steps.append(("H", t, i))
        steps.append(("T", t))
    give(total)
    return steps


def stage_index(nc, sem, ident, qiT, kiT, wi, mask, h_dram, w_in, b_merge, gates):
    with ExitStack() as c:
        sb = lambda n, s, d=F32: c.enter_context(nc.sbuf_tensor(f"i_{n}", s, d))
        hT = [sb(f"hT_{n}", [P, KD, T], F32R) for n in ("hi", "lo")]
        ws = sb("ws", [P, KD, P])
        wh = sb("wh", [P, 2, KD, P], F32R)
        wl = sb("wl", [P, 2, KD, P], F32R)
        ob = sb("ob", [P, 2, GT])
        bias_m = sb("bias_m", [P, 16])
        q = sb("q", [P, 2, H, P], F32R)
        k = sb("k", [P, T], F32R)
        w = sb("w", [P, NT, H])
        relu = sb("relu", [P, 3, WIDE])
        score = sb("score", [P, 2, T + 8])
        above = sb("above", [P, T], BF16)
        bias = sb("bias", [P, T], BF16)
        halves = sb("halves", [P, HALVINGS + 1])
        steps8 = sb("steps8", [P, 8])
        lim = sb("lim", [P, 2])
        rng = sb("rng", [P, 1])
        mid = sb("mid", [P, 1])
        widths = sb("widths", [P, HALVINGS + 1])
        count = sb("count", [P, 1])
        side = sb("side", [P, 1])
        few = sb("few", [P, 1])
        off = sb("off", [P, 1])
        left = sb("left", [P, 1])
        rounds = sb("rounds", [1, 1])
        rounds_i = sb("rounds_i", [1, 1], I32)
        best = sb("best", [P, 8])
        taken = sb("taken", [P, 8])
        gone = sb("gone", [P, 8])
        p_s = c.enter_context(nc.psum_tensor("i_p_s", [P, 2, WIDE], F32))
        p_l = c.enter_context(nc.psum_tensor("i_p_l", [P, GT], F32))
        p_g = c.enter_context(nc.psum_tensor("i_p_g", [P, 3, GT], F32))
        k_in, stored, bias_in, w_loaded, w_hi, w_split, filled, evacuated = (
            sem(f"i_{n}") for n in ("k_in", "stored", "bias_in", "w_loaded", "w_hi", "w_split", "filled",
                                    "evacuated"))
        q_in, h_in, g_stored = sem("i_q_in", 2), sem("i_h_in", NG), sem("i_g_stored", 2)
        consts, scored, relued, summed, masked, counted, turned, made, fixed = (
            sem(f"i_{n}") for n in ("consts", "scored", "relued", "summed", "masked", "counted", "turned",
                                    "made", "fixed"))
        block = c.enter_context(nc.Block())

        def chunks(t):
            keys = P * (t + 1)
            return [(k0, min(WIDE, keys - k0)) for k0 in range(0, keys, WIDE)]

        tiles = range(TOPK // P, NT)
        steps = index_steps(tiles, chunks)
        wanted = gate_chunks()
        n_at, n = {}, 0
        for t in tiles:
            n_at[t] = n
            n += H * len(chunks(t))
        n_at[NT] = n

        @block.sync
        def _(sp):
            def load(n):
                if n >= 1:
                    sp.wait_ge(w_split, n)
                c0 = wanted[n][0]
                sp.dma_start(ws[:], w_in[:, c0:c0 + P].rearrange("(k p) n -> p k n", p=P)).then_inc(w_loaded, 16)

            load(0)
            sp.dma_start(bias_m[:], b_merge.rearrange("(j p) -> p j", p=P),
                         allow_slow_non_contiguous=True).then_inc(bias_in, 16)
            for g in range(NG):
                s = slice(g * GT, (g + 1) * GT)
                for half in range(2):
                    sp.dma_start(hT[half][:, :, s].bitcast(F32), h_dram[half, :, :, s]).then_inc(h_in[g], 16)
                if g == 0:
                    load(1)
            for u in range(NG * len(wanted)):
                n, g = divmod(u, NG)
                if g == 0 and 1 <= n < len(wanted) - 1:
                    load(n + 1)
                row = wanted[n][1]
                sp.wait_ge(evacuated, u + 1)
                sp.dma_start(gates[row:row + P, g * GT:(g + 1) * GT], ob[:, u % 2]).then_inc(g_stored[u % 2], 16)
            for p in range(2):
                sp.wait_ge(g_stored[p], 16 * (NG * len(wanted) // 2))

        @block.tensor
        def _(pe):
            pe.wait_ge(k_in, 80)
            n = 0
            for step in steps:
                if step[0] == "I":
                    _, t, h, k0, width = step
                    if h == 0 and k0 == 0:
                        pe.wait_ge(q_in[t % 2], 64 * ((t - tiles[0]) // 2 + 1))
                    if n >= 2:
                        pe.wait_ge(relued, n - 1)
                    for x in range(0, width, GT):
                        y = min(GT, width - x)
                        last = nc.tensor.matmul(p_s[:, n % 2, x:x + y], q[:, t % 2, h],
                                                k[:, k0 + x:k0 + x + y], start=True, stop=True)
                    last.then_inc(scored, 1)
                    n += 1
                elif step[0] == "T":
                    pe.wait_ge(counted, step[1] - tiles[0] + 1)
                    nc.tensor.transpose(p_l[0:1, 0:P], left[:], ident[:]).then_inc(turned, 1)
                elif step[0] == "G":
                    _, u, b = step
                    chunk, g = divmod(u, NG)
                    if b == 0:
                        pe.wait_ge(w_split, chunk + 1)
                        pe.wait_ge(h_in[g], 32)
                        if u >= 3:
                            pe.wait_ge(evacuated, u - 2)
                    s = slice(g * GT, (g + 1) * GT)
                    last = mm3(nc.tensor, p_g[:, u % 3], (wh[:, chunk % 2, b], wl[:, chunk % 2, b]),
                               [x[:, b, s] for x in hT], start=b == 0, stop=b == KD - 1)
                    if b == KD - 1:
                        last.then_inc(filled, 1)

        @block.scalar
        def _(act):
            act.wait_ge(bias_in, 16)
            n = 0
            for step in steps:
                if step[0] == "I":
                    width = step[4]
                    act.wait_ge(scored, n + 1)
                    if n >= 3:
                        act.wait_ge(summed, n - 2)
                    nc.scalar.activation(relu[:, n % 3, 0:width], p_s[:, n % 2, 0:width],
                                         ACT.Relu).then_inc(relued, 1)
                    n += 1
                elif step[0] == "W":
                    chunk = step[1]
                    act.wait_ge(w_loaded, 16 * (chunk + 1))
                    if chunk >= 2:
                        act.wait_ge(filled, NG * (chunk - 1))
                    nc.scalar.activation(wh[:, chunk % 2], ws[:], ACT.Copy).then_inc(w_hi, 1)
                elif step[0] == "G" and step[2] == KD - 1:
                    u = step[1]
                    _, _, func, bias_col = wanted[u // NG]
                    act.wait_ge(filled, u + 1)
                    if u >= 2:
                        act.wait_ge(g_stored[u % 2], 16 * (u // 2))
                    if bias_col is None:
                        nc.scalar.activation(ob[:, u % 2], p_g[:, u % 3], func).then_inc(evacuated, 1)
                    else:
                        nc.scalar.activation(ob[:, u % 2], p_g[:, u % 3], func,
                                             bias=bias_m[:, bias_col:bias_col + 1]).then_inc(evacuated, 1)

        @block.gpsimd
        def _(pool):
            def load(t):
                for r in range(4):
                    src = qiT[r // 2].rearrange("j (r d) t -> d (j r) t", d=IDX)
                    pool.dma_start(q[IDX * r:IDX * (r + 1), t % 2].bitcast(F32),
                                   src[:, :, t * P:(t + 1) * P]).then_inc(q_in[t % 2], 16)

            load(tiles[0])
            pool.dma_start(w[:], wi.rearrange("(t p) h -> p t h", p=P)).then_inc(k_in, 16)
            for r in range(4):
                pool.dma_start(k[IDX * r:IDX * (r + 1)].bitcast(F32), kiT[r % 2]).then_inc(k_in, 16)
            load(tiles[1])
            nc.gpsimd.iota(steps8[:], pattern=[[1, 8]], base=0, channel_multiplier=0,
                           allow_small_or_imprecise_dtypes=True).then_inc(consts, 1)
            for t in range(NT):
                keys = P * (t + 1)
                if t in n_at:
                    pool.wait_ge(summed, n_at[t + 1])
                    d = score[:, t % 2, keys - P:keys]
                    nc.gpsimd.affine_select(out=d, in_=d, compare_op=ALU.is_ge, fill=FUTURE, base=0,
                                            pattern=[[-1, P]], channel_multiplier=1).then_inc(masked, 1)
                    if t + 2 < NT:
                        load(t + 2)
                    pool.wait_ge(made, t - tiles[0] + 1)
                else:
                    if t >= 1:
                        pool.wait_ge(stored, 16 * t)
                    nc.gpsimd.memset(bias[:, 0:keys], 0.0)
                    pool.drain()
                d = bias[:, keys - P:keys]
                nc.gpsimd.affine_select(out=d, in_=d, compare_op=ALU.is_ge, fill=NEG, base=0,
                                        pattern=[[-1, P]], channel_multiplier=1).then_inc(fixed, 1)
                pool.wait_ge(fixed, t + 1)
                pool.dma_start(mask[t * P:(t + 1) * P, 0:keys], bias[:, 0:keys]).then_inc(stored, 16)
            pool.wait_ge(stored, 16 * NT)

        @block.vector
        def _(dve):
            for i in range(HALVINGS + 1):
                nc.vector.memset(halves[:, i:i + 1], 2.0 ** -(i + 1))
            dve.wait_ge(k_in, 80)
            dve.wait_ge(consts, 1)
            n = 0
            for step in steps:
                if step[0] == "W":
                    chunk = step[1]
                    dve.wait_ge(w_hi, chunk + 1)
                    nc.vector.tensor_tensor(wl[:, chunk % 2], ws[:], wh[:, chunk % 2].bitcast(F32),
                                            ALU.subtract).then_inc(w_split, 1)
                    continue
                if step[0] == "G":
                    continue
                t = step[1]
                keys = P * (t + 1)
                s = score[:, t % 2, 0:keys]
                if step[0] == "I":
                    _, _, h, k0, width = step
                    dve.wait_ge(relued, n + 1)
                    r, acc = relu[:, n % 3, 0:width], score[:, t % 2, k0:k0 + width]
                    if h == 0:
                        nc.vector.tensor_scalar(acc, r, w[:, t, 0:1], None, ALU.mult).then_inc(summed, 1)
                    else:
                        dve.wait_ge(summed, n + 1 - len(chunks(t)))
                        nc.vector.scalar_tensor_tensor(out=acc, in0=r, scalar=w[:, t, h:h + 1], in1=acc,
                                                       op0=ALU.mult, op1=ALU.add).then_inc(summed, 1)
                    n += 1
                elif step[0] == "M":
                    dve.wait_ge(masked, t - tiles[0] + 1)
                    sample = score[:, t % 2, 0:keys - P:(keys - P) // 256]
                    nc.vector.tensor_reduce(lim[:, 0:1], sample, AX.X, ALU.max)
                    nc.vector.tensor_reduce(lim[:, 1:2], sample, AX.X, ALU.min)
                    dve.drain()
                    nc.vector.tensor_tensor(rng[:], lim[:, 0:1], lim[:, 1:2], ALU.subtract)
                    dve.drain()
                    nc.vector.tensor_scalar(widths[:], halves[:], rng[:], 1.25, ALU.mult, ALU.mult)
                    dve.drain()
                    nc.vector.tensor_tensor(mid[:], lim[:, 0:1], widths[:, 0:1], ALU.subtract)
                    dve.drain()
                elif step[0] == "H":
                    i = step[2]
                    nc.vector.tensor_scalar(above[:, 0:keys], s, mid[:], None, ALU.is_ge, ALU.add,
                                            accum_out=count[:])
                    dve.drain()
                    nc.vector.tensor_scalar(side[:], count[:], TOPK - 0.5, 0.5, ALU.is_ge, ALU.subtract)
                    dve.drain()
                    nc.vector.scalar_tensor_tensor(out=mid[:], in0=side[:], scalar=widths[:, i:i + 1],
                                                   in1=mid[:], op0=ALU.mult, op1=ALU.add)
                    dve.drain()
                elif step[0] == "T":
                    nc.vector.tensor_tensor(mid[:], mid[:], widths[:, HALVINGS - 1:HALVINGS], ALU.add)
                    dve.drain()
                    nc.vector.tensor_scalar(above[:, 0:keys], s, mid[:], None, ALU.is_ge, ALU.add,
                                            accum_out=count[:])
                    dve.drain()
                    nc.vector.tensor_scalar(few[:], count[:], TOPK - 0.5, None, ALU.is_lt)
                    dve.drain()
                    nc.vector.tensor_scalar(off[:], few[:], NEG, None, ALU.mult)
                    nc.vector.tensor_tensor(left[:], few[:], count[:], ALU.mult)
                    dve.drain()
                    nc.vector.tensor_scalar(left[:], left[:], -1.0, float(TOPK), ALU.mult, ALU.add)\
                        .then_inc(counted, 1)
                    nc.vector.scalar_tensor_tensor(out=s, in0=above[:, 0:keys], scalar=off[:], in1=s,
                                                   op0=ALU.mult, op1=ALU.add)
                    dve.wait_ge(turned, t - tiles[0] + 1)
                    nc.vector.tensor_reduce(rounds[:], p_l[0:1, 0:P], AX.X, ALU.max)
                    dve.drain()
                    nc.vector.tensor_scalar(rounds[:], rounds[:], 3.5, 0.125, ALU.add, ALU.mult)
                    dve.drain()
                    nc.vector.tensor_scalar(rounds[:], rounds[:], ROUNDER, None, ALU.add)
                    dve.drain()
                    nc.vector.tensor_scalar(rounds[:], rounds[:], ROUNDER, None, ALU.subtract)
                    dve.drain()
                    nc.vector.tensor_copy(rounds_i[:], rounds[:])
                    dve.drain()
                    n_rounds = dve.value_load(rounds_i[0:1, 0:1], min_val=1, max_val=TOPK // 8)
                    whole = score[:, t % 2, 0:keys + 8]
                    with dve.Fori(0, n_rounds) as _i:
                        nc.vector.memset(score[:, t % 2, keys:keys + 8], SENTINEL)
                        nc.vector.max(out=best[:], in_=s)
                        nc.vector.tensor_scalar(taken[:], steps8[:], left[:], None, ALU.is_lt)
                        dve.drain()
                        nc.vector.tensor_scalar(left[:], left[:], 8.0, None, ALU.subtract)
                        nc.vector.tensor_tensor(best[:], best[:], taken[:], ALU.mult)
                        nc.vector.tensor_scalar(gone[:], taken[:], 1.0, -SENTINEL, ALU.subtract, ALU.mult)
                        dve.drain()
                        nc.vector.tensor_tensor(best[:], best[:], gone[:], ALU.add)
                        dve.drain()
                        nc.vector.match_replace(out=whole, in_to_replace=best[:], in_values=whole, imm_value=NEG)
                        dve.drain()
                    dve.wait_ge(stored, 16 * t)
                    nc.vector.tensor_scalar(bias[:, 0:keys], s, NEG / 2, NEG, ALU.is_ge,
                                            ALU.mult).then_inc(made, 1)


class Dsa(Attention):
    scale = HD ** -0.5

    def __init__(self, qbT, kbT, vb, mask, oT):
        self.qbT, self.kbT, self.vb, self.mask, self.oT = qbT, kbT, vb, mask, oT
        self.units = [dict(keys=[P * (t + 1)] * 4, blocks=[(j, 0) for j in range(t + 1)])
                      for t in range(NT) for g in range(KV)]

    def setup(self, nc, sem, ident, ctx, sems):
        sb = lambda n, s, d=F32: ctx.enter_context(nc.sbuf_tensor(f"dsa_{n}", s, d))
        self.nc, self.sems = nc, sems
        self.q = sb("q", [P, 2, H, P], F32R)
        self.k_hi = sb("k_hi", [P, KV, T], F32R)
        self.k_lo = sb("k_lo", [HD, KV, T], F32R)
        self.v = sb("v", [P, NT, KV, P], F32R)
        self.m = sb("mask", [P, 2, T], BF16)
        self.q_in, self.m_in = sem("dsa_q_in", 2), sem("dsa_m_in", 2)
        self.k_in, self.v_in = sem("dsa_k_in"), sem("dsa_v_in")

    def pe_start(self, pe):
        pe.wait_ge(self.k_in, 16 * 3)

    def load(self, sp, n):
        t, g = n // KV, n % KV
        if g:
            return
        if t >= 2:
            sp.wait_ge(self.sems["moved"], self.sems["n_s"][KV * (t - 1)])
        at = slice(t * P, (t + 1) * P)
        for half in range(2):
            sp.dma_start(self.q[half * HD:(half + 1) * HD, t % 2].bitcast(F32),
                         self.qbT[half].rearrange("j (r d) t -> d (j r) t", d=HD)[:, :, at])\
                .then_inc(self.q_in[t % 2], 16)
        keys = P * (t + 1)
        sp.dma_start(self.m[:, t % 2, 0:keys], self.mask[at, 0:keys]).then_inc(self.m_in[t % 2], 16)
        if n == 0:
            k = [self.kbT[half].rearrange("(g d) t -> d g t", d=HD) for half in range(2)]
            for dst, src in ((self.k_hi[0:HD], k[0]), (self.k_hi[HD:P], k[0]), (self.k_lo[:], k[1])):
                sp.dma_start(dst.bitcast(F32), src).then_inc(self.k_in, 16)
            for half in range(2):
                for g in range(KV):
                    sp.dma_start(self.v[:, :, g, half * HD:(half + 1) * HD].bitcast(F32),
                                 self.vb[half, :, g * HD:(g + 1) * HD].rearrange("(j p) d -> p j d", p=P))\
                        .then_inc(self.v_in, 16)

    def wait_scores(self, pe, n):
        pe.wait_ge(self.q_in[n // KV % 2], 32 * (n // KV // 2 + 1))

    def wait_values(self, pe, n):
        if n == 0:
            pe.wait_ge(self.v_in, 16 * 4)

    def wait_bias(self, dve, n, s):
        dve.wait_ge(self.m_in[n // KV % 2], 16 * (n // KV // 2 + 1))

    def scores(self, out, n, s, k0, w):
        t, g = n // KV, n % KV
        q = self.q[:, t % 2, 4 * g + s]
        self.nc.tensor.matmul(out, q, self.k_hi[:, g, k0:k0 + w], start=True, stop=False)
        return self.nc.tensor.matmul(out, q[0:HD], self.k_lo[:, g, k0:k0 + w], start=False, stop=True)

    def bias(self, n, s, k0, w):
        return self.m[:, n // KV % 2, k0:k0 + w]

    def values(self, n, j):
        return self.v[:, j, n % KV]

    def store(self, n):
        t, g = n // KV, n % KV
        rows = self.oT[g * 4 * HD:(g + 1) * 4 * HD, t * P:(t + 1) * P]
        return rows.rearrange("(h d) t -> d h t", d=HD)


def t5_one_hot():
    out = np.zeros((32, 3 * P), np.float32)
    for dist in range(WINDOW):
        if dist < 16:
            bucket = dist
        else:
            ratio = np.log(np.float32(dist) / np.float32(16)) / np.float32(math.log(8.0))
            bucket = min(31, 16 + int(np.float32(ratio) * np.float32(16)))
        out[bucket, 2 * P - 1 - dist] = 1.0
    return out


class BiasJob:

    def __init__(self, one_hot, table, spread):
        self.one_hot, self.table, self.spread = one_hot, table, spread

    def setup(self, nc, ctx):
        sb = lambda n, s: ctx.enter_context(nc.sbuf_tensor(f"t_{n}", s, F32))
        self.nc = nc
        self.row = sb("row", [WH, 3 * P])
        self.stored = nc.alloc_semaphore(name="t_stored")

    def start(self, sem, hot, tab, ps):
        self.hot, self.tab, self.ps = hot, tab, ps
        self.loaded, self.product, self.filled = (sem(f"t_{n}") for n in ("loaded", "product", "filled"))

    def sync(self, sp):
        sp.dma_start(self.hot[:], self.one_hot).then_inc(self.loaded, 16)
        sp.dma_start(self.tab[:], self.table).then_inc(self.loaded, 16)
        sp.wait_ge(self.filled, 2)
        sp.dma_start(self.spread, self.row[:].unsqueeze(1).broadcast_to([WH, P, 3 * P]))\
            .then_inc(self.stored, 16)

    def finish(self, sp):
        sp.wait_ge(self.stored, 16)

    def tensor(self, pe):
        pe.wait_ge(self.loaded, 32)
        self.nc.tensor.matmul(self.ps[:], self.tab[:], self.hot[:], start=True, stop=True)\
            .then_inc(self.product, 1)

    def vector(self, dve):
        v = self.nc.vector
        v.memset(self.row[:], NEG).then_inc(self.filled, 1)
        dve.wait_ge(self.filled, 1)
        dve.wait_ge(self.product, 1)
        v.tensor_scalar(self.row[:, P:2 * P], self.ps[:, P:2 * P], 1 / Window.scale, None, ALU.mult)\
            .then_inc(self.filled, 1)


class Window(Attention):
    scale = HD ** -0.5
    width = 2 * P
    depth = 3
    ahead = 6
    lead = 3
    split_ring = 3
    lag = 2
    output_late = 2
    packed = False
    batched = True

    def __init__(self, qT, kT, v, spread, sinks, oT):
        self.qT, self.kT, self.v_dram, self.spread, self.sinks, self.oT = qT, kT, v, spread, sinks, oT
        self.units = [dict(keys=[P * min(2, t + 1)] * 4, blocks=[(j, 0) for j in range(min(2, t + 1))])
                      for t in range(NT) for g in range(WKV)]

    def setup(self, nc, sem, ident, ctx, sems):
        sb = lambda n, s, d=F32: ctx.enter_context(nc.sbuf_tensor(f"win_{n}", s, d))
        self.nc, self.sems = nc, sems
        self.q_raw = sb("q_raw", [P, 2, WH, P])
        self.k_raw = sb("k_raw", [P, 2, WKV, P])
        self.v_raw = sb("v_raw", [P, 2, WKV * HD])
        self.q = sb("q", [P, 2, WH, P], F32R)
        self.k_hi = sb("k_hi", [P, WKV, 4, P], F32R)
        self.k_lo = sb("k_lo", [HD, WKV, 4, P], F32R)
        self.v = sb("v", [P, 4, WKV, P], F32R)
        self.b = sb("bias", [P, WH, 2 * P])
        self.sink8 = sb("sink8", [P, WH])
        self.sink_arg = sb("sink_arg", [P, self.depth, 4])
        self.e_sink = sb("e_sink", [P, self.depth, 4])
        self.tile_in = sem("win_tile_in", 2)
        self.const_in, self.sink_shifted, self.kv_split, self.q_hi = (
            sem(f"win_{n}") for n in ("const_in", "sink_shifted", "kv_split", "q_hi"))

    def load(self, sp, n):
        t, g = n // WKV, n % WKV
        if g:
            return
        at = slice(t * P, (t + 1) * P)
        if t >= 2:
            sp.wait_ge(self.kv_split, t - 1)
        done = self.tile_in[t % 2]
        for rows in (slice(0, HD), slice(HD, P)):
            sp.dma_start(self.q_raw[rows, t % 2],
                         self.qT.rearrange("(h d) t -> d h t", d=HD)[:, :, at]).then_inc(done, 16)
            sp.dma_start(self.k_raw[rows, t % 2],
                         self.kT.rearrange("(h d) t -> d h t", d=HD)[:, :, at]).then_inc(done, 16)
        sp.dma_start(self.v_raw[:, t % 2], self.v_dram[at, :]).then_inc(done, 16)
        if n == 0:
            sp.dma_start(self.sink8[:], self.sinks.partition_broadcast(P)).then_inc(self.const_in, 16)
            flat = self.spread.rearrange("h r u -> h (r u)")[:, P - 1:P - 1 + P * (3 * P - 1)]
            toeplitz = flat.rearrange("h (q u) -> q h u", u=3 * P - 1)[:, :, 0:2 * P]
            sp.dma_start(self.b[:], toeplitz).then_inc(self.const_in, 16)

    def pool_start(self, pool):
        self.split_tile(pool, 0)

    def pool_unit(self, pool, n):
        if n % WKV == 0 and n // WKV + 1 < NT:
            self.split_tile(pool, n // WKV + 1)

    def split_tile(self, pool, t):
        p, r = t % 2, t % 4
        pool.wait_ge(self.tile_in[p], 80 * (t // 2 + 1))
        if t >= 4:
            pool.wait_ge(self.sems["multiplied"], self.sems["n_b"][WKV * (t - 2)])
        v_raw = self.v_raw[:, p].rearrange("p (g d) -> p g d", d=HD)
        g = self.nc.gpsimd
        g.tensor_copy(self.k_hi[:, :, r], self.k_raw[:, p])
        g.tensor_copy(self.v[:, r, :, 0:HD], v_raw)
        pool.drain()
        g.tensor_tensor(self.k_lo[:, :, r], self.k_raw[0:HD, p], self.k_hi[0:HD, :, r].bitcast(F32),
                        ALU.subtract)
        pool.drain()
        g.tensor_tensor(self.v[:, r, :, HD:P], v_raw, self.v[:, r, :, 0:HD].bitcast(F32), ALU.subtract)
        pool.drain()
        pool.wait_ge(self.q_hi, t + 1)
        g.tensor_tensor(self.q[HD:P, p], self.q_raw[HD:P, p], self.q[HD:P, p].bitcast(F32),
                        ALU.subtract).then_inc(self.kv_split, 1)
        pool.drain()

    def dve_start(self, dve):
        dve.wait_ge(self.const_in, 32)
        self.nc.vector.tensor_scalar(self.sink8[:], self.sink8[:], 1 / self.scale, None,
                                     ALU.mult)
        dve.drain()

    def act_start(self, act):
        self.round_queries(act, 0)

    def round_queries(self, act, t):
        p = t % 2
        act.wait_ge(self.tile_in[p], 80 * (t // 2 + 1))
        if t >= 2:
            act.wait_ge(self.sems["moved"], self.sems["n_s"][WKV * (t - 1)])
        self.nc.scalar.activation(self.q[:, p], self.q_raw[:, p], ACT.Copy).then_inc(self.q_hi, 1)

    def act_sub(self, act, n, s, shift):
        if n % WKV == 2 and s == 0 and n // WKV + 1 < NT:
            self.round_queries(act, n // WKV + 1)
        if s == 0:
            if n >= self.depth:
                act.wait_ge(self.sems["inverted"], n - self.depth + 1)
            act.wait_ge(self.sink_shifted, n + 1)
            self.nc.scalar.activation(self.e_sink[:, n % self.depth], self.sink_arg[:, n % self.depth], ACT.Exp)

    def shift_made(self, dve, n, shift):
        h = 4 * (n % WKV)
        dve.drain()
        self.nc.vector.scalar_tensor_tensor(out=self.sink_arg[:, n % self.depth], in0=self.sink8[:, h:h + 4],
                                            scalar=self.scale, in1=shift, op0=ALU.mult,
                                            op1=ALU.add).then_inc(self.sink_shifted, 1)

    def least_max(self, n, s):
        h = 4 * (n % WKV) + s
        return self.sink8[:, h:h + 1]

    def add_sinks(self, dve, n, sums):
        self.nc.vector.tensor_tensor(sums, sums, self.e_sink[:, n % self.depth], ALU.add)
        dve.drain()

    def wait_scores(self, pe, n):
        pe.wait_ge(self.kv_split, n // WKV + 1)

    def wait_values(self, pe, n): ...

    def scores(self, out, n, s, k0, w):
        t, g = n // WKV, n % WKV
        q = self.q[:, t % 2, 4 * g + s]
        first = (t - w // P + 1) % 4
        runs = [(first, w // P)] if first + w // P <= 4 else [(3, 1), (0, 1)]
        at = 0
        for r, tiles in runs:
            o = out[:, at:at + tiles * P]
            hi = self.k_hi[:, g, r:r + tiles].rearrange("p r t -> p (r t)")
            lo = self.k_lo[:, g, r:r + tiles].rearrange("p r t -> p (r t)")
            self.nc.tensor.matmul(o, q, hi, start=True, stop=False)
            last = self.nc.tensor.matmul(o, q[0:HD], lo, start=False, stop=True)
            at += tiles * P
        return last

    def bias(self, n, s, k0, w):
        return self.b[:, 4 * (n % WKV) + s, 2 * P - w:2 * P]

    def values(self, n, j):
        t, g = n // WKV, n % WKV
        return self.v[:, (t - len(self.units[n]["blocks"]) + 1 + j) % 4, g]

    def store(self, n):
        t, g = n // WKV, n % WKV
        rows = self.oT[g * 4 * HD:(g + 1) * 4 * HD, t * P:(t + 1) * P]
        return rows.rearrange("(h d) t -> d h t", d=HD)


def stage_branch(nc, sem, oaT, obT, gates, w_mla, w_dsa, mergedT):
    KO = 4
    WCOLS = 256
    with ExitStack() as c:
        sb = lambda n, s, d=F32: c.enter_context(nc.sbuf_tensor(f"m_{n}", s, d))
        raw = sb("raw", [P, 2, KO, D])
        w = [[sb(f"w{x}_{n}", [P, KO, D], F32R) for n in ("hi", "lo")] for x in "ab"]
        o = sb("o", [P, 2, KO, GT])
        gate = sb("gate", [P, 2, KO, GT])
        oh = sb("oh", [P, 2, KO, GT], F32R)
        ol = sb("ol", [P, 2, KO, GT], F32R)
        m = sb("m", [P, 2, 2, GT])
        part = sb("part", [P, 2, GT])
        total = sb("total", [P, 2, GT])
        ps = c.enter_context(nc.psum_tensor("m_ps", [P, 4, 2, GT], F32))
        w_in = sem("m_w_in", D // WCOLS)
        o_in, m_in, stored = sem("m_o_in", 2), sem("m_m_in", 2), sem("m_stored", 2)
        w_hi, w_lo, gated, hi_done, lo_done, filled, weighed, added = (
            sem(f"m_{n}") for n in ("w_hi", "w_lo", "gated", "hi_done", "lo_done", "filled", "weighed",
                                    "added"))
        block = c.enter_context(nc.Block())
        view = lambda x: x.rearrange("(k p) t -> p k t", p=P)
        tok = lambda g: slice(g * GT, (g + 1) * GT)

        @block.sync
        def _(sp):
            def load_weights(piece):
                cols = slice(piece * WCOLS, (piece + 1) * WCOLS)
                for x, src in enumerate((w_mla, w_dsa)):
                    sp.dma_start(raw[:, x, :, cols], view(src)[:, :, cols]).then_inc(w_in[piece], 16)

            def load(g):
                for x, src in enumerate((oaT, obT)):
                    if g:
                        sp.wait_ge(lo_done, 2 * g - 1 + x)
                    sp.dma_start(o[:, x], view(src)[:, :, tok(g)]).then_inc(o_in[x], 16)
                    sp.dma_start(gate[:, x], view(gates[x * 512:(x + 1) * 512])[:, :, tok(g)])\
                        .then_inc(o_in[x], 16)

            def load_m(n):
                g, f = n // KD, n % KD
                if n >= 2:
                    sp.wait_ge(weighed, 2 * (n - 1))
                for x in range(2):
                    r = 1024 * (x + 1) + f * P
                    sp.dma_start(m[:, n % 2, x], gates[r:r + P, tok(g)]).then_inc(m_in[n % 2], 16)

            def store(n):
                g, f = n // KD, n % KD
                sp.wait_ge(added, n + 1)
                sp.dma_start(mergedT[f * P:(f + 1) * P, tok(g)], total[:, n % 2]).then_inc(stored[n % 2], 16)

            load_weights(0)
            load(0)
            load_m(0)
            for piece in range(1, D // WCOLS):
                load_weights(piece)
            for n in range(NG * KD):
                if n % KD == 0 and n // KD + 1 < NG:
                    load(n // KD + 1)
                if n + 1 < NG * KD:
                    load_m(n + 1)
                store(n)
            for p in range(2):
                sp.wait_ge(stored[p], 16 * (NG * KD // 2))

        @block.scalar
        def _(act):
            def round_weights(piece):
                cols = slice(piece * WCOLS, (piece + 1) * WCOLS)
                act.wait_ge(w_in[piece], 32)
                for x in range(2):
                    nc.scalar.activation(w[x][0][:, :, cols], raw[:, x, :, cols], ACT.Copy).then_inc(w_hi, 1)

            round_weights(0)
            for g in range(NG):
                if g == 1:
                    for piece in range(1, D // WCOLS):
                        round_weights(piece)
                for x in range(2):
                    act.wait_ge(gated, 2 * g + x + 1)
                    if g:
                        act.wait_ge(filled, 2 * KD * (g - 1) + 2 * KD)
                    nc.scalar.activation(oh[:, x], o[:, x], ACT.Copy).then_inc(hi_done, 1)

        @block.gpsimd
        def _(pool):
            for g in range(NG):
                for x in range(2):
                    pool.wait_ge(hi_done, 2 * g + x + 1)
                    nc.gpsimd.tensor_tensor(ol[:, x], o[:, x], oh[:, x].bitcast(F32),
                                            ALU.subtract).then_inc(lo_done, 1)

        @block.vector
        def _(dve):
            def gated_group(g):
                for x in range(2):
                    dve.wait_ge(o_in[x], 32 * (g + 1))
                    nc.vector.tensor_tensor(o[:, x], o[:, x], gate[:, x], ALU.mult).then_inc(gated, 1)

            def split_weights(piece):
                cols = slice(piece * WCOLS, (piece + 1) * WCOLS)
                for x in range(2):
                    dve.wait_ge(w_hi, 2 * piece + x + 1)
                    nc.vector.tensor_tensor(w[x][1][:, :, cols], raw[:, x, :, cols],
                                            w[x][0][:, :, cols].bitcast(F32), ALU.subtract).then_inc(w_lo, 1)

            split_weights(0)
            gated_group(0)
            for piece in range(1, D // WCOLS):
                split_weights(piece)
            for n in range(NG * KD):
                g = n // KD
                if n % KD == 2 and g + 1 < NG:
                    gated_group(g + 1)
                dve.wait_ge(m_in[n % 2], 32 * (n // 2 + 1))
                if n:
                    dve.wait_ge(added, n)
                for x in range(2):
                    dve.wait_ge(filled, 2 * n + x + 1)
                    nc.vector.tensor_tensor(part[:, x], ps[:, n % 4, x], m[:, n % 2, x],
                                            ALU.mult).then_inc(weighed, 1)
                dve.wait_ge(weighed, 2 * n + 2)
                if n >= 2:
                    dve.wait_ge(stored[n % 2], 16 * (n // 2))
                nc.vector.tensor_tensor(total[:, n % 2], part[:, 0], part[:, 1], ALU.add).then_inc(added, 1)

        @block.tensor
        def _(pe):
            for n in range(NG * KD):
                g, f = n // KD, n % KD
                if g == 0:
                    pe.wait_ge(w_lo, 2 * (f * P // WCOLS) + 2)
                if n >= 4:
                    pe.wait_ge(weighed, 2 * (n - 3))
                for x in range(2):
                    if f == 0:
                        pe.wait_ge(lo_done, 2 * g + x + 1)
                    for k in range(KO):
                        cols = slice(f * P, (f + 1) * P)
                        last = mm3(nc.tensor, ps[:, n % 4, x], [y[:, k, cols] for y in w[x]],
                                   (oh[:, x, k], ol[:, x, k]), start=k == 0, stop=k == KO - 1)
                    last.then_inc(filled, 1)


def stage_out(nc, sem, tag, actT, gateT, weight, residual, out, final_gain=None):
    GO = 2 * P
    with ExitStack() as c:
        sb = lambda n, s, d=F32: c.enter_context(nc.sbuf_tensor(f"{tag}_{n}", s, d))
        raw = sb("raw", [P, 4, D])
        w = [sb(f"w_{n}", [P, KD, D], F32R) for n in ("hi", "lo")]
        a = sb("a", [P, 2, KD, GO])
        gate = sb("gate", [P, KD, GO]) if gateT is not None else None
        ah = sb("ah", [P, 2, KD, GO], F32R)
        al = sb("al", [P, 2, KD, GO], F32R)
        x = sb("x", [P, 2, D])
        y = sb("y", [P, 2, D])
        if final_gain is not None:
            gain = sb("gain", [P, D])
            junk = sb("junk", [P, D])
            ss, ms, sd, rs = (sb(n, [P, NT]) for n in ("ss", "ms", "sd", "rs"))
        ps = c.enter_context(nc.psum_tensor(f"{tag}_ps", [P, 4, 2, GT], F32))
        w_in = sem(f"{tag}_w_in", 4)
        a_in, x_in, stored = (sem(f"{tag}_{n}", 2) for n in ("a_in", "x_in", "stored"))
        gate_in, gain_in, w_hi, w_lo, gated, hi_done, lo_done, filled, added, squared, meaned, rooted, done = (
            sem(f"{tag}_{n}") for n in ("gate_in", "gain_in", "w_hi", "w_lo", "gated", "hi_done", "lo_done",
                                        "filled", "added", "squared", "meaned", "rooted", "done"))
        block = c.enter_context(nc.Block())
        view = lambda z: z.rearrange("(k p) t -> p k t", p=P)
        n_groups = T // GO

        @block.sync
        def _(sp):
            def load(g):
                s = slice(g * GO, (g + 1) * GO)
                if g >= 2:
                    sp.wait_ge(lo_done, g - 1)
                sp.dma_start(a[:, g % 2], view(actT)[:, :, s]).then_inc(a_in[g % 2], 16)
                if gate is not None:
                    if g >= 1:
                        sp.wait_ge(gated, g)
                    sp.dma_start(gate[:], view(gateT)[:, :, s]).then_inc(gate_in, 16)

            def load_x(t):
                if t >= 2:
                    sp.wait_ge(added, t - 1)
                sp.dma_start(x[:, t % 2], residual[t * P:(t + 1) * P, :]).then_inc(x_in[t % 2], 16)

            load(0)
            for k in range(KD):
                if k >= 4:
                    sp.wait_ge(w_lo, k - 3)
                sp.dma_start(raw[:, k % 4], weight[k * P:(k + 1) * P, :]).then_inc(w_in[k % 4], 16)
            load(1)
            if final_gain is not None:
                sp.dma_start(gain[:], final_gain.partition_broadcast(P)).then_inc(gain_in, 16)
            load_x(0)
            load_x(1)
            for t in range(NT):
                if t % 2 == 0 and t // 2 + 2 < n_groups:
                    load(t // 2 + 2)
                sp.wait_ge(done, t + 1)
                sp.dma_start(out[t * P:(t + 1) * P, :], y[:, t % 2]).then_inc(stored[t % 2], 16)
                if t + 2 < NT:
                    load_x(t + 2)
            for p in range(2):
                sp.wait_ge(stored[p], 16 * (NT // 2))

        @block.gpsimd
        def _(pool):
            for g in range(n_groups):
                pool.wait_ge(hi_done, g + 1)
                if g >= 2:
                    pool.wait_ge(filled, 4 * (g - 1))
                nc.gpsimd.tensor_tensor(al[:, g % 2], a[:, g % 2], ah[:, g % 2].bitcast(F32),
                                        ALU.subtract).then_inc(lo_done, 1)

        @block.scalar
        def _(act):
            def hi(g):
                if gate is not None:
                    act.wait_ge(gated, g + 1)
                else:
                    act.wait_ge(a_in[g % 2], 16 * (g // 2 + 1))
                if g >= 2:
                    act.wait_ge(filled, 4 * (g - 1))
                nc.scalar.activation(ah[:, g % 2], a[:, g % 2], ACT.Copy).then_inc(hi_done, 1)

            hi(0)
            for k in range(KD):
                act.wait_ge(w_in[k % 4], 16 * (k // 4 + 1))
                nc.scalar.activation(w[0][:, k], raw[:, k % 4], ACT.Copy).then_inc(w_hi, 1)
            hi(1)
            for t in range(NT):
                if t % 2 == 0 and 2 <= t // 2 + 1 < n_groups:
                    hi(t // 2 + 1)
                if final_gain is not None:
                    act.wait_ge(added, t + 1)
                    nc.scalar.activation(junk[:], y[:, t % 2], ACT.Square,
                                         accum_out=ss[:, t:t + 1]).then_inc(squared, 1)
                    act.wait_ge(meaned, t + 1)
                    nc.scalar.activation(sd[:, t:t + 1], ms[:, t:t + 1], ACT.Sqrt).then_inc(rooted, 1)

        @block.vector
        def _(dve):
            def multiply_gate(g):
                if gate is not None:
                    dve.wait_ge(a_in[g % 2], 16 * (g // 2 + 1))
                    dve.wait_ge(gate_in, 16 * (g + 1))
                    nc.vector.tensor_tensor(a[:, g % 2], a[:, g % 2], gate[:], ALU.mult).then_inc(gated, 1)

            def finish(t):
                dve.wait_ge(squared, t + 1)
                nc.vector.tensor_scalar(ms[:, t:t + 1], ss[:, t:t + 1], 1.0 / D, EPS, ALU.mult,
                                        ALU.add).then_inc(meaned, 1)
                dve.wait_ge(rooted, t + 1)
                nc.vector.reciprocal(rs[:, t:t + 1], sd[:, t:t + 1])
                dve.drain()
                nc.vector.scalar_tensor_tensor(out=y[:, t % 2], in0=y[:, t % 2], scalar=rs[:, t:t + 1],
                                               in1=gain[:], op0=ALU.mult, op1=ALU.mult).then_inc(done, 1)

            multiply_gate(0)
            for k in range(KD):
                dve.wait_ge(w_hi, k + 1)
                nc.vector.tensor_tensor(w[1][:, k], raw[:, k % 4], w[0][:, k].bitcast(F32),
                                        ALU.subtract).then_inc(w_lo, 1)
            multiply_gate(1)
            if final_gain is not None:
                dve.wait_ge(gain_in, 16)
            for t in range(NT):
                if t % 2 == 0 and 2 <= t // 2 + 1 < n_groups:
                    multiply_gate(t // 2 + 1)
                dve.wait_ge(x_in[t % 2], 16 * (t // 2 + 1))
                if t >= 2:
                    dve.wait_ge(stored[t % 2], 16 * (t // 2))
                dve.wait_ge(filled, 2 * t + 2)
                last = nc.vector.tensor_tensor(y[:, t % 2], ps[:, t % 4].rearrange("p a b -> p (a b)"),
                                               x[:, t % 2], ALU.add)
                last.then_inc(added, 1)
                if final_gain is None:
                    dve.wait_ge(added, t + 1)
                    dve.sem_inc(done, 1)
                elif t >= 1:
                    finish(t - 1)
            if final_gain is not None:
                finish(NT - 1)

        @block.tensor
        def _(pe):
            def multiply(t, b, k):
                g, s = t // 2 % 2, slice(t % 2 * P, (t % 2 + 1) * P)
                cols = slice(b * GT, (b + 1) * GT)
                last = mm3(nc.tensor, ps[:, t % 4, b], (ah[:, g, k, s], al[:, g, k, s]),
                           [z[:, k, cols] for z in w], start=k == 0, stop=k == KD - 1)
                if k == KD - 1:
                    last.then_inc(filled, 1)

            pe.wait_ge(lo_done, 1)
            for k in range(KD):
                pe.wait_ge(w_lo, k + 1)
                for t in range(2):
                    for b in range(2):
                        multiply(t, b, k)
            for t in range(2, NT):
                pe.wait_ge(lo_done, t // 2 + 1)
                if t >= 4:
                    pe.wait_ge(added, t - 3)
                for b in range(2):
                    for k in range(KD):
                        multiply(t, b, k)


def fm_run(count, column, dst, row, func=ACT.Copy):
    return Run("fm", count, lambda j: [(0, column + P * j, P)],
               lambda j, g: dst[bass.ds(row + P * j, P), g * GT:(g + 1) * GT], func)


def first_layer_runs(cqT, tm):
    tm_parts = [[(0, C_PE, 32), (32, C_QB, 242)], [(0, C_QB + 242, 274)],
                [(0, C_QB + 516, 252), (252, C_QI, 22)], [(0, C_QI + 22, 274)]]
    return [Run("tm", 4, lambda j: tm_parts[j],
                lambda j, t: tm[t * P:(t + 1) * P, j * TM_CHUNK:(j + 1) * TM_CHUNK]),
            fm_run(3, C_Q, cqT, 0)]


def second_layer_runs(qT, kT, v, zT):
    nq, nkv = WH * HD, WKV * HD
    return [Run("tm", 1, lambda j: [(0, nq + nkv, nkv)], lambda j, t: v[t * P:(t + 1) * P, :]),
            fm_run(2, 0, qT, 0),
            fm_run(6, 2 * P, qT, 2 * P),
            fm_run(2, nq, kT, 0),
            fm_run(8, nq + 2 * nkv, zT, 0, ACT.Silu)]


def stage_constants(nc, sem, ident, bias):
    made = sem("ident_made")
    with (nc.psum_tensor("t_ps", [WH, 3 * P], F32) as ps, nc.sbuf_tensor("t_hot", [32, 3 * P], F32) as hot,
          nc.sbuf_tensor("t_tab", [32, WH], F32) as tab):
        bias.start(sem, hot, tab, ps)
        with nc.Block() as block:
            @block.sync
            def _(sp):
                bias.sync(sp)

            @block.tensor
            def _(pe):
                bias.tensor(pe)

            @block.vector
            def _(dve):
                bias.vector(dve)

            @block.gpsimd
            def _(pool):
                nc.gpsimd.memset(ident[:], 0.0).then_inc(made, 1)
                pool.wait_ge(made, 1)
                nc.gpsimd.affine_select(out=ident[:], in_=ident[:], compare_op=ALU.not_equal, fill=1.0,
                                        base=0, pattern=[[-1, P]], channel_multiplier=1).then_inc(made, 1)


def program(nc, a, out):
    with ExitStack() as c:
        sem = Sems(nc)
        dram = lambda n, *s, d=F32: nc.dram_tensor(f"scratch_{n}", s, d).ap()
        cqT, tm, gates = dram("cqT", 384, T), dram("tm", T, TM_W), dram("gates", 3072, T)
        qkT, va = dram("qkT", 2, 2 * H, QK, T), dram("va", 2, T, H * HD)
        qbT, kbT, vb = dram("qbT", 2, 4, P, T), dram("kbT", 2, P, T), dram("vb", 2, T, P)
        qiT, kiT, wi = dram("qiT", 2, 2, P, T), dram("kiT", 2, IDX, T), dram("wi", T, H)
        h_dram = dram("h", 2, P, KD, T)
        mask = dram("mask", T, T, d=BF16)
        oaT, obT, mergedT = dram("oaT", H * HD, T), dram("obT", H * HD, T), dram("mergedT", D, T)
        x1 = dram("x1", T, D)
        q2T, k2T, v2 = dram("q2T", WH * HD, T), dram("k2T", WKV * HD, T), dram("v2", T, WKV * HD)
        z2T, o2T = dram("z2T", WH * HD, T), dram("o2T", WH * HD, T)
        spread = dram("spread", WH, P, 3 * P)
        ident = c.enter_context(nc.sbuf_tensor("ident", [P, P], F32))

        with ExitStack() as c1:
            bias = BiasJob(a["one_hot"], a["t5_table_2"], spread)
            bias.setup(nc, c1)
            stage_constants(nc, sem, ident, bias)
            sem.end_stage()
            hT = [c1.enter_context(nc.sbuf_tensor(f"h1T_{n}", [P, KD, T], F32R)) for n in ("hi", "lo")]
            stage_project(nc, sem, "p1", Norm(a["x"][0], a["norm_gain"][0], ident), hT, a["w_in"][0], TM_CHUNK,
                          first_layer_runs(cqT, tm), h_dram, bias)
            sem.end_stage()
        stage_qkv(nc, sem, ident, a, cqT, tm, qkT, qbT, kbT, qiT, kiT, va, vb, wi)
        sem.end_stage()
        stage_attention(nc, sem, "mla", ident, Mla(qkT, va, oaT))
        sem.end_stage()
        stage_index(nc, sem, ident, qiT, kiT, wi, mask, h_dram, a["w_in"][0],
                    a["b_merge"][0].rearrange("a n -> (a n)"), gates)
        sem.end_stage()
        stage_attention(nc, sem, "dsa", ident, Dsa(qbT, kbT, vb, mask, obT))
        sem.end_stage()
        stage_branch(nc, sem, oaT, obT, gates, a["w_branch_mla"][0], a["w_branch_dsa"][0], mergedT)
        sem.end_stage()
        stage_out(nc, sem, "o1", mergedT, None, a["w_out"][0], a["x"][0], x1)
        sem.end_stage()

        with ExitStack() as c1:
            hT = [c1.enter_context(nc.sbuf_tensor(f"h2T_{n}", [P, KD, T], F32R)) for n in ("hi", "lo")]
            stage_project(nc, sem, "p2", Norm(x1, a["norm_g_2"][0], ident), hT, a["a_w_in_2"][0], WKV * HD,
                          second_layer_runs(q2T, k2T, v2, z2T))
            sem.end_stage()
        stage_attention(nc, sem, "win", ident, Window(q2T, k2T, v2, spread, a["a_sinks_2"][0], o2T))
        sem.end_stage()
        stage_out(nc, sem, "o2", o2T, z2T, a["a_w_out_2"][0], x1, out[0], a["final_g_2"])
        sem.end_stage()


_INS = ["x", "positions", "norm_gain", "w_in", "b_merge", "mla_q_norm", "mla_w_uq", "mla_kv_norm",
        "mla_w_ukv", "mla_q_gain", "mla_k_gain", "dsa_q_gain", "dsa_k_gain", "w_branch_mla",
        "w_branch_dsa", "w_out", "t5_table_2", "norm_g_2", "final_g_2", "a_w_in_2", "a_sinks_2",
        "a_w_out_2"]


def kernel(**inputs):
    import concourse.bacc as bacc
    from concourse.bass_utils import run_bass_kernel_spmd

    nc = bacc.Bacc("TRN2", target_bir_lowering=False, num_devices=1)
    given = {name: np.ascontiguousarray(inputs[name]) for name in _INS}
    given["one_hot"] = t5_one_hot()
    arrays, aps = {}, {}
    for name, x in given.items():
        arrays[f"in_{name}"] = x
        aps[name] = nc.dram_tensor(f"in_{name}", x.shape, mybir.dt.from_np(x.dtype), kind="ExternalInput").ap()
    out = nc.dram_tensor("out_x", (1, T, D), F32, kind="ExternalOutput").ap()
    program(nc, aps, out)
    r = run_bass_kernel_spmd(nc, [arrays], core_ids=[0])
    return r.results[0]["out_x"]
```
